# Optimizing a Trainium2 kernel written in Bass

```python
import math
import jax, jax.numpy as jnp
from jax import lax
import numpy as np

D_MODEL = 2048
BATCH = 1
SEQ = 512
DEPTH = 1

N_MEM = 256
HEAD_DIM = 128
GDN_HEADS = 8
SB_HEADS = 4
MEM_HEADS = 4
GDN_WIDTH = GDN_HEADS * HEAD_DIM
SB_WIDTH = SB_HEADS * HEAD_DIM
MEM_WIDTH = MEM_HEADS * HEAD_DIM
MIX_WIDTH = GDN_WIDTH + SB_WIDTH + MEM_WIDTH
IN_COLS = 4 * GDN_WIDTH + 2 * GDN_HEADS + 3 * SB_WIDTH + MEM_WIDTH
CONV_WIDTH = 4
GDN_CHUNK = 64
SB_BLOCK = 128
PEER_HEADS = 8
PEER_N_KEYS = 128
PEER_N_EXPERTS = PEER_N_KEYS * PEER_N_KEYS
PEER_TOPK = 16
PEER_D_HALF = 128
PEER_D_QUERY = 2 * PEER_D_HALF
PEER_TOKEN_BLOCK = 128
DEEPNORM_ALPHA = (2 * DEPTH) ** 0.25
DEEPNORM_BETA = (8 * DEPTH) ** -0.25
LN_EPS = 1e-5
RMS_EPS = 1e-6

kernel_name = 'hybrid_gdn_stickbreak_mem_peer_deepnorm'

def layer_norm(x, w, b):
    xf = x.astype(jnp.float32)
    mu = jnp.mean(xf, axis=-1, keepdims=True)
    var = jnp.mean(jnp.square(xf - mu), axis=-1, keepdims=True)
    return ((xf - mu) * lax.rsqrt(var + LN_EPS) * w.astype(jnp.float32) + b.astype(jnp.float32)).astype(x.dtype)

def rms_norm(x, w):
    xf = x.astype(jnp.float32)
    return xf * lax.rsqrt(jnp.mean(jnp.square(xf), axis=-1, keepdims=True) + RMS_EPS) * w.astype(jnp.float32)

def l2_normalize(x):
    return x * lax.rsqrt(jnp.sum(jnp.square(x), axis=-1, keepdims=True) + RMS_EPS)

def causal_conv(x, w):
    T = x.shape[1]
    xp = jnp.pad(x, ((0, 0), (CONV_WIDTH - 1, 0), (0, 0)))
    return sum(xp[:, i:i + T] * w[i] for i in range(CONV_WIDTH))

def to_heads(t, n_heads):
    B, T, _ = t.shape
    return t.reshape(B, T, n_heads, HEAD_DIM).transpose(0, 2, 1, 3)

def gated_delta_rule_chunked(q, k, v, g, beta):
    f32 = jnp.float32
    q, k, v, g, beta = (t.astype(f32) for t in (q, k, v, g, beta))
    B, H, T, Dk = q.shape
    Dv = v.shape[-1]
    C = GDN_CHUNK
    N = T // C
    q = q.reshape(B, H, N, C, Dk)
    k = k.reshape(B, H, N, C, Dk)
    v = v.reshape(B, H, N, C, Dv)
    beta = beta.reshape(B, H, N, C)
    g = jnp.cumsum(g.reshape(B, H, N, C), axis=-1)
    k_beta = k * beta[..., None]
    v_beta = v * beta[..., None]
    tril = jnp.tril(jnp.ones((C, C), dtype=bool))
    strict = jnp.tril(jnp.ones((C, C), dtype=bool), -1)
    decay = jnp.exp(jnp.where(tril, g[..., :, None] - g[..., None, :], -jnp.inf))
    lower = jnp.where(strict, jnp.einsum('bhnid,bhnjd->bhnij', k_beta, k) * decay, 0.0)
    a_mat = lower + jnp.eye(C, dtype=f32)
    u = lax.linalg.triangular_solve(a_mat, v_beta, left_side=True, lower=True, unit_diagonal=True)
    w = lax.linalg.triangular_solve(a_mat, k_beta * jnp.exp(g)[..., None], left_side=True, lower=True, unit_diagonal=True)
    qk = jnp.einsum('bhnid,bhnjd->bhnij', q, k) * decay

    def step(S, inp):
        q_c, k_c, u_c, w_c, g_c, qk_c = inp
        v_new = u_c - jnp.einsum('bhcd,bhde->bhce', w_c, S)
        o = jnp.einsum('bhcd,bhde->bhce', q_c * jnp.exp(g_c)[..., None], S) + jnp.einsum('bhij,bhje->bhie', qk_c, v_new)
        g_last = g_c[..., -1]
        S = S * jnp.exp(g_last)[..., None, None] + jnp.einsum('bhcd,bhce->bhde', k_c * jnp.exp(g_last[..., None] - g_c)[..., None], v_new)
        return S, o

    xs = tuple(jnp.moveaxis(t, 2, 0) for t in (q, k, u, w, g, qk))
    S0 = jnp.zeros((B, H, Dk, Dv), f32)
    _, o = lax.scan(step, S0, xs)
    return jnp.moveaxis(o, 0, 2).reshape(B, H, T, Dv)

def stick_breaking_attention(q, k, v):
    T = q.shape[2]
    scale = HEAD_DIM ** -0.5
    outs = []
    for blk in range(T // SB_BLOCK):
        t0 = blk * SB_BLOCK
        t1 = t0 + SB_BLOCK
        qb = q[:, :, t0:t1]
        kb = k[:, :, :t1]
        vb = v[:, :, :t1]
        z = jnp.einsum('bhqd,bhkd->bhqk', qb, kb).astype(jnp.float32) * scale
        causal = jnp.arange(t1)[None, :] < (t0 + jnp.arange(SB_BLOCK))[:, None]
        log_not = jnp.where(causal, -jax.nn.softplus(z), 0.0)
        after = lax.cumsum(log_not, axis=3, reverse=True) - log_not
        a = jnp.where(causal, jnp.exp(jax.nn.log_sigmoid(z) + after), 0.0)
        outs.append(jnp.einsum('bhqk,bhkd->bhqd', a.astype(vb.dtype), vb))
    return jnp.concatenate(outs, axis=2)

def mixing_block(h, mem, w_in, conv_w, a_log, dt_bias, gdn_norm_w, sb_norm_w, mem_norm_w,
                 ln_mem_w, ln_mem_b, w_mem_kv, w_out):
    B, T, _ = h.shape
    f32 = jnp.float32
    proj = h @ w_in
    o1 = 3 * GDN_WIDTH
    o2 = o1 + GDN_WIDTH
    o3 = o2 + GDN_HEADS
    o4 = o3 + GDN_HEADS
    o5 = o4 + 3 * SB_WIDTH
    gdn_qkv, gdn_z, gdn_a, gdn_b, sb_qkv, mem_q = jnp.split(proj, [o1, o2, o3, o4, o5], axis=-1)

    qkv = jax.nn.silu(causal_conv(gdn_qkv, conv_w))
    q, k, v = (to_heads(t, GDN_HEADS) for t in jnp.split(qkv, 3, axis=-1))
    q = l2_normalize(q.astype(f32)) * HEAD_DIM ** -0.5
    k = l2_normalize(k.astype(f32))
    g = -jnp.exp(a_log.astype(f32)) * jax.nn.softplus(gdn_a.astype(f32) + dt_bias.astype(f32))
    beta = jax.nn.sigmoid(gdn_b.astype(f32))
    o_gdn = gated_delta_rule_chunked(q, k, v, g.transpose(0, 2, 1), beta.transpose(0, 2, 1))
    o_gdn = o_gdn.transpose(0, 2, 1, 3)
    z = gdn_z.reshape(B, T, GDN_HEADS, HEAD_DIM).astype(f32)
    o_gdn = (rms_norm(o_gdn, gdn_norm_w) * jax.nn.silu(z)).reshape(B, T, GDN_WIDTH)

    q_sb, k_sb, v_sb = (to_heads(t, SB_HEADS) for t in jnp.split(sb_qkv, 3, axis=-1))
    o_sb = stick_breaking_attention(q_sb, k_sb, v_sb).transpose(0, 2, 1, 3)
    o_sb = rms_norm(o_sb, sb_norm_w.reshape(SB_HEADS, HEAD_DIM)).reshape(B, T, SB_WIDTH)

    m = layer_norm(mem, ln_mem_w, ln_mem_b)
    mk, mv = jnp.split(m @ w_mem_kv, 2, axis=-1)
    mk = mk.reshape(B, N_MEM, MEM_HEADS, HEAD_DIM)
    mv = mv.reshape(B, N_MEM, MEM_HEADS, HEAD_DIM)
    qm = mem_q.reshape(B, T, MEM_HEADS, HEAD_DIM)
    s = jnp.einsum('bthd,bmhd->bhtm', qm, mk).astype(f32) * HEAD_DIM ** -0.5
    p = jax.nn.softmax(s, axis=-1)
    o_mem = jnp.einsum('bhtm,bmhd->bthd', p.astype(mv.dtype), mv)
    o_mem = rms_norm(o_mem, mem_norm_w.reshape(MEM_HEADS, HEAD_DIM)).reshape(B, T, MEM_WIDTH)

    o = jnp.concatenate([o_gdn, o_sb, o_mem], axis=-1).astype(h.dtype)
    return o @ w_out

def peer_ffn(h, wq, keys1, keys2, u, v):
    B, T, D = h.shape
    TB = PEER_TOKEN_BLOCK
    nb = (B * T) // TB
    xt = h.reshape(B * T, D)
    q = (xt @ wq).reshape(B * T, PEER_HEADS, 2, PEER_D_HALF)
    s1 = jnp.einsum('thd,kd->thk', q[:, :, 0], keys1).astype(jnp.float32)
    s2 = jnp.einsum('thd,kd->thk', q[:, :, 1], keys2).astype(jnp.float32)
    v1, i1 = lax.top_k(s1, PEER_TOPK)
    v2, i2 = lax.top_k(s2, PEER_TOPK)
    cand_s = (v1[..., :, None] + v2[..., None, :]).reshape(B * T, PEER_HEADS, PEER_TOPK * PEER_TOPK)
    cand_i = (i1[..., :, None] * PEER_N_KEYS + i2[..., None, :]).reshape(B * T, PEER_HEADS, PEER_TOPK * PEER_TOPK)
    top_s, pos = lax.top_k(cand_s, PEER_TOPK)
    idx = jnp.take_along_axis(cand_i, pos, axis=-1)
    gate = jax.nn.softmax(top_s, axis=-1)

    def expert_block(args):
        xb, ib, gb = args
        ub = jnp.take(u, ib, axis=0)
        act = jax.nn.gelu(jnp.einsum('td,thkd->thk', xb, ub).astype(jnp.float32), approximate=False)
        wgt = (gb * act).astype(v.dtype)
        return jnp.einsum('thk,thkd->td', wgt, jnp.take(v, ib, axis=0))

    out = lax.map(expert_block, (xt.reshape(nb, TB, D),
                                 idx.reshape(nb, TB, PEER_HEADS, PEER_TOPK),
                                 gate.reshape(nb, TB, PEER_HEADS, PEER_TOPK)))
    return out.reshape(B, T, D).astype(h.dtype)

def setup_inputs(seed: int = 0) -> dict:
    key = jax.random.key(seed)
    ks = jax.random.split(key, 32)
    f32 = jnp.float32
    L = DEPTH

    def nrm(k, shape, scale):
        return jax.random.normal(k, shape, f32) * scale

    def gain(k, shape):
        return 1.0 + 0.02 * jax.random.normal(k, shape, f32)

    def bias(k, shape):
        return 0.02 * jax.random.normal(k, shape, f32)

    dt = jnp.exp(jax.random.uniform(ks[6], (L, GDN_HEADS), f32, math.log(1e-3), math.log(1e-1)))
    return {
        'x': nrm(ks[0], (BATCH, SEQ, D_MODEL), 1.0),
        'mem': nrm(ks[1], (BATCH, N_MEM, D_MODEL), 1.0),
        'ln_emb_w': gain(ks[2], (D_MODEL,)),
        'ln_emb_b': bias(ks[3], (D_MODEL,)),
        'w_in': nrm(ks[4], (L, D_MODEL, IN_COLS), D_MODEL ** -0.5),
        'conv_w': nrm(ks[5], (L, CONV_WIDTH, 3 * GDN_WIDTH), CONV_WIDTH ** -0.5),
        'a_log': jnp.log(jax.random.uniform(ks[7], (L, GDN_HEADS), f32, 1.0, 16.0)),
        'dt_bias': dt + jnp.log(-jnp.expm1(-dt)),
        'gdn_norm_w': gain(ks[8], (L, HEAD_DIM)),
        'sb_norm_w': gain(ks[9], (L, SB_WIDTH)),
        'mem_norm_w': gain(ks[10], (L, MEM_WIDTH)),
        'ln_mem_w': gain(ks[11], (L, D_MODEL)),
        'ln_mem_b': bias(ks[12], (L, D_MODEL)),
        'w_mem_kv': nrm(ks[13], (L, D_MODEL, 2 * MEM_WIDTH), D_MODEL ** -0.5),
        'w_out': nrm(ks[14], (L, MIX_WIDTH, D_MODEL), MIX_WIDTH ** -0.5 * DEEPNORM_BETA),
        'ln1_w': gain(ks[15], (L, D_MODEL)),
        'ln1_b': bias(ks[16], (L, D_MODEL)),
        'peer_wq': nrm(ks[17], (L, D_MODEL, PEER_HEADS * PEER_D_QUERY), D_MODEL ** -0.5),
        'peer_keys1': nrm(ks[18], (L, PEER_N_KEYS, PEER_D_HALF), PEER_D_HALF ** -0.5),
        'peer_keys2': nrm(ks[19], (L, PEER_N_KEYS, PEER_D_HALF), PEER_D_HALF ** -0.5),
        'peer_u': nrm(ks[20], (L, PEER_N_EXPERTS, D_MODEL), D_MODEL ** -0.5),
        'peer_v': nrm(ks[21], (L, PEER_N_EXPERTS, D_MODEL), DEEPNORM_BETA),
        'ln2_w': gain(ks[22], (L, D_MODEL)),
        'ln2_b': bias(ks[23], (L, D_MODEL)),
    }

def reference(x, mem, ln_emb_w, ln_emb_b, w_in, conv_w, a_log, dt_bias, gdn_norm_w, sb_norm_w,
              mem_norm_w, ln_mem_w, ln_mem_b, w_mem_kv, w_out, ln1_w, ln1_b, peer_wq, peer_keys1,
              peer_keys2, peer_u, peer_v, ln2_w, ln2_b):
    h = layer_norm(x, ln_emb_w, ln_emb_b)
    for l in range(DEPTH):
        mix = mixing_block(h, mem, w_in[l], conv_w[l], a_log[l], dt_bias[l], gdn_norm_w[l], sb_norm_w[l],
                           mem_norm_w[l], ln_mem_w[l], ln_mem_b[l], w_mem_kv[l], w_out[l])
        h = layer_norm(DEEPNORM_ALPHA * h + mix, ln1_w[l], ln1_b[l])
        ffn = peer_ffn(h, peer_wq[l], peer_keys1[l], peer_keys2[l], peer_u[l], peer_v[l])
        h = layer_norm(DEEPNORM_ALPHA * h + ffn, ln2_w[l], ln2_b[l])
    return h


_drawn_inputs = setup_inputs


def setup_inputs(seed=0):
    import zlib

    import numpy as np

    out = dict(_drawn_inputs(seed))
    spreads = {}
    factors = {'gdn_norm_w': 3.017,
     'sb_norm_w': 3.048,
     'mem_norm_w': 2.969,
     'ln2_w': 2.826,
     'ln2_b': 2.879}
    for name, (base, spread) in spreads.items():
        noise = np.random.default_rng([zlib.crc32(name.encode()), seed]).standard_normal(out[name].shape)
        drawn = base * np.exp(spread * noise) if base else spread * noise
        out[name] = __import__('jax').numpy.asarray(drawn.astype(out[name].dtype))
    for name, factor in factors.items():
        out[name] = (out[name] * factor).astype(out[name].dtype)
    return out
```

```python
from contextlib import ExitStack, contextmanager

import numpy as np

import concourse.bass as bass
from concourse import mybir

F32 = mybir.dt.float32
F32R = mybir.dt.float32r
U32 = mybir.dt.uint32
ALU = mybir.AluOpType
ACT = mybir.ActivationFunctionType
AX_X = mybir.AxisListType.X

P = 128
T = 512
TB = T // P
D = 2048
KD = D // P
M = 256
MB = M // P
GH, SH, MH = 8, 4, 4
HEADS = GH + SH + MH
TAPS = 4
LEVELS = 7
PH, KEYS, TOPK = 8, 128, 16
EB = 4
GROUPS = KEYS // EB
TG = 32
NTG = T // TG
UNIT = 2048
COLS = 512
DB = D // COLS
KQ = UNIT // COLS
LN_EPS, RMS_EPS = 1e-5, 1e-6
ALPHA = 2.0 ** 0.25
SCALE = float(P) ** -0.5
NEG = -3.0e38
G_LOG, G_RUN, G_BETA_HALF, G_NEG_BETA, G_BETA_EXP, G_TO_END, G_TOTAL = range(7)
G_KINDS = 7
FILL_FIRST, FILL_LEVEL, FILL_CHUNK = 12, 10, 10
UNITS_ATT = 6 * SH
UNITS_GDN = 4 * GH
UNITS_OUT = DB * (HEADS // KQ)
UNITS_Q = 2 * PH


def at(const, per=0, i=None):
    return const if i is None else i * per + const


def over_blocks(tile):
    return tile.unsqueeze(1).to_broadcast([P, TB, P])


def over_columns(col):
    return col.unsqueeze(2).to_broadcast([P, TB, P])


def blocks(tile):
    return tile.rearrange("p (b n) -> p b n", b=TB)


class Chain:

    def __init__(self, eng, sem, base, per=0, i=None, apart=None):
        self.apart = apart
        self.eng, self.sem, self.base, self.per, self.i, self.n = eng, sem, base, per, i, 0

    def mark(self, ins):
        self.n += 1
        ins.then_inc(self.sem, 1)

    def wait(self):
        self.eng.wait_ge(self.sem, at(self.base + self.n, self.per, self.i))

    def wait_apart(self):
        self.wait()
        self.eng.sem_inc(self.apart, 1)

    def link(self, ins):
        self.mark(ins)
        self.wait()


@contextmanager
def phase(nc):
    with ExitStack() as ctx:
        ctx.semaphores = []
        yield ctx
    nc.clear_and_free_semaphores(ctx.semaphores)
    nc.all_engine_barrier()


def phase_semaphore(nc, ctx, name):
    ctx.semaphores.append(nc.alloc_semaphore(name))
    return ctx.semaphores[-1]


class Core:

    def __init__(self, nc, ctx):
        self.nc = nc

        def sb(name, shape, dt=F32):
            return ctx.enter_context(nc.sbuf_tensor(name, shape, dt))

        def sem(name):
            return ctx.enter_context(nc.semaphore(name))

        self.s_free = {name: sem(name) for name in (
            "att_ot_free", "gdn_ot_free", "gdn_bank_free", "mix_added", "spread_mm", "spread_copied", "spread_out_free", "expert_added")}
        self.ident = sb("ident", [P, P])
        self.ones = sb("ones", [P, P])
        self.tri_le = sb("tri_le", [P, P])
        self.tri_ge = sb("tri_ge", [P, P])
        self.iota = sb("iota", [P, P])
        self.half_neg = sb("half_neg", [P, 2 * TB])
        self.rms_eps = sb("rms_eps", [P, 1])
        self.act_hi = sb("act_hi", [P, KD, T], F32R)
        self.act_lo = sb("act_lo", [P, KD, T], F32R)
        self.w_raw = sb("w_raw", [P, 2, UNIT])
        self.w_hi = sb("w_hi", [P, 2, UNIT], F32R)
        self.w_lo = sb("w_lo", [P, 2, UNIT], F32R)
        self.bank = ctx.enter_context(nc.psum_tensor("bank", [P, 8, 512], F32))
        self.s_loaded = [sem("w_loaded_even"), sem("w_loaded_odd")]
        self.s_hi = sem("w_hi_done")
        self.s_lo = sem("w_lo_done")
        self.s_used = sem("w_unit_used")

    def load_unit(self, sp, src, c, per=0, i=None):
        if c >= 2:
            sp.wait_ge(self.s_lo, at(c - 1, per, i))
        sp.dma_start(self.w_raw[:, c % 2, :], src).then_inc(self.s_loaded[c % 2], 16)

    def split_hi(self, act, c, per=0, i=None):
        act.wait_ge(self.s_loaded[c % 2], at(16 * (c // 2 + 1), 8 * per, i))
        if c >= 2:
            act.wait_ge(self.s_used, at(c - 1, per, i))
        act.activation(self.w_hi[:, c % 2, :], self.w_raw[:, c % 2, :], ACT.Copy).then_inc(self.s_hi, 1)

    def split_lo(self, dve, c, per=0, i=None):
        dve.wait_ge(self.s_hi, at(c + 1, per, i))
        dve.tensor_tensor(self.w_lo[:, c % 2, :], self.w_raw[:, c % 2, :],
                          self.w_hi[:, c % 2, :].bitcast(F32), ALU.subtract).then_inc(self.s_lo, 1)

    def by_feature(self, pe, out, c, per=0, i=None, part=(0, 48), hi=None, lo=None):
        hi = self.act_hi if hi is None else hi
        lo = self.act_lo if lo is None else lo
        slot = c % 2
        for m in range(*part):
            k, term = divmod(m, 3)
            if m == 0:
                pe.wait_ge(self.s_lo, at(c + 1, per, i))
            w = (self.w_lo if term == 2 else self.w_hi)[:, slot, k * P:(k + 1) * P]
            x = (lo if term == 1 else hi)[:, k, :]
            mm = pe.matmul(out, w, x, start=(m == 0), stop=(m == 3 * KD - 1))
            if m == 3 * KD - 1:
                mm.then_inc(self.s_used, 1)

    def by_token(self, pe, outs, hi, lo, first, last, c, per=0, i=None):
        slot = c % 2
        pe.wait_ge(self.s_lo, at(c + 1, per, i))
        for b in range(TB):
            for k in range(KQ):
                for term in range(3):
                    x = (lo if term == 2 else hi)[:, k, b * P:(b + 1) * P]
                    w = (self.w_lo if term == 1 else self.w_hi)[:, slot, k * COLS:(k + 1) * COLS]
                    mm = pe.matmul(outs[b], x, w, start=(first and k == 0 and term == 0),
                                   stop=(last and k == KQ - 1 and term == 2))
        mm.then_inc(self.s_used, 1)


def constants(core):
    nc = core.nc
    with phase(nc) as ctx:
        filled, cut = (phase_semaphore(nc, ctx, n) for n in ("const_filled", "const_cut"))
        block = ctx.enter_context(nc.Block())

        @block.gpsimd
        def _(pool):
            pool.memset(core.ident[:, :], 0.0).then_inc(filled, 1)
            for tile in (core.ones, core.tri_le, core.tri_ge):
                pool.memset(tile[:, :], 1.0).then_inc(filled, 1)
            pool.memset(core.half_neg[:, :], -0.5).then_inc(filled, 1)
            pool.memset(core.rms_eps[:, :], RMS_EPS).then_inc(filled, 1)
            pool.wait_ge(filled, 6)
            pool.affine_select(out=core.ident[:, :], in_=core.ident[:, :], compare_op=ALU.not_equal, fill=1.0,
                               base=0, pattern=[[-1, P]], channel_multiplier=1).then_inc(cut, 1)
            pool.affine_select(out=core.tri_le[:, :], in_=core.tri_le[:, :], compare_op=ALU.is_ge, fill=0.0,
                               base=0, pattern=[[1, P]], channel_multiplier=-1).then_inc(cut, 1)
            pool.affine_select(out=core.tri_ge[:, :], in_=core.tri_ge[:, :], compare_op=ALU.is_ge, fill=0.0,
                               base=0, pattern=[[-1, P]], channel_multiplier=1).then_inc(cut, 1)
            pool.iota(core.iota[:, :], pattern=[[1, P]], base=0, channel_multiplier=0,
                      allow_small_or_imprecise_dtypes=True).then_inc(cut, 1)


class LayerNorm:

    def __init__(self, core, ctx, name):
        nc = core.nc
        self.core = core
        self.stats = ctx.enter_context(nc.sbuf_tensor(name + "_stats", [P, 4, 6], F32))
        self.mean_var = ctx.enter_context(nc.sbuf_tensor(name + "_mean_var", [P, 2], F32))
        self.var = ctx.enter_context(nc.sbuf_tensor(name + "_var_eps", [P, 1], F32))
        self.rstd = ctx.enter_context(nc.sbuf_tensor(name + "_rstd", [P, 1], F32))
        self.s_var = phase_semaphore(nc, ctx, name + "_var_ready")
        self.s_rstd = phase_semaphore(nc, ctx, name + "_rstd_ready")

    def on_vector(self, dve, chain, n, x, out, weight, bias, signal):
        for q in range(4):
            chain.mark(dve.bn_stats(self.stats[:, q, :], x[:, q * 512:(q + 1) * 512]))
        chain.wait()
        chain.link(dve.bn_aggr(self.mean_var[:, :], self.stats[:, :, :]))
        dve.tensor_scalar(self.var[:, :], self.mean_var[:, 1:2], LN_EPS, None, ALU.add).then_inc(self.s_var, 1)
        dve.wait_ge(self.s_rstd, n + 1)
        chain.link(dve.tensor_scalar(out, x, self.mean_var[:, 0:1], self.rstd[:, 0:1], ALU.subtract, ALU.mult))
        chain.link(dve.tensor_tensor(out, out, weight, ALU.mult))
        dve.tensor_tensor(out, out, bias, ALU.add).then_inc(signal, 1)

    def on_gpsimd(self, pool, n):
        pool.wait_ge(self.s_var, n + 1)
        pool.tensor_tensor(self.rstd[:, :], self.var[:, :], self.core.half_neg[:, 0:1], ALU.pow).then_inc(self.s_rstd, 1)


def embed(core, mem_hi, mem_lo, dram):
    nc = core.nc
    tiles = [("x", b) for b in range(TB)] + [("m", b) for b in range(MB)]
    with phase(nc) as ctx:
        def sb(name, shape, dt=F32):
            return ctx.enter_context(nc.sbuf_tensor(name, shape, dt))

        def sem(name):
            return phase_semaphore(nc, ctx, "embed_" + name)

        rows = sb("rows", [P, 2, D])
        emb_w, emb_b = sb("emb_w", [P, D]), sb("emb_b", [P, D])
        ln = LayerNorm(core, ctx, "ln0")
        s_params, s_chain = sem("params_loaded"), sem("dve_chain")
        s_row = [sem("rows_loaded_even"), sem("rows_loaded_odd")]
        s_normed, s_turned = sem("rows_normed"), sem("rows_turned")
        s_t_hi, s_t_lo = sem("turned_hi"), sem("turned_lo")
        s_kept = [sem("h_kept_even"), sem("h_kept_odd")]
        block = ctx.enter_context(nc.Block())

        @block.sync
        def _(sp):
            sp.dma_start(emb_w[:, :], dram["ln_emb_w"].partition_broadcast(P)).then_inc(s_params, 16)
            sp.dma_start(emb_b[:, :], dram["ln_emb_b"].partition_broadcast(P)).then_inc(s_params, 16)
            for n, (kind, b) in enumerate(tiles):
                if n >= 2:
                    sp.wait_ge(s_turned, 4 * (n - 1))
                    if n - 2 < TB:
                        sp.wait_ge(s_kept[n % 2], 16 * (n // 2))
                if n == TB:
                    sp.dma_start(emb_w[:, :], dram["ln_mem_w"].partition_broadcast(P)).then_inc(s_params, 16)
                    sp.dma_start(emb_b[:, :], dram["ln_mem_b"].partition_broadcast(P)).then_inc(s_params, 16)
                src = dram["x" if kind == "x" else "mem"][b * P:(b + 1) * P, :]
                sp.dma_start(rows[:, n % 2, :], src).then_inc(s_row[n % 2], 16)
                if n == TB - 1:
                    sp.wait_ge(s_normed, TB)
            for kept in s_kept:
                sp.wait_ge(kept, 16 * TB // 2)

        @block.gpsimd
        def _(pool):
            for n in range(len(tiles)):
                ln.on_gpsimd(pool, n)
                if n < TB:
                    pool.wait_ge(s_normed, n + 1)
                    pool.dma_start(dram["h_kept"][n * P:(n + 1) * P, :], rows[:, n % 2, :]).then_inc(s_kept[n % 2], 16)

        @block.tensor
        def _(pe):
            for n in range(len(tiles)):
                pe.wait_ge(s_normed, n + 1)
                for q in range(4):
                    u = 4 * n + q
                    if u >= 2:
                        pe.wait_ge(s_t_lo, u - 1)
                    for j in range(4):
                        k = 4 * q + j
                        mm = pe.transpose(core.bank[:, u % 2, j * P:(j + 1) * P],
                                          rows[:, n % 2, k * P:(k + 1) * P], core.ident[:, :])
                    mm.then_inc(s_turned, 1)

        def slots(n, q):
            kind, b = tiles[n]
            hi, lo = (core.act_hi, core.act_lo) if kind == "x" else (mem_hi, mem_lo)
            return [a[:, 4 * q:4 * q + 4, b * P:(b + 1) * P] for a in (hi, lo)]

        @block.scalar
        def _(act):
            for n in range(len(tiles)):
                for q in range(4):
                    u = 4 * n + q
                    act.wait_ge(s_turned, u + 1)
                    act.activation(slots(n, q)[0], blocks(core.bank[:, u % 2, :]), ACT.Copy).then_inc(s_t_hi, 1)

        @block.vector
        def _(dve):
            chain = Chain(dve, s_chain, 0)

            def low_parts(n):
                for q in range(4):
                    u = 4 * n + q
                    dve.wait_ge(s_t_hi, u + 1)
                    hi, lo = slots(n, q)
                    dve.tensor_tensor(lo, blocks(core.bank[:, u % 2, :]), hi.bitcast(F32), ALU.subtract).then_inc(s_t_lo, 1)

            for n, (kind, b) in enumerate(tiles):
                dve.wait_ge(s_row[n % 2], 16 * (n // 2 + 1))
                dve.wait_ge(s_params, 32 if n < TB else 64)
                x = rows[:, n % 2, :]
                ln.on_vector(dve, chain, n, x, x, emb_w[:, :], emb_b[:, :], s_normed)
                if n >= 1:
                    low_parts(n - 1)
            low_parts(len(tiles) - 1)


class RmsTail:

    def __init__(self, core, ctx, name, sq):
        nc = core.nc
        self.core, self.sq = core, sq
        f = lambda n, s: ctx.enter_context(nc.sbuf_tensor(name + n, s, F32))
        sem = lambda n: phase_semaphore(nc, ctx, name + n)
        self.o, self.on, self.ot = (f(x, [P, TB, P]) for x in ("_o", "_on", "_ot"))
        self.ms, self.rstd = f("_ms", [P, TB]), f("_rstd", [P, TB])
        self.s_ms, self.s_rstd, self.s_on = sem("_ms_ready"), sem("_rstd_ready"), sem("_normed")
        self.s_turned, self.s_ot, self.s_kept = sem("_turned"), sem("_ot_ready"), sem("_kept")

    def norm_on_vector(self, dve, chain, count):
        chain.link(dve.tensor_tensor(self.sq[:, :, :], self.o[:, :, :], self.o[:, :, :], ALU.mult))
        chain.link(dve.tensor_reduce(self.ms[:, :], self.sq[:, :, :], AX_X, ALU.add))
        dve.tensor_scalar(self.ms[:, :], self.ms[:, :], 1.0 / P, RMS_EPS, ALU.mult, ALU.add).then_inc(self.s_ms, 1)
        dve.wait_ge(self.s_rstd, count)
        dve.tensor_tensor(self.on[:, :, :], self.o[:, :, :], over_columns(self.rstd[:, :]), ALU.mult).then_inc(self.s_on, 1)

    def on_gpsimd(self, pool, n):
        pool.wait_ge(self.s_ms, n + 1)
        pool.tensor_tensor(self.rstd[:, :], self.ms[:, :], self.core.half_neg[:, 0:TB], ALU.pow).then_inc(self.s_rstd, 1)

    def turn(self, pe, n, bank):
        pe.wait_ge(self.s_on, n + 1)
        for b in range(TB):
            mm = pe.transpose(bank[:, b * P:(b + 1) * P], self.on[:, b, :], self.core.ident[:, :])
        mm.then_inc(self.s_turned, 1)

    def keep(self, pool, n, dst):
        pool.wait_ge(self.s_ot, n + 1)
        pool.dma_start(dst, self.ot[:, :, :].rearrange("p b n -> p (b n)")).then_inc(self.s_kept, 16)


def attention(core, mem_hi, mem_lo, dram):
    nc = core.nc
    bank = core.bank
    with phase(nc) as ctx:
        def sb(name, shape, dt=F32):
            return ctx.enter_context(nc.sbuf_tensor(name, shape, dt))

        def sem(name):
            return phase_semaphore(nc, ctx, "attention_" + name)

        mk, mv, mvt = sb("mk", [P, M]), sb("mv", [P, M]), sb("mvt", [P, MB, P])
        mq, sq, sk, sv = (sb(x, [P, T]) for x in ("mq", "sq", "sk", "sv"))
        svt = sb("svt", [P, TB, P])
        neg_max, row_sum, inv_sum = (sb(x, [P, TB]) for x in ("neg_max", "row_sum", "inv_sum"))
        prob, prob_t = sb("prob", [P, TB, M]), sb("prob_t", [P, MB, T])
        z, soft, absz = sb("z", [P, TB, T]), sb("soft", [P, TB, T]), sb("absz", [P, 2, T])
        before, not_before = sb("before", [P, P]), sb("not_before", [P, P])
        norm_w = sb("norm_w", [P, MH + SH])
        norm_now = sb("norm_now", [P, 2])
        sq_tail = sb("sq_tail", [P, TB, P])
        mt, st = RmsTail(core, ctx, "mem", sq_tail), RmsTail(core, ctx, "stick", sq_tail)
        s_chain, s_const, s_ot_free = sem("dve_chain"), sem("masks_made"), core.s_free["att_ot_free"]
        s_params = sem("params_loaded")
        s_proj = [sem(f"{x}_copied") for x in ("mk", "mv", "mq", "sq", "sk", "sv")]
        s_mvt, s_mvt_sb, s_svt, s_svt_sb = sem("mv_turned"), sem("mvt_copied"), sem("sv_turned"), sem("svt_copied")
        s_scores, s_max, s_prob = sem("mem_scores"), sem("mem_max"), sem("mem_prob")
        s_probt, s_probt_sb, s_mo = sem("prob_turned"), sem("prob_t_copied"), sem("mem_o")
        s_z, s_z_sb, s_abs, s_exp, s_ln = sem("z_ready"), sem("z_copied"), sem("abs_z"), sem("exp_abs"), sem("ln_one_plus")
        s_soft, s_masked = sem("softplus"), sem("softplus_masked")
        s_after, s_arg, s_att, s_amasked, s_so = sem("suffix_sums"), sem("log_weight"), sem("att_exp"), sem("att_masked"), sem("stick_o")
        block = ctx.enter_context(nc.Block())
        UT = 6

        @block.sync
        def _(sp):
            sp.dma_start(norm_w[:, :], dram["att_norm_w"]).then_inc(s_params, 16)

            def unit(s, u):
                return dram["w_mem_kv"][s * 2 + u] if u < 2 else dram["w_att"][s * 4 + u - 2]

            for u in range(2):
                core.load_unit(sp, unit(0, u), u)
            with sp.Fori(0, SH - 1) as s:
                for u in range(UT):
                    core.load_unit(sp, unit(s, u + 2) if u + 2 < UT else unit(s + 1, u + 2 - UT), u + 2, UT, s)
            for u in range(UT):
                n = u + 2
                core.load_unit(sp, unit(SH - 1, n) if n < UT else dram["w_gdn"][n - UT], UT * (SH - 1) + n)

        @block.tensor
        def _(pe):
            with pe.Fori(0, SH) as s:
                def project(u, out, part=(0, 48)):
                    if u >= 2 and part[0] == 0:
                        pe.wait_ge(s_proj[u - 2], s + 1)
                    hl = dict(hi=mem_hi, lo=mem_lo) if u < 2 else {}
                    core.by_feature(pe, out, u, UT, s, part, **hl)

                project(0, bank[:, 0, 0:M])
                project(1, bank[:, 1, 0:M])
                project(2, bank[:, 0, :])
                pe.wait_ge(s_proj[1], s + 1)
                for j in range(MB):
                    mm = pe.transpose(bank[:, 2, j * P:(j + 1) * P], mv[:, j * P:(j + 1) * P], core.ident[:, :])
                mm.then_inc(s_mvt, 1)
                project(3, bank[:, 1, :])
                pe.wait_ge(s_proj[2], s + 1)
                for b in range(TB):
                    mm = pe.matmul(bank[:, 4 + b // 2, (b % 2) * M:(b % 2 + 1) * M], mq[:, b * P:(b + 1) * P],
                                   mk[:, :], start=True, stop=True)
                mm.then_inc(s_scores, 1)
                project(4, bank[:, 0, :])
                pe.wait_ge(s_prob, 4 * s + 4)
                for j in range(MB):
                    for b in range(TB):
                        mm = pe.transpose(bank[:, 6 + j, b * P:(b + 1) * P], prob[:, b, j * P:(j + 1) * P], core.ident[:, :])
                mm.then_inc(s_probt, 1)
                project(5, bank[:, 1, :])
                pe.wait_ge(s_mvt_sb, s + 1)
                pe.wait_ge(s_probt_sb, s + 1)
                for b in range(TB):
                    for j in range(MB):
                        mm = pe.matmul(bank[:, 2, b * P:(b + 1) * P], prob_t[:, j, b * P:(b + 1) * P], mvt[:, j, :],
                                       start=(j == 0), stop=(j == MB - 1))
                mm.then_inc(s_mo, 1)
                pe.wait_ge(s_proj[5], s + 1)
                for j in range(TB):
                    mm = pe.transpose(bank[:, 3, j * P:(j + 1) * P], sv[:, j * P:(j + 1) * P], core.ident[:, :])
                mm.then_inc(s_svt, 1)
                for j in range(TB):
                    w = j * P
                    if j >= 2:
                        pe.wait_ge(s_soft, 4 * s + j - 1)
                    pe.matmul(bank[:, 4 + j % 2, w:T], sk[:, w:w + P], sq[:, w:T], start=True, stop=True).then_inc(s_z, 1)
                pe.wait_ge(s_masked, 4 * s + 4)
                for j in range(TB):
                    if j >= 2:
                        pe.wait_ge(s_arg, 4 * s + j - 1)
                    for jj in range(j, TB):
                        mm = pe.matmul(bank[:, 6 + j % 2, jj * P:T], (core.tri_ge if jj == j else core.ones)[:, :],
                                       soft[:, jj, jj * P:T], start=(jj == j), stop=(jj == TB - 1))
                    mm.then_inc(s_after, 1)
                mt.turn(pe, s, bank[:, 4, :])
                pe.wait_ge(s_att, 4 * s + 4)
                pe.wait_ge(s_svt_sb, s + 1)
                for b in range(TB):
                    for j in range(b + 1):
                        mm = pe.matmul(bank[:, 5, b * P:(b + 1) * P], z[:, j, b * P:(b + 1) * P], svt[:, j, :],
                                       start=(j == 0), stop=(j == b))
                mm.then_inc(s_so, 1)
                st.turn(pe, s, bank[:, 3, :])

        @block.scalar
        def _(act):
            act.preload_act_table_set("natural_log_exp_and_others")
            core.split_hi(act, 0)
            core.split_hi(act, 1)

            def turn(i, base):
                c, per = UT * base, UT
                s1 = lambda m, k: at(m * base + k, m, i)

                def copied(u, dst, src, scale=1.0):
                    act.wait_ge(core.s_used, at(c + u + 1, per, i))
                    act.activation(dst, src, ACT.Copy, scale=scale).then_inc(s_proj[u], 1)
                    core.split_hi(act, c + u + 2, per, i)

                copied(0, mk[:, :], bank[:, 0, 0:M])
                copied(1, mv[:, :], bank[:, 1, 0:M])
                copied(2, mq[:, :], bank[:, 0, :], SCALE)
                act.wait_ge(s_mvt, s1(1, 1))
                act.activation(mvt[:, :, :], bank[:, 2, 0:M].rearrange("p (b n) -> p b n", b=MB), ACT.Copy).then_inc(s_mvt_sb, 1)
                copied(3, sq[:, :], bank[:, 1, :], SCALE)
                act.wait_ge(s_max, s1(2, 2))
                for b in range(TB):
                    act.activation(prob[:, b, :], bank[:, 4 + b // 2, (b % 2) * M:(b % 2 + 1) * M], ACT.Exp,
                                   bias=neg_max[:, b:b + 1], accum_out=row_sum[:, b:b + 1]).then_inc(s_prob, 1)
                copied(4, sk[:, :], bank[:, 0, :])
                act.wait_ge(s_probt, s1(1, 1))
                act.activation(prob_t[:, :, :], bank[:, 6:8, :], ACT.Copy).then_inc(s_probt_sb, 1)
                copied(5, sv[:, :], bank[:, 1, :])
                act.wait_ge(s_svt, s1(1, 1))
                act.activation(svt[:, :, :], blocks(bank[:, 3, :]), ACT.Copy).then_inc(s_svt_sb, 1)
                for j in range(TB):
                    w = slice(j * P, T)
                    act.wait_ge(s_z, s1(4, j + 1))
                    act.activation(z[:, j, w], bank[:, 4 + j % 2, w], ACT.Copy).then_inc(s_z_sb, 1)
                    act.wait_ge(s_abs, s1(4, j + 1))
                    act.activation(absz[:, j % 2, w], absz[:, j % 2, w], ACT.Exp, scale=-1.0).then_inc(s_exp, 1)
                    act.wait_ge(s_exp, s1(4, j + 1))
                    act.activation(absz[:, j % 2, w], absz[:, j % 2, w], ACT.Ln, bias=1.0).then_inc(s_ln, 1)
                for j in range(TB):
                    act.wait_ge(s_amasked, s1(4, j + 1))
                    act.activation(z[:, j, j * P:T], z[:, j, j * P:T], ACT.Exp).then_inc(s_att, 1)

            with act.Fori(0, SH) as i:
                turn(i, 0)

        @block.vector
        def _(dve):
            core.split_lo(dve, 0)
            core.split_lo(dve, 1)
            PER = 8
            dve.wait_ge(s_params, 16)

            def turn(i, base):
                c, per = UT * base, UT
                chain = Chain(dve, s_chain, PER * base, PER, i)
                s1 = lambda m, k: at(m * base + k, m, i)

                def split(u):
                    core.split_lo(dve, c + u, per, i)

                split(2)
                split(3)
                split(4)
                split(5)
                dve.wait_ge(s_scores, s1(1, 1))
                for b in range(2):
                    dve.tensor_reduce(neg_max[:, 2 * b:2 * b + 2], bank[:, 4 + b, :].rearrange("p (b n) -> p b n", b=2),
                                      AX_X, ALU.max, negate=True).then_inc(s_max, 1)
                dve.wait_ge(s_ot_free, s1(1, 1))
                chain.mark(dve.tensor_copy(norm_now[:, :], norm_w[:, bass.ds(at(2 * base, 2, i), 2)]))
                split(6)
                dve.wait_ge(s_prob, s1(4, 4))
                chain.link(dve.reciprocal(inv_sum[:, :], row_sum[:, :]))
                split(7)
                dve.wait_ge(s_mo, s1(1, 1))
                chain.link(dve.tensor_tensor(mt.o[:, :, :], blocks(bank[:, 2, :]), over_columns(inv_sum[:, :]), ALU.mult))
                mt.norm_on_vector(dve, chain, s1(1, 1))
                for j in range(TB):
                    w = slice(j * P, T)
                    dve.wait_ge(s_z_sb, s1(4, j + 1))
                    dve.scalar_tensor_tensor(out=absz[:, j % 2, w], in0=z[:, j, w], scalar=-1.0, in1=z[:, j, w],
                                             op0=ALU.mult, op1=ALU.max).then_inc(s_abs, 1)
                    dve.wait_ge(s_ln, s1(4, j + 1))
                    dve.scalar_tensor_tensor(out=soft[:, j, w], in0=bank[:, 4 + j % 2, w], scalar=0.0, in1=absz[:, j % 2, w],
                                             op0=ALU.max, op1=ALU.add).then_inc(s_soft, 1)
                for j in range(TB):
                    w = slice(j * P, T)
                    dve.wait_ge(s_after, s1(4, j + 1))
                    dve.tensor_tensor(z[:, j, w], z[:, j, w], bank[:, 6 + j % 2, w], ALU.subtract).then_inc(s_arg, 1)
                dve.wait_ge(mt.s_turned, s1(1, 1))
                dve.tensor_scalar(mt.ot[:, :, :], blocks(bank[:, 4, :]), norm_now[:, 0:1], None, ALU.mult).then_inc(mt.s_ot, 1)
                dve.wait_ge(s_so, s1(1, 1))
                chain.link(dve.tensor_copy(st.o[:, :, :], blocks(bank[:, 5, :])))
                st.norm_on_vector(dve, chain, s1(1, 1))
                dve.wait_ge(st.s_turned, s1(1, 1))
                dve.tensor_scalar(st.ot[:, :, :], blocks(bank[:, 3, :]), norm_now[:, 1:2], None, ALU.mult).then_inc(st.s_ot, 1)
                return chain.n

            with dve.Fori(0, SH) as i:
                n = turn(i, 0)
            assert n == PER, n

        @block.gpsimd
        def _(pool):
            pool.tensor_tensor(before[:, :], core.tri_le[:, :], core.ident[:, :], ALU.subtract).then_inc(s_const, 1)
            pool.wait_ge(s_const, 1)
            pool.tensor_scalar(not_before[:, :], before[:, :], 1e30, -1e30, ALU.mult, ALU.add).then_inc(s_const, 1)
            pool.wait_ge(s_const, 2)
            pool.sem_inc(s_ot_free, 1)
            with pool.Fori(0, SH) as s:
                mt.on_gpsimd(pool, s)
                for j in range(TB):
                    d = soft[:, j, j * P:(j + 1) * P]
                    pool.wait_ge(s_soft, 4 * s + j + 1)
                    pool.tensor_tensor(d, d, before[:, :], ALU.mult).then_inc(s_masked, 1)
                for j in range(TB):
                    d = z[:, j, j * P:(j + 1) * P]
                    pool.wait_ge(s_arg, 4 * s + j + 1)
                    pool.tensor_tensor(d, d, not_before[:, :], ALU.add).then_inc(s_amasked, 1)
                mt.keep(pool, s, dram["o_kept"][s + GH + SH])
                st.on_gpsimd(pool, s)
                st.keep(pool, s, dram["o_kept"][s + GH])
                pool.wait_ge(mt.s_kept, 16 * s + 16)
                pool.wait_ge(st.s_kept, 16 * s + 16)
                pool.sem_inc(s_ot_free, 1)


def delta_net(core, dram):
    nc = core.nc
    bank = core.bank
    U0, UT = UNITS_ATT, 4
    Q, K, V, Z = range(4)
    PAD = TAPS - 1
    with phase(nc) as ctx:
        def sb(name, shape, dt=F32):
            return ctx.enter_context(nc.sbuf_tensor(name, shape, dt))

        def sem(name):
            return phase_semaphore(nc, ctx, "delta_" + name)

        level_mask = sb("level_mask", [P, LEVELS, P])
        wg, wg_hi, wg_lo = sb("wg", [P, KD, 2 * GH]), sb("wg_hi", [P, KD, 2 * GH], F32R), sb("wg_lo", [P, KD, 2 * GH], F32R)
        dt_bias, a_log = sb("dt_bias", [P, GH]), sb("a_log", [P, GH])
        gx, gabs, glog, gtotal, gbeta = (sb(n, [P, TB, GH]) for n in ("gx", "gabs", "glog", "gtotal", "gbeta"))
        gate_cols = sb("gate_cols", [P, GH, G_KINDS, TB])
        conv_w, norm_w = sb("conv_w", [P, GH * 3 * TAPS]), sb("gdn_norm_w", [P, 1])
        taps = sb("taps", [P, 3, TAPS])
        pre = sb("pre", [P, 4, PAD + T])
        y, th, squares = sb("y", [P, 4, T]), sb("th", [P, T]), sb("squares", [P, 2, T])
        log_row, beta_row = sb("log_row", [P, TB, P]), sb("beta_row", [P, TB, P])
        decay, decay_le, exp_run = sb("decay", [P, T]), sb("decay_le", [P, T]), sb("exp_run", [P, T])
        sq_sum, inv_norm = sb("sq_sum", [P, 2, TB]), sb("inv_norm", [P, 2, TB])
        col = sb("col", [P, 5, TB])
        now, gate = sb("col_now", [P, 5, TB]), sb("gate", [P, G_KINDS, TB])
        low_t, qk_t, q_run = sb("low_t", [P, T]), sb("qk_t", [P, T]), sb("q_run", [P, T])
        prod, inv, inv_t = sb("prod", [P, T]), sb("inv", [P, T]), sb("inv_t", [P, T])
        k_beta, k_end, v_beta = sb("k_beta", [P, T]), sb("k_end", [P, T]), sb("v_beta", [P, T])
        w_t, v_new, state = sb("w_t", [P, T]), sb("v_new", [P, T]), sb("state", [P, P])
        tail = RmsTail(core, ctx, "gdn", sb("gdn_sq", [P, TB, P]))
        C_RQ, C_RK, C_NEG_BETA, C_BETA_EXP, C_TO_END = range(5)

        s_params, s_chain, s_zero, s_ot_free = sem("params_loaded"), sem("dve_chain"), sem("pads_zeroed"), core.s_free["gdn_ot_free"]
        s_bank_free = core.s_free["gdn_bank_free"]
        s_g_in, s_g_split, s_g_proj, s_g_dve, s_g_act, s_g_sums = (
            sem(n) for n in ("gates_in", "gates_split", "gates_proj", "gates_dve", "gates_act", "gates_sums"))
        s_fill, s_cut = sem("masks_filled"), sem("masks_cut")
        s_copied = [sem(f"copied_{x}") for x in "qkvz"]
        s_conv, s_tanh, s_y = ([sem(f"{n}_{x}") for x in "qkvz"] for n in ("conv", "tanh", "silu"))
        s_squares, s_ssq, s_sum, s_inv_norm = sem("squares"), sem("square_sums"), sem("sums_plus_eps"), sem("inv_norms")
        s_log_row, s_beta_row, s_log_b, s_beta_b = sem("log_row"), sem("beta_row"), sem("log_broadcast"), sem("beta_broadcast")
        s_diff, s_exp, s_exp_run, s_decay, s_decay_le = sem("log_decay"), sem("decay_exp"), sem("run_exp"), sem("decay"), sem("decay_masked")
        s_q_run, s_turned_k, s_turned_v, s_kk, s_qk = sem("q_decayed"), sem("k_turned"), sem("v_turned"), sem("kk_ready"), sem("qk_ready")
        s_low, s_prod_mm, s_prod = sem("low_ready"), sem("prod_mm"), sem("prod_ready")
        s_x_mm, s_x, s_xt_mm, s_xt = sem("inv_mm"), sem("inv_ready"), sem("inv_t_mm"), sem("inv_t_ready")
        s_taken, s_w_mm, s_w = sem("kv_scaled"), sem("w_mm"), sem("w_ready")
        s_v_mm, s_v, s_s_mm, s_s, s_o = sem("v_new_mm"), sem("v_new_ready"), sem("state_mm"), sem("state_ready"), sem("o_ready")
        block = ctx.enter_context(nc.Block())

        def chunk(tile, n):
            return tile[:, n * P:(n + 1) * P]

        def kind(k):
            return gate_cols[:, :, k, :].rearrange("p h b -> p b h")

        def per_head(row):
            return row.unsqueeze(1).to_broadcast([P, TB, GH])

        def column(k, head):
            return gate_cols[:, bass.ds(head, 1), k, :].rearrange("p h b -> p (h b)")

        @block.sync
        def _(sp):
            sp.dma_start(wg[:, :, :], dram["w_gates"]).then_inc(s_g_in, 16)
            sp.dma_start(dt_bias[:, :], dram["dt_bias"].partition_broadcast(P)).then_inc(s_g_in, 16)
            sp.dma_start(a_log[:, :], dram["a_log"].partition_broadcast(P)).then_inc(s_g_in, 16)
            sp.dma_start(conv_w[:, :], dram["conv_w"]).then_inc(s_params, 16)
            sp.dma_start(norm_w[:, :], dram["gdn_norm_w"]).then_inc(s_params, 16)
            with sp.Fori(0, GH - 1) as i:
                for u in range(UT):
                    core.load_unit(sp, dram["w_gdn"][i * UT + u + 2], U0 + 2 + u, UT, i)
            for u in range(UT):
                n = (GH - 1) * UT + u + 2
                src = dram["w_gdn"][n] if n < UNITS_GDN else dram["w_out"][n - UNITS_GDN, 0]
                core.load_unit(sp, src, U0 + n)

        @block.tensor
        def _(pe):
            def broadcast_logs(h):
                pe.wait_ge(s_log_row, h)
                pe.matmul(bank[:, 2, :], core.ones[:, :], log_row[:, :, :], start=True, stop=True).then_inc(s_log_b, 1)

            def broadcast_betas(h):
                pe.wait_ge(s_beta_row, h)
                pe.matmul(bank[:, 3, :], core.ones[:, :], beta_row[:, :, :], start=True, stop=True).then_inc(s_beta_b, 1)

            def square_sums(h):
                pe.wait_ge(s_squares, h)
                for x in (Q, K):
                    for n in range(TB):
                        mm = pe.matmul(bank[:, 3, TB * x + n:TB * x + n + 1], chunk(squares[:, x, :], n), core.ones[:, 0:1],
                                       start=True, stop=True)
                mm.then_inc(s_ssq, 1)

            def turn(i, base, project):
                s1 = lambda m, k: at(m * base + k, m, i)
                c = U0 + UT * (base + 1)
                filled = [0]

                def fill(n):
                    while project and n > 0:
                        u, m = divmod(filled[0], 48)
                        e = min(48, m + n)
                        if m == 0 and u >= 2:
                            pe.wait_ge(s_copied[u - 2], s1(1, 2))
                        core.by_feature(pe, bank[:, u % 2, :], c + u, UT, i, (m, e))
                        filled[0] += e - m
                        n -= e - m

                for x in (Q, K, V):
                    pe.wait_ge(s_y[x], s1(1, 1))
                for n in range(TB):
                    mm = pe.matmul(chunk(bank[:, 5, :], n), chunk(y[:, K, :], n), chunk(y[:, K, :], n), start=True, stop=True)
                mm.then_inc(s_kk, 1)
                for n in range(TB):
                    mm = pe.transpose(chunk(bank[:, 7, :], n), chunk(y[:, V, :], n), core.ident[:, :])
                mm.then_inc(s_turned_v, 1)
                for n in range(TB):
                    mm = pe.matmul(chunk(bank[:, 4, :], n), chunk(y[:, K, :], n), chunk(y[:, Q, :], n), start=True, stop=True)
                mm.then_inc(s_qk, 1)
                fill(FILL_FIRST)
                pe.wait_ge(s_bank_free, s1(1, 1))
                for n in range(TB):
                    mm = pe.transpose(chunk(bank[:, 6, :], n), chunk(y[:, K, :], n), core.ident[:, :])
                mm.then_inc(s_turned_k, 1)
                for lv in range(LEVELS):
                    fill(FILL_LEVEL)
                    if lv == 0:
                        pe.wait_ge(s_low, s1(1, 1))
                    else:
                        pe.wait_ge(s_x, s1(LEVELS - 1, lv))
                    for n in range(TB):
                        if lv == 0:
                            mm = pe.transpose(chunk(bank[:, 2, :], n), chunk(low_t, n), core.ident[:, :])
                        else:
                            mm = pe.matmul(chunk(bank[:, 2, :], n), chunk(low_t, n), chunk(inv, n), start=True, stop=True)
                    mm.then_inc(s_prod_mm, 1)
                    fill(FILL_LEVEL)
                    pe.wait_ge(s_prod, s1(LEVELS, lv + 1))
                    if lv:
                        pe.wait_ge(s_xt, s1(LEVELS, lv))
                        if lv < LEVELS - 1:
                            for n in range(TB):
                                mm = pe.matmul(chunk(bank[:, 3, :], n), chunk(inv_t, n), chunk(prod, n), start=True, stop=True)
                            mm.then_inc(s_x_mm, 1)
                    for n in range(TB):
                        if lv == 0:
                            mm = pe.transpose(chunk(bank[:, 5, :], n), chunk(prod, n), core.ident[:, :])
                        else:
                            mm = pe.matmul(chunk(bank[:, 5, :], n), chunk(prod, n), chunk(inv_t, n), start=True, stop=True)
                    mm.then_inc(s_xt_mm, 1)
                if project:
                    broadcast_logs(s1(1, 2))
                pe.wait_ge(s_xt, s1(LEVELS, LEVELS))
                pe.wait_ge(s_taken, s1(4, 4))
                for n in range(TB):
                    mm = pe.matmul(chunk(bank[:, 6, :], n), chunk(k_beta, n), chunk(inv_t, n), start=True, stop=True)
                mm.then_inc(s_w_mm, 1)
                for n in range(TB):
                    if n == 1:
                        pe.wait_ge(s_w, s1(1, 1))
                        pe.wait_ge(s_q_run, s1(1, 1))
                    if n:
                        pe.wait_ge(s_s, s1(TB - 1, n))
                    mm = pe.matmul(chunk(bank[:, 7, :], n), chunk(inv_t, n), chunk(v_beta, n), start=True, stop=(n == 0))
                    if n:
                        mm = pe.matmul(chunk(bank[:, 7, :], n), chunk(w_t, n), state[:, :], start=False, stop=True)
                    mm.then_inc(s_v_mm, 1)
                    if n:
                        pe.matmul(chunk(bank[:, 4, :], n), chunk(q_run, n), state[:, :], start=True, stop=False)
                    fill(FILL_CHUNK)
                    pe.wait_ge(s_v, s1(TB, n + 1))
                    if n < TB - 1:
                        pe.matmul(bank[:, 5, 0:P], chunk(k_end, n), chunk(v_new, n), start=True, stop=True).then_inc(s_s_mm, 1)
                    mm = pe.matmul(chunk(bank[:, 4, :], n), chunk(qk_t, n), chunk(v_new, n), start=(n == 0), stop=True)
                    if n == 1 and project:
                        square_sums(s1(1, 2))
                mm.then_inc(s_o, 1)
                if project:
                    broadcast_betas(s1(1, 2))
                tail.turn(pe, s1(1, 0), bank[:, 6, :])
                assert not project or filled[0] == 4 * 48

            pe.wait_ge(s_g_split, 2)
            for b in range(TB):
                for k in range(KD):
                    for term, (x, w) in enumerate(((core.act_hi, wg_hi), (core.act_hi, wg_lo), (core.act_lo, wg_hi))):
                        mm = pe.matmul(bank[:, 2, b * 2 * GH:(b + 1) * 2 * GH], x[:, k, b * P:(b + 1) * P], w[:, k, :],
                                       start=(k == 0 and term == 0), stop=(k == KD - 1 and term == 2))
            mm.then_inc(s_g_proj, 1)
            core.by_feature(pe, bank[:, 0, :], U0)
            pe.wait_ge(s_g_dve, 6)
            flat = glog[:, :, :].rearrange("p b h -> p (b h)")
            pe.matmul(bank[:, 3, 0:TB * GH], core.tri_le[:, :], flat, start=True, stop=True).then_inc(s_g_sums, 1)
            pe.matmul(bank[:, 4, 0:TB * GH], core.ones[:, :], flat, start=True, stop=True).then_inc(s_g_sums, 1)
            for u in range(1, UT):
                if u >= 2:
                    pe.wait_ge(s_copied[u - 2], 1)
                core.by_feature(pe, bank[:, u % 2, :], U0 + u)
                if u == 2:
                    broadcast_logs(1)
            square_sums(1)
            broadcast_betas(1)
            with pe.Fori(0, GH - 1) as i:
                turn(i, 0, True)
            turn(None, GH - 1, False)

        @block.scalar
        def _(act):
            def copied(u, h, used, per, i):
                act.wait_ge(core.s_used, at(used, per, i))
                act.activation(pre[:, u, PAD:PAD + T], bank[:, u % 2, :], ACT.Copy).then_inc(s_copied[u], 1)

            def tanh(x, h):
                act.wait_ge(s_conv[x], h)
                act.activation(th[:, :], y[:, x, :], ACT.Tanh, scale=0.5).then_inc(s_tanh[x], 1)

            def tanh_z(h):
                act.wait_ge(s_y[V], h)
                act.wait_ge(s_copied[Z], h)
                act.activation(th[:, :], pre[:, Z, PAD:PAD + T], ACT.Tanh, scale=0.5).then_inc(s_tanh[Z], 1)

            def square(h):
                act.wait_ge(s_y[Q], h)
                act.wait_ge(s_y[K], h)
                act.activation(squares[:, :, :], y[:, Q:K + 1, :], ACT.Square, scale=0.5).then_inc(s_squares, 1)

            def exp_of_runs(h):
                act.wait_ge(s_log_b, h)
                act.activation(exp_run[:, :], bank[:, 2, :], ACT.Exp).then_inc(s_exp_run, 1)

            def exp_of_decays(h):
                act.wait_ge(s_diff, h)
                act.activation(decay[:, :], decay[:, :], ACT.Exp).then_inc(s_exp, 1)

            def turn(i, base, project):
                s1 = lambda m, k: at(m * base + k, m, i)
                c = U0 + UT * (base + 1)

                def take(u):
                    if project:
                        copied(u, None, c + u + 1, UT, i)
                        core.split_hi(act, c + u + 2, UT, i)

                def take_w():
                    act.wait_ge(s_w_mm, s1(1, 1))
                    act.activation(w_t[:, :], bank[:, 6, :], ACT.Copy, scale=-1.0).then_inc(s_w, 1)

                tanh_z(s1(1, 1))
                if not project:
                    take_w()
                    return
                h = s1(1, 2)
                take(0)
                tanh(Q, h)
                take(1)
                tanh(K, h)
                take(2)
                exp_of_runs(h)
                take_w()
                square(h)
                exp_of_decays(h)
                tanh(V, h)
                take(3)

            act.preload_act_table_set("natural_log_exp_and_others")
            act.wait_ge(s_g_in, 48)
            act.activation(wg_hi[:, :, :], wg[:, :, :], ACT.Copy).then_inc(s_g_split, 1)
            act.activation(a_log[:, :], a_log[:, :], ACT.Exp).then_inc(s_g_act, 1)
            act.wait_ge(s_g_dve, 3)
            act.activation(gabs[:, :, :], gabs[:, :, :], ACT.Exp, scale=-1.0).then_inc(s_g_act, 1)
            act.wait_ge(s_g_act, 2)
            act.activation(gabs[:, :, :], gabs[:, :, :], ACT.Ln, bias=1.0).then_inc(s_g_act, 1)
            act.activation(gbeta[:, :, :], gbeta[:, :, :], ACT.Exp, scale=-1.0).then_inc(s_g_act, 1)
            act.preload_act_table_set("exp_and_others")
            copied(0, 1, U0 + 1, 0, None)
            core.split_hi(act, U0 + 2)
            act.wait_ge(s_g_dve, 13)
            act.activation(gx[:, :, :], gx[:, :, :], ACT.Exp).then_inc(s_g_act, 1)
            act.activation(gabs[:, :, :], gabs[:, :, :], ACT.Exp).then_inc(s_g_act, 1)
            act.activation(gtotal[:, :, :], gtotal[:, :, :], ACT.Exp).then_inc(s_g_act, 1)
            tanh(Q, 1)
            copied(1, 1, U0 + 2, 0, None)
            core.split_hi(act, U0 + 3)
            tanh(K, 1)
            square(1)
            copied(2, 1, U0 + 3, 0, None)
            core.split_hi(act, U0 + 4)
            exp_of_runs(1)
            exp_of_decays(1)
            tanh(V, 1)
            copied(3, 1, U0 + 4, 0, None)
            core.split_hi(act, U0 + 5)
            with act.Fori(0, GH - 1) as i:
                turn(i, 0, True)
            turn(None, GH - 1, False)

        @block.vector
        def _(dve):
            n_taps = 3 * TAPS

            def conv(chain, x, h, some):
                if some[0] == 0:
                    dve.wait_ge(s_copied[x], h)
                for tap in some:
                    src, w = pre[:, x, tap:tap + T], taps[:, x, tap:tap + 1]
                    if tap == 0:
                        ins = dve.tensor_scalar(y[:, x, :], src, w, None, ALU.mult)
                    else:
                        ins = dve.scalar_tensor_tensor(out=y[:, x, :], in0=src, scalar=w, in1=y[:, x, :],
                                                       op0=ALU.mult, op1=ALU.add)
                    if tap == TAPS - 1:
                        ins.then_inc(s_conv[x], 1)
                    else:
                        chain.link(ins)

            def silu(x, h):
                dve.wait_ge(s_tanh[x], h)
                src = pre[:, Z, PAD:PAD + T] if x == Z else y[:, x, :]
                dve.scalar_tensor_tensor(out=y[:, x, :], in0=th[:, :], scalar=1.0, in1=src,
                                         op0=ALU.add, op1=ALU.mult).then_inc(s_y[x], 1)

            def log_rows(h):
                dve.tensor_tensor(log_row[:, :, :], over_blocks(core.tri_le[:, :]), over_columns(column(G_LOG, h)), ALU.mult).then_inc(s_log_row, 1)

            def decays(chain, head, h):
                dve.wait_ge(s_log_b, h)
                dve.wait_ge(s_exp_run, h)
                chain.link(dve.tensor_tensor(blocks(decay[:, :]), blocks(bank[:, 2, :]), over_columns(column(G_RUN, head)), ALU.subtract))
                dve.tensor_scalar(decay[:, :], decay[:, :], 0.0, None, ALU.min).then_inc(s_diff, 1)

            def norms(h):
                dve.wait_ge(s_ssq, h)
                dve.tensor_scalar(sq_sum[:, :, :], bank[:, 3, 0:2 * TB].rearrange("p (x b) -> p x b", x=2), RMS_EPS, None,
                                  ALU.add).then_inc(s_sum, 1)

            def columns(chain, head, h):
                dve.wait_ge(s_inv_norm, h)
                chain.mark(dve.tensor_scalar(col[:, C_RQ, :], inv_norm[:, Q, :], 0.5 * SCALE, None, ALU.mult))
                chain.link(dve.tensor_scalar(col[:, C_RK, :], inv_norm[:, K, :], 0.5, None, ALU.mult))
                chain.mark(dve.tensor_tensor(col[:, C_NEG_BETA, :], column(G_NEG_BETA, head), col[:, C_RK, :], ALU.mult))
                chain.mark(dve.tensor_tensor(col[:, C_BETA_EXP, :], column(G_BETA_EXP, head), col[:, C_RK, :], ALU.mult))
                chain.mark(dve.tensor_tensor(col[:, C_TO_END, :], column(G_TO_END, head), col[:, C_RK, :], ALU.mult))
                chain.wait()
                dve.tensor_tensor(beta_row[:, :, :], over_blocks(core.ident[:, :]), over_columns(col[:, C_NEG_BETA, :]), ALU.mult).then_inc(s_beta_row, 1)
                dve.wait_ge(s_exp, h)
                dve.tensor_tensor(blocks(decay[:, :]), blocks(decay[:, :]), over_columns(col[:, C_RK, :]), ALU.mult).then_inc(s_decay, 1)

            def turn(i, base, project, start, per):
                s1 = lambda m, k: at(m * base + k, m, i)
                c = U0 + UT * (base + 1)
                chain = Chain(dve, s_chain, start + per * base, per, i)
                h, head = s1(1, 2), s1(1, 1)

                def split(u):
                    core.split_lo(dve, c + u + 2, UT, i)

                chain.mark(dve.tensor_copy(gate[:, :, :], gate_cols[:, bass.ds(s1(1, 0), 1), :, :].rearrange("p h k b -> p (h k) b")))
                chain.mark(dve.tensor_copy(now[:, :, :], col[:, :, :]))
                dve.wait_ge(s_kk, s1(1, 1))
                dve.wait_ge(s_decay, s1(1, 1))
                chain.link(dve.tensor_tensor(low_t[:, :], bank[:, 5, :], decay[:, :], ALU.mult))
                dve.wait_ge(s_beta_b, s1(1, 1))
                dve.tensor_tensor(low_t[:, :], low_t[:, :], bank[:, 3, :], ALU.mult).then_inc(s_low, 1)
                if project:
                    chain.link(dve.tensor_copy(taps[:, :, :].rearrange("p c k -> p (c k)"), conv_w[:, bass.ds(s1(n_taps, n_taps), n_taps)]))
                for lv in range(LEVELS):
                    dve.wait_ge(s_prod_mm, s1(LEVELS, lv + 1))
                    mask = level_mask[:, lv, :].unsqueeze(1).to_broadcast([P, TB, P])
                    dve.tensor_tensor(blocks(prod[:, :]), blocks(bank[:, 2, :]), mask, ALU.mult).then_inc(s_prod, 1)
                    if lv == 0:
                        dve.wait_ge(s_prod, s1(LEVELS, 1))
                        dve.tensor_tensor(blocks(inv[:, :]), blocks(prod[:, :]), over_blocks(core.ident[:, :]), ALU.add).then_inc(s_x, 1)
                        dve.wait_ge(s_turned_k, s1(1, 1))
                        dve.tensor_tensor(blocks(k_beta[:, :]), blocks(bank[:, 6, :]), over_columns(now[:, C_BETA_EXP, :]), ALU.mult).then_inc(s_taken, 1)
                    elif lv < LEVELS - 1:
                        dve.wait_ge(s_x_mm, s1(LEVELS - 2, lv))
                        dve.tensor_tensor(inv[:, :], inv[:, :], bank[:, 3, :], ALU.add).then_inc(s_x, 1)
                    dve.wait_ge(s_xt_mm, s1(LEVELS, lv + 1))
                    x_t = blocks(inv_t[:, :]) if lv else over_blocks(core.ident[:, :])
                    dve.tensor_tensor(blocks(inv_t[:, :]), x_t, blocks(bank[:, 5, :]), ALU.add).then_inc(s_xt, 1)
                    if lv == 1:
                        dve.tensor_tensor(blocks(k_end[:, :]), blocks(bank[:, 6, :]), over_columns(now[:, C_TO_END, :]), ALU.mult).then_inc(s_taken, 1)
                        dve.wait_ge(s_turned_v, s1(1, 1))
                        dve.tensor_tensor(blocks(v_beta[:, :]), blocks(bank[:, 7, :]), over_columns(gate[:, G_BETA_HALF, :]), ALU.mult).then_inc(s_taken, 1)
                        silu(Z, s1(1, 1))
                    if lv == 2:
                        dve.wait_ge(s_qk, s1(1, 1))
                        dve.wait_ge(s_decay_le, s1(1, 1))
                        dve.tensor_tensor(qk_t[:, :], bank[:, 4, :], decay_le[:, :], ALU.mult).then_inc(s_taken, 1)
                        if project:
                            dve.wait_ge(s_q_run, s1(1, 1))
                            split(0)
                            conv(chain, Q, h, (0, 1))
                    if project and lv == 3:
                        conv(chain, Q, h, (2, 3))
                    if project and lv == 4:
                        silu(Q, h)
                        split(1)
                        conv(chain, K, h, (0,))
                    if project and lv == 5:
                        conv(chain, K, h, (1, 2, 3))
                        log_rows(head)
                if project:
                    silu(K, h)
                    split(2)
                for n in range(TB):
                    dve.wait_ge(s_v_mm, s1(TB, n + 1))
                    dve.tensor_copy(chunk(v_new, n), chunk(bank[:, 7, :], n)).then_inc(s_v, 1)
                    if n < TB - 1:
                        dve.wait_ge(s_s_mm, s1(TB - 1, n + 1))
                        if n == 0:
                            dve.tensor_copy(state[:, :], bank[:, 5, 0:P]).then_inc(s_s, 1)
                        else:
                            dve.wait_ge(s_s, s1(TB - 1, n))
                            dve.scalar_tensor_tensor(out=state[:, :], in0=state[:, :], scalar=gate[:, G_TOTAL, n:n + 1],
                                                     in1=bank[:, 5, 0:P], op0=ALU.mult, op1=ALU.add).then_inc(s_s, 1)
                    if project and n == 0:
                        conv(chain, V, h, (0, 1))
                    if project and n == 1:
                        conv(chain, V, h, (2, 3))
                        norms(h)
                    if project and n == 2:
                        decays(chain, head, h)
                if project:
                    columns(chain, head, h)
                dve.wait_ge(s_o, s1(1, 1))
                chain.link(dve.tensor_tensor(tail.o[:, :, :], blocks(bank[:, 4, :]), over_columns(now[:, C_RQ, :]), ALU.mult))
                tail.norm_on_vector(dve, chain, s1(1, 1))
                if project:
                    silu(V, h)
                    split(3)
                dve.wait_ge(tail.s_turned, s1(1, 1))
                dve.wait_ge(s_ot_free, s1(1, 1))
                dve.scalar_tensor_tensor(out=tail.ot[:, :, :], in0=blocks(bank[:, 6, :]), scalar=norm_w[:, 0:1],
                                         in1=blocks(y[:, Z, :]), op0=ALU.mult, op1=ALU.mult).then_inc(tail.s_ot, 1)
                return chain.n

            g_links = [0]

            def link(ins):
                g_links[0] += 1
                ins.then_inc(s_g_dve, 1)
                dve.wait_ge(s_g_dve, g_links[0])

            dve.memset(pre[:, :, 0:PAD], 0.0).then_inc(s_zero, 1)
            dve.wait_ge(s_g_split, 1)
            dve.tensor_tensor(wg_lo[:, :, :], wg[:, :, :], wg_hi[:, :, :].bitcast(F32), ALU.subtract).then_inc(s_g_split, 1)
            dve.wait_ge(s_g_proj, 1)
            ab = bank[:, 2, 0:TB * 2 * GH].rearrange("p (b k h) -> p b k h", b=TB, k=2)
            link(dve.tensor_tensor(gx[:, :, :], ab[:, :, 0, :], per_head(dt_bias[:, :]), ALU.add))
            link(dve.scalar_tensor_tensor(out=gabs[:, :, :], in0=gx[:, :, :], scalar=-1.0, in1=gx[:, :, :],
                                          op0=ALU.mult, op1=ALU.max))
            link(dve.tensor_copy(gbeta[:, :, :], ab[:, :, 1, :]))
            dve.wait_ge(s_g_act, 3)
            link(dve.scalar_tensor_tensor(out=glog[:, :, :], in0=gx[:, :, :], scalar=0.0, in1=gabs[:, :, :],
                                          op0=ALU.max, op1=ALU.add))
            link(dve.tensor_tensor(glog[:, :, :], glog[:, :, :], per_head(a_log[:, :]), ALU.mult))
            link(dve.tensor_scalar(glog[:, :, :], glog[:, :, :], -1.0, None, ALU.mult))
            dve.wait_ge(s_g_act, 4)
            link(dve.tensor_scalar(gbeta[:, :, :], gbeta[:, :, :], 1.0, None, ALU.add))
            link(dve.reciprocal(gbeta[:, :, :], gbeta[:, :, :]))
            link(dve.tensor_scalar(kind(G_BETA_HALF), gbeta[:, :, :], 0.5, None, ALU.mult))
            link(dve.tensor_scalar(kind(G_NEG_BETA), gbeta[:, :, :], -1.0, None, ALU.mult))
            dve.wait_ge(s_g_sums, 2)
            run = bank[:, 3, 0:TB * GH].rearrange("p (b h) -> p b h", b=TB)
            link(dve.tensor_copy(gx[:, :, :], run))
            link(dve.tensor_copy(gtotal[:, :, :], bank[:, 4, 0:TB * GH].rearrange("p (b h) -> p b h", b=TB)))
            link(dve.tensor_tensor(gabs[:, :, :], gtotal[:, :, :], gx[:, :, :], ALU.subtract))
            link(dve.tensor_copy(kind(G_RUN), run))
            link(dve.tensor_copy(kind(G_LOG), glog[:, :, :]))
            log_rows(0)
            core.split_lo(dve, U0 + 2)
            dve.wait_ge(s_g_act, 7)
            link(dve.tensor_tensor(kind(G_BETA_EXP), gbeta[:, :, :], gx[:, :, :], ALU.mult))
            link(dve.tensor_copy(kind(G_TO_END), gabs[:, :, :]))
            link(dve.tensor_copy(kind(G_TOTAL), gtotal[:, :, :]))
            chain = Chain(dve, s_chain, 0)
            dve.wait_ge(s_zero, 1)
            dve.wait_ge(s_params, 32)
            dve.wait_ge(s_cut, 2 * LEVELS)
            chain.link(dve.tensor_scalar(norm_w[:, :], norm_w[:, :], 0.5, None, ALU.mult))
            chain.link(dve.tensor_copy(taps[:, :, :].rearrange("p c k -> p (c k)"), conv_w[:, 0:n_taps]))
            conv(chain, Q, 1, range(TAPS))
            silu(Q, 1)
            core.split_lo(dve, U0 + 3)
            conv(chain, K, 1, range(TAPS))
            silu(K, 1)
            core.split_lo(dve, U0 + 4)
            decays(chain, 0, 1)
            conv(chain, V, 1, range(TAPS))
            silu(V, 1)
            norms(1)
            columns(chain, 0, 1)
            core.split_lo(dve, U0 + 5)
            PER = 22
            with dve.Fori(0, GH - 1) as i:
                n = turn(i, 0, True, chain.n, PER)
            assert n == PER, n
            turn(None, GH - 1, False, chain.n, PER)

        @block.gpsimd
        def _(pool):
            def inv_norms(h):
                pool.wait_ge(s_sum, h)
                pool.tensor_tensor(inv_norm[:, :, :], sq_sum[:, :, :], core.half_neg[:, :].rearrange("p (x b) -> p x b", x=2), ALU.pow).then_inc(s_inv_norm, 1)

            def masked_decay(h):
                pool.wait_ge(s_decay, h)
                pool.tensor_tensor(blocks(decay_le[:, :]), blocks(decay[:, :]), over_blocks(core.tri_le[:, :]), ALU.mult).then_inc(s_decay_le, 1)

            def turn(i, base, project):
                s1 = lambda m, k: at(m * base + k, m, i)
                pool.wait_ge(s_y[Q], s1(1, 1))
                pool.wait_ge(s_exp_run, s1(1, 1))
                pool.tensor_tensor(q_run[:, :], y[:, Q, :], exp_run[:, :], ALU.mult).then_inc(s_q_run, 1)
                if project:
                    inv_norms(s1(1, 2))
                    masked_decay(s1(1, 2))
                tail.on_gpsimd(pool, s1(1, 0))
                pool.wait_ge(tail.s_ot, s1(1, 1))
                pool.sem_inc(s_bank_free, 1)
                tail.keep(pool, s1(1, 0), dram["o_kept"][s1(1, 0)])
                pool.wait_ge(tail.s_kept, s1(16, 16))
                pool.sem_inc(s_ot_free, 1)

            pool.memset(level_mask[:, :, :], 0.0).then_inc(s_fill, 1)
            pool.wait_ge(s_fill, 1)
            for lv in range(LEVELS):
                s = 1 << lv
                n = P // (2 * s)
                low = level_mask[:, lv, :].rearrange("p (n s) -> p n s", s=2 * s)[:, :, 0:s]
                pool.memset(low, 1.0).then_inc(s_fill, 1)
                pool.wait_ge(s_fill, lv + 2)
                pool.affine_select(out=low, in_=low, compare_op=ALU.is_ge, fill=0.0, base=-s,
                                   pattern=[[-2 * s, n], [0, s]], channel_multiplier=1).then_inc(s_cut, 1)
                pool.wait_ge(s_cut, 2 * lv + 1)
                pool.affine_select(out=low, in_=low, compare_op=ALU.is_ge, fill=0.0, base=2 * s - 1,
                                   pattern=[[2 * s, n], [0, s]], channel_multiplier=-1).then_inc(s_cut, 1)
            pool.sem_inc(s_ot_free, 1)
            pool.sem_inc(s_bank_free, 1)
            inv_norms(1)
            masked_decay(1)
            with pool.Fori(0, GH - 1) as i:
                turn(i, 0, True)
            turn(None, GH - 1, False)


def mix_out(core, dram):
    nc = core.nc
    bank = core.bank
    U0 = UNITS_ATT + UNITS_GDN
    STAGES = 4
    with phase(nc) as ctx:
        def sb(name, shape, dt=F32):
            return ctx.enter_context(nc.sbuf_tensor(name, shape, dt))

        def sem(name):
            return phase_semaphore(nc, ctx, "mix_out_" + name)

        rows, staged = sb("mix_rows", [P, TB, D]), sb("o_staged", [P, STAGES, T])
        ln_w, ln_b = sb("ln1_w", [P, D]), sb("ln1_b", [P, D])
        ln = LayerNorm(core, ctx, "ln1")
        s_params, s_rows, s_chain = sem("params_loaded"), sem("h_loaded"), sem("dve_chain")
        s_o = [sem(f"o_loaded{n}") for n in range(STAGES)]
        s_o_hi, s_o_lo, s_added = sem("o_hi"), sem("o_lo"), core.s_free["mix_added"]
        s_normed, s_turned, s_t_hi, s_t_lo, s_kept = sem("h1_normed"), sem("h1_turned"), sem("turned_hi"), sem("turned_lo"), sem("h1_kept")
        block = ctx.enter_context(nc.Block())

        def slots(n, q):
            return [a[:, 4 * q:4 * q + 4, n * P:(n + 1) * P] for a in (core.act_hi, core.act_lo)]

        def low_part(dve, u):
            dve.wait_ge(s_t_hi, u + 1)
            hi, lo = slots(u // 4, u % 4)
            dve.tensor_tensor(lo, blocks(bank[:, u % 2, :]), hi.bitcast(F32), ALU.subtract).then_inc(s_t_lo, 1)

        @block.sync
        def _(sp):
            for h in range(HEADS):
                if h >= STAGES:
                    sp.wait_ge(s_o_lo, h - STAGES + 1)
                sp.dma_start(staged[:, h % STAGES, :], dram["o_kept"][h]).then_inc(s_o[h % STAGES], 16)
            sp.dma_start(rows[:, :, :], dram["h_kept"].rearrange("(b p) d -> p b d", p=P)).then_inc(s_rows, 16)
            sp.dma_start(ln_w[:, :], dram["ln1_w"].partition_broadcast(P)).then_inc(s_params, 16)
            sp.dma_start(ln_b[:, :], dram["ln1_b"].partition_broadcast(P)).then_inc(s_params, 16)
            for u in range(UNITS_OUT):
                n = u + 2
                src = dram["w_out"][n % DB, n // DB] if n < UNITS_OUT else dram["peer_wq"][n - UNITS_OUT]
                core.load_unit(sp, src, U0 + n)
            for n in range(TB):
                sp.wait_ge(s_normed, n + 1)
                sp.dma_start(dram["h1_kept"][n * P:(n + 1) * P, :], rows[:, n, :]).then_inc(s_kept, 16)
            sp.wait_ge(s_kept, 16 * TB)

        @block.tensor
        def _(pe):
            pe.wait_ge(s_o_lo, HEADS)
            with pe.Fori(0, 2) as i:
                for d in range(2):
                    pe.wait_ge(s_added, i * 8 + 4 * d + 4)
                    for q in range(DB):
                        core.by_token(pe, [bank[:, 4 * d + b, :] for b in range(TB)],
                                      core.act_hi[:, 4 * q:4 * q + 4, :], core.act_lo[:, 4 * q:4 * q + 4, :],
                                      q == 0, q == DB - 1, U0 + 4 * d + q, 8, i)
            for n in range(TB):
                pe.wait_ge(s_normed, n + 1)
                for q in range(4):
                    u = 4 * n + q
                    if u >= 2:
                        pe.wait_ge(s_t_lo, u - 1)
                    for j in range(4):
                        k = 4 * q + j
                        mm = pe.transpose(bank[:, u % 2, j * P:(j + 1) * P], rows[:, n, k * P:(k + 1) * P], core.ident[:, :])
                    mm.then_inc(s_turned, 1)

        @block.scalar
        def _(act):
            for h in range(HEADS):
                act.wait_ge(s_o[h % STAGES], 16 * (h // STAGES + 1))
                act.activation(core.act_hi[:, h, :], staged[:, h % STAGES, :], ACT.Copy).then_inc(s_o_hi, 1)
            with act.Fori(0, 2) as i:
                for u in range(8):
                    core.split_hi(act, U0 + u + 2, 8, i)
            for u in range(4 * TB):
                act.wait_ge(s_turned, u + 1)
                act.activation(slots(u // 4, u % 4)[0], blocks(bank[:, u % 2, :]), ACT.Copy).then_inc(s_t_hi, 1)

        @block.vector
        def _(dve):
            dve.sem_inc(s_added, 8)
            for h in range(HEADS):
                dve.wait_ge(s_o_hi, h + 1)
                dve.tensor_tensor(core.act_lo[:, h, :], staged[:, h % STAGES, :], core.act_hi[:, h, :].bitcast(F32),
                                  ALU.subtract).then_inc(s_o_lo, 1)
            dve.wait_ge(s_rows, 16)
            with dve.Fori(0, 2) as i:
                for d in range(2):
                    for q in range(DB):
                        core.split_lo(dve, U0 + 4 * d + q + 2, 8, i)
                    dve.wait_ge(core.s_used, at(U0 + 4 * d + 4, 8, i))
                    for b in range(TB):
                        r = rows[:, b, bass.ds(i * 2 * COLS + d * COLS, COLS)]
                        dve.scalar_tensor_tensor(out=r, in0=r, scalar=ALPHA, in1=bank[:, 4 * d + b, :],
                                                 op0=ALU.mult, op1=ALU.add).then_inc(s_added, 1)
            dve.wait_ge(s_added, 8 + 16)
            dve.wait_ge(s_params, 32)
            chain = Chain(dve, s_chain, 0)
            for n in range(TB):
                ln.on_vector(dve, chain, n, rows[:, n, :], rows[:, n, :], ln_w[:, :], ln_b[:, :], s_normed)
                for q in range(4 * (n - 1), 4 * n) if n else ():
                    low_part(dve, q)
            for q in range(4 * (TB - 1), 4 * TB):
                low_part(dve, q)

        @block.gpsimd
        def _(pool):
            for n in range(TB):
                ln.on_gpsimd(pool, n)


def route(core, dram, chosen):
    nc = core.nc
    bank = core.bank
    U0, UT = UNITS_ATT + UNITS_GDN + UNITS_OUT, 2
    C = TOPK * TOPK
    with phase(nc) as ctx:
        def sb(name, shape, dt=F32):
            return ctx.enter_context(nc.sbuf_tensor(name, shape, dt))

        def sem(name):
            return phase_semaphore(nc, ctx, "route_" + name)

        keys, q_t = sb("keys", [P, 2, KEYS]), sb("q_t", [P, 2, T])
        score, left = sb("score", [P, 2 * TB, KEYS]), sb("left", [P, 2 * TB, KEYS])
        best, best_i, best_f = sb("best", [P, 2 * TB, TOPK]), sb("best_i", [P, 2 * TB, TOPK], U32), sb("best_f", [P, 2 * TB, TOPK])
        cand, cand_left = sb("cand", [P, TB, C]), sb("cand_left", [P, TB, C])
        top, pos = sb("top", [P, TB, TOPK]), sb("pos", [P, TB, TOPK], U32)
        rank_i, rank = sb("rank_i", [P, 2, TB, TOPK], U32), sb("rank", [P, 2, TB, TOPK])
        hit = sb("hit", [P, 2, TB, C])
        ex, total, inv = sb("ex", [P, TB, TOPK]), sb("total", [P, TB]), sb("inv_total", [P, TB])
        s_keys, s_chain, s_apart = sem("keys_loaded"), sem("dve_chain"), sem("waits_apart")
        s_q, s_score_mm, s_score, s_rank, s_hit, s_shifted, s_ex = (
            sem(n) for n in ("q_copied", "score_mm", "score_copied", "ranks_ready", "hits_ready", "top_shifted", "top_exp"))
        block = ctx.enter_context(nc.Block())

        def grid(tile):
            return tile.rearrange("p b (k a) -> p b k a", a=TOPK)

        def along_rank(tile):
            return tile.unsqueeze(3).to_broadcast([P, TB, TOPK, TOPK])

        def along_chosen(tile):
            return tile.unsqueeze(2).to_broadcast([P, TB, TOPK, TOPK])

        numbers = core.iota[:, 0:TOPK].unsqueeze(1).unsqueeze(1).to_broadcast([P, TB, TOPK, TOPK])

        @block.sync
        def _(sp):
            sp.dma_start(keys[:, :, :], dram["peer_keys"].rearrange("p (s k) -> p s k", s=2)).then_inc(s_keys, 16)
            with sp.Fori(0, PH - 1) as h:
                for u in range(UT):
                    core.load_unit(sp, dram["peer_wq"][h * UT + u + 2], U0 + u + 2, UT, h)
            for u in range(UT):
                core.load_unit(sp, dram["peer_u"][u], U0 + UNITS_Q + u)

        @block.tensor
        def _(pe):
            pe.wait_ge(s_keys, 16)
            with pe.Fori(0, PH) as h:
                for u in range(UT):
                    core.by_feature(pe, bank[:, u, :], U0 + u, UT, h)
                for u in range(UT):
                    pe.wait_ge(s_q, h * 2 + u + 1)
                    for b in range(TB):
                        mm = pe.matmul(bank[:, 2 + u, b * P:(b + 1) * P], q_t[:, u, b * P:(b + 1) * P], keys[:, u, :],
                                       start=True, stop=True)
                mm.then_inc(s_score_mm, 1)

        @block.scalar
        def _(act):
            with act.Fori(0, PH) as h:
                for u in range(UT):
                    act.wait_ge(core.s_used, at(U0 + u + 1, UT, h))
                    act.activation(q_t[:, u, :], bank[:, u, :], ACT.Copy).then_inc(s_q, 1)
                    core.split_hi(act, U0 + u + 2, UT, h)
                act.wait_ge(s_score_mm, h + 1)
                act.activation(score[:, :, :].rearrange("p b n -> p (b n)").rearrange("p (s n) -> p s n", s=2),
                               bank[:, 2:4, :], ACT.Copy).then_inc(s_score, 1)
                act.wait_ge(s_shifted, h + 1)
                act.activation(ex[:, :, :], ex[:, :, :], ACT.Exp).then_inc(s_ex, 1)

        @block.vector
        def _(dve):
            def top16(chain, x, spare, val, idx, n):
                for b in range(n):
                    chain.mark(dve.max(val[:, b, 0:8], x[:, b, :]))
                chain.wait_apart()
                for b in range(n):
                    chain.mark(dve.max_index(idx[:, b, 0:8], val[:, b, 0:8], x[:, b, :]))
                    chain.mark(dve.match_replace(spare[:, b, :], val[:, b, 0:8], x[:, b, :], NEG))
                chain.wait_apart()
                for b in range(n):
                    chain.mark(dve.max(val[:, b, 8:16], spare[:, b, :]))
                chain.wait_apart()
                for b in range(n):
                    chain.mark(dve.max_index(idx[:, b, 8:16], val[:, b, 8:16], spare[:, b, :]))
                chain.wait_apart()

            PER = 70
            with dve.Fori(0, PH) as h:
                chain = Chain(dve, s_chain, 0, PER, h, apart=s_apart)
                core.split_lo(dve, U0 + 2, UT, h)
                core.split_lo(dve, U0 + 3, UT, h)
                dve.wait_ge(s_score, h + 1)
                dve.sem_inc(s_apart, 1)
                top16(chain, score, left, best, best_i, 2 * TB)
                chain.mark(dve.tensor_copy(best_f[:, :, :], best_i[:, :, :]))
                chain.mark(dve.tensor_tensor(grid(cand[:, :, :]), along_rank(best[:, 0:TB, :]), along_chosen(best[:, TB:2 * TB, :]), ALU.add))
                chain.wait_apart()
                top16(chain, cand, cand_left, top, pos, TB)
                chain.mark(dve.tensor_scalar(rank_i[:, 0, :, :], pos[:, :, :], 4, None, ALU.logical_shift_right))
                chain.mark(dve.tensor_scalar(rank_i[:, 1, :, :], pos[:, :, :], TOPK - 1, None, ALU.bitwise_and))
                dve.tensor_tensor(ex[:, :, :], top[:, :, :], top[:, :, 0:1].to_broadcast([P, TB, TOPK]), ALU.subtract).then_inc(s_shifted, 1)
                chain.wait()
                chain.link(dve.tensor_copy(rank[:, :, :, :], rank_i[:, :, :, :]))
                for s in range(2):
                    dve.tensor_tensor(grid(hit[:, s, :, :]), along_rank(rank[:, s, :, :]), numbers, ALU.is_equal).then_inc(s_rank, 1)
                dve.wait_ge(s_ex, h + 1)
                chain.link(dve.tensor_reduce(total[:, :], ex[:, :, :], AX_X, ALU.add))
                chain.link(dve.reciprocal(inv[:, :], total[:, :]))
                here = bass.ds(h * TOPK, TOPK)
                chain.mark(dve.tensor_tensor(chosen[:, 2, :, here], ex[:, :, :], inv[:, :].unsqueeze(2).to_broadcast([P, TB, TOPK]), ALU.mult))
                for s in range(2):
                    dve.wait_ge(s_hit, h * 2 + s + 1)
                    chain.mark(dve.tensor_reduce(chosen[:, s, :, here], grid(hit[:, s, :, :]), AX_X, ALU.add))
                chain.wait()
            assert chain.n == PER, chain.n

        @block.gpsimd
        def _(pool):
            with pool.Fori(0, PH) as h:
                for s in range(2):
                    pool.wait_ge(s_rank, h * 2 + s + 1)
                    pool.tensor_tensor(grid(hit[:, s, :, :]), grid(hit[:, s, :, :]), along_chosen(best_f[:, s * TB:(s + 1) * TB, :]),
                                       ALU.mult).then_inc(s_hit, 1)


def spread(core, dram, chosen):
    nc = core.nc
    bank = core.bank
    QUADS = TG // 4
    with phase(nc) as ctx:
        def sb(name, shape, dt=F32):
            return ctx.enter_context(nc.sbuf_tensor(name, shape, dt))

        def sem(name):
            return phase_semaphore(nc, ctx, "spread_" + name)

        by_choice = sb("by_choice", [P, 3, T])
        now = sb("choices_now", [P, 2, 3, TG])
        row_hot, col_hot = sb("row_hot", [P, 2, 4, KEYS]), sb("col_hot", [P, 2, 4, KEYS])
        out = sb("gates_out", [P, 2, KEYS, TG])
        s_turned, s_by_choice, s_now = sem("chosen_turned"), sem("by_choice_copied"), sem("group_taken")
        s_hot, s_mm = sem("one_hots_ready"), core.s_free["spread_mm"]
        s_out, s_free = core.s_free["spread_copied"], core.s_free["spread_out_free"]
        s_kept = [sem("gates_kept_even"), sem("gates_kept_odd")]
        block = ctx.enter_context(nc.Block())

        @block.sync
        def _(sp):
            sp.sem_inc(s_free, 2)
            with sp.Fori(0, NTG // 2) as i:
                for par in range(2):
                    sp.wait_ge(s_out, i * 2 * QUADS + (par + 1) * QUADS + 4)
                    sp.dma_start(dram["gates_kept"][i * 2 + par], out[:, par, :, :]).then_inc(s_kept[par], 16)
                    sp.wait_ge(s_kept[par], i * 16 + 16)
                    sp.sem_inc(s_free, 1)

        @block.tensor
        def _(pe):
            for kind in range(3):
                for b in range(TB):
                    mm = pe.transpose(bank[:, kind, b * P:(b + 1) * P], chosen[:, kind, b, :], core.ident[:, :])
                mm.then_inc(s_turned, 1)
            pe.sem_inc(s_mm, 2)
            with pe.Fori(0, NTG // 2) as i:
                for q in range(2 * QUADS):
                    pe.wait_ge(s_hot, i * 2 * QUADS + q + 1)
                    pe.wait_ge(s_out, i * 2 * QUADS + q + 1)
                    for t in range(4):
                        mm = pe.matmul(bank[:, 4 + q % 4, t * P:(t + 1) * P], col_hot[:, q % 2, t, :], row_hot[:, q % 2, t, :],
                                       start=True, stop=True)
                    mm.then_inc(s_mm, 1)

        @block.scalar
        def _(act):
            for kind in range(3):
                act.wait_ge(s_turned, kind + 1)
                act.activation(by_choice[:, kind, :], bank[:, kind, :], ACT.Copy).then_inc(s_by_choice, 1)
            act.sem_inc(s_out, 4)
            with act.Fori(0, NTG // 2) as i:
                for q in range(2 * QUADS):
                    par, t = divmod(q, QUADS)
                    if t == 0:
                        act.wait_ge(s_free, i * 2 + par + 1)
                    act.wait_ge(s_mm, i * 2 * QUADS + q + 3)
                    act.activation(out[:, par, :, 4 * t:4 * t + 4], bank[:, 4 + q % 4, :].rearrange("p (t n) -> p n t", t=4),
                                   ACT.Copy).then_inc(s_out, 1)

        @block.vector
        def _(dve):
            dve.wait_ge(s_by_choice, 3)
            with dve.Fori(0, NTG // 2) as i:
                for par in range(2):
                    dve.wait_ge(s_mm, i * 2 * QUADS + par * QUADS + 1)
                    dve.tensor_copy(now[:, par, :, :], by_choice[:, :, bass.ds(i * 2 * TG + par * TG, TG)]).then_inc(s_now, 1)
                    dve.wait_ge(s_now, i * 2 + par + 1)
                    for q in range(QUADS):
                        n = par * QUADS + q
                        dve.wait_ge(s_mm, i * 2 * QUADS + n + 1)
                        for t in range(4):
                            c = 4 * q + t
                            dve.tensor_scalar(row_hot[:, n % 2, t, :], core.iota[:, :], now[:, par, 0, c:c + 1], None, ALU.is_equal)
                            ins = dve.tensor_scalar(col_hot[:, n % 2, t, :], core.iota[:, :], now[:, par, 1, c:c + 1],
                                                    now[:, par, 2, c:c + 1], ALU.is_equal, ALU.mult)
                        ins.then_inc(s_hot, 1)


def experts(core, dram, acc):
    nc = core.nc
    bank = core.bank
    E0 = UNITS_ATT + UNITS_GDN + UNITS_OUT + UNITS_Q
    with phase(nc) as ctx:
        def sb(name, shape, dt=F32):
            return ctx.enter_context(nc.sbuf_tensor(name, shape, dt))

        def sem(name):
            return phase_semaphore(nc, ctx, "experts_" + name)

        gates = sb("gates_in", [P, 2, NTG, EB, TG])
        gelu, weighted = sb("gelu", [P, 2, T]), sb("weighted", [P, 2, T])
        p_hi, p_lo = sb("p_hi", [P, 2, EB, T], F32R), sb("p_lo", [P, 2, EB, T], F32R)
        s_gates = [sem("gates_even"), sem("gates_odd")]
        s_acc, s_scaled = sem("h1_loaded"), sem("h1_scaled")
        s_gelu, s_weighted, s_p_hi, s_p_lo = sem("gelu_done"), sem("gates_applied"), sem("p_hi_done"), sem("p_lo_done")
        s_out, s_added = sem("out_block_ready"), core.s_free["expert_added"]
        block = ctx.enter_context(nc.Block())

        def u_unit(g, c):
            return (E0 + c, 0, None) if g == (0, 0, None) else (E0 + 4 + 8 * (g[0] - 1) + c, 8 * g[1], g[2])

        def v_unit(g, d):
            return (E0 + 4 + 8 * g[0] + (0 if g == (GROUPS - 1, 0, None) else 4) + d, 8 * g[1], g[2])

        def steps(eng, inner, outer):
            inner((0, 0, None))
            with eng.Fori(0, (GROUPS - 2) // 2) as j:
                for k in range(2):
                    inner((k + 1, 2, j))
                    outer((k, 2, j))
            inner((GROUPS - 1, 0, None))
            outer((GROUPS - 2, 0, None))
            outer((GROUPS - 1, 0, None))

        @block.sync
        def _(sp):
            sp.dma_start(acc[:, :, :], dram["h1_kept"].rearrange("(b p) d -> p b d", p=P)).then_inc(s_acc, 16)

            def load_gates(g):
                if g[0] >= 2 or g[2] is not None and g[0] + g[1] >= 2 and g[0] > 1:
                    sp.wait_ge(s_weighted, at(EB * (g[0] - 1), EB * g[1], g[2]))
                src = dram["gates_kept"][:, :, bass.ds(at(EB * g[0], EB * g[1], g[2]), EB), :]
                sp.dma_start(gates[:, g[0] % 2, :, :, :].rearrange("p g k t -> p g (k t)"),
                             src.rearrange("g p k t -> p g (k t)")).then_inc(s_gates[g[0] % 2], 16)

            def u_src(g, c):
                return dram["peer_u"][at(EB * g[0] + c, EB * g[1], g[2])]

            def v_src(g, d):
                return dram["peer_v"][at(g[0], g[1], g[2]), d]

            load_gates((0, 0, None))
            load_gates((1, 0, None))
            for c in (2, 3):
                core.load_unit(sp, u_src((0, 0, None), c), E0 + c)
            for c in (0, 1):
                core.load_unit(sp, u_src((1, 0, None), c), E0 + 4 + c)
            with sp.Fori(0, (GROUPS - 2) // 2) as j:
                for k in range(2):
                    g, before, after = (k + 1, 2, j), (k, 2, j), (k + 2, 2, j)
                    for c in (2, 3):
                        core.load_unit(sp, u_src(g, c), *u_unit(g, c))
                    load_gates(after)
                    for d in range(DB):
                        core.load_unit(sp, v_src(before, d), *v_unit(before, d))
                    for c in (0, 1):
                        core.load_unit(sp, u_src(after, c), *u_unit(after, c))
            last = (GROUPS - 1, 0, None)
            for c in (2, 3):
                core.load_unit(sp, u_src(last, c), *u_unit(last, c))
            for g in ((GROUPS - 2, 0, None), last):
                for d in range(DB):
                    core.load_unit(sp, v_src(g, d), *v_unit(g, d))

        @block.tensor
        def _(pe):
            def inner(g):
                for c in range(EB):
                    if c >= 2 or g[0]:
                        pe.wait_ge(s_gelu, at(EB * g[0] + c - 1, EB * g[1], g[2]))
                    core.by_feature(pe, bank[:, c % 2, :], *u_unit(g, c))

            def outer(g):
                for d in range(DB):
                    n, per, i = v_unit(g, d)
                    pe.wait_ge(core.s_lo, at(n + 1, per, i))
                    if d == 0:
                        pe.wait_ge(s_p_lo, at(EB * (g[0] + 1), EB * g[1], g[2]))
                    for b in range(TB):
                        pe.wait_ge(s_added, at(16 * g[0] + 4 * d + b + 1, 16 * g[1], g[2]))
                        for k in range(EB):
                            for term in range(3):
                                x = (p_lo if term == 2 else p_hi)[:, g[0] % 2, k, b * P:(b + 1) * P]
                                w = (core.w_lo if term == 1 else core.w_hi)[:, n % 2, k * COLS:(k + 1) * COLS]
                                mm = pe.matmul(bank[:, 4 + b, :], x, w, start=(k == 0 and term == 0),
                                               stop=(k == EB - 1 and term == 2))
                        mm.then_inc(core.s_used if b == TB - 1 else s_out, 1)

            steps(pe, inner, outer)

        @block.scalar
        def _(act):
            def split(n, per, i):
                if per or n + 2 < E0 + 2 * KEYS:
                    core.split_hi(act, n + 2, per, i)

            def inner(g):
                for c in range(EB):
                    n, per, i = u_unit(g, c)
                    cnt = lambda k: at(EB * g[0] + c + k, EB * g[1], g[2])
                    act.wait_ge(core.s_used, at(n + 1, per, i))
                    if c >= 2 or g[0]:
                        act.wait_ge(s_weighted, cnt(-1))
                    act.activation(gelu[:, c % 2, :], bank[:, c % 2, :], ACT.Gelu).then_inc(s_gelu, 1)
                    split(n, per, i)
                    act.wait_ge(s_weighted, cnt(1))
                    act.activation(p_hi[:, g[0] % 2, c, :], weighted[:, c % 2, :], ACT.Copy).then_inc(s_p_hi, 1)

            def outer(g):
                for d in range(DB):
                    split(*v_unit(g, d))

            steps(act, inner, outer)

        @block.gpsimd
        def _(pool):
            def inner(g):
                for c in range(EB):
                    cnt = lambda k: at(EB * g[0] + c + k, EB * g[1], g[2])
                    if c == 0:
                        pool.wait_ge(s_gates[g[0] % 2], at(16 * (g[0] // 2 + 1), 8 * g[1], g[2]))
                    pool.wait_ge(s_gelu, cnt(1))
                    if c >= 2 or g[0]:
                        pool.wait_ge(s_p_lo, cnt(-1))
                    pool.tensor_tensor(weighted[:, c % 2, :].rearrange("p (g t) -> p g t", g=NTG),
                                       gelu[:, c % 2, :].rearrange("p (g t) -> p g t", g=NTG),
                                       gates[:, g[0] % 2, :, c, :], ALU.mult).then_inc(s_weighted, 1)

            steps(pool, inner, lambda g: None)

        @block.vector
        def _(dve):
            dve.sem_inc(s_added, TB)
            dve.wait_ge(s_acc, 16)
            dve.tensor_scalar(acc[:, :, :], acc[:, :, :], ALPHA, None, ALU.mult).then_inc(s_scaled, 1)
            dve.wait_ge(s_scaled, 1)

            def split(n, per, i):
                if per or n + 2 < E0 + 2 * KEYS:
                    core.split_lo(dve, n + 2, per, i)

            def inner(g):
                for c in range(EB):
                    split(*u_unit(g, c))
                    dve.wait_ge(s_p_hi, at(EB * g[0] + c + 1, EB * g[1], g[2]))
                    dve.tensor_tensor(p_lo[:, g[0] % 2, c, :], weighted[:, c % 2, :], p_hi[:, g[0] % 2, c, :].bitcast(F32),
                                      ALU.subtract).then_inc(s_p_lo, 1)

            def outer(g):
                for d in range(DB):
                    n, per, i = v_unit(g, d)
                    for b in range(TB):
                        if b < TB - 1:
                            dve.wait_ge(s_out, at(12 * g[0] + 3 * d + b + 1, 12 * g[1], g[2]))
                        else:
                            dve.wait_ge(core.s_used, at(n + 1, per, i))
                        a = acc[:, b, d * COLS:(d + 1) * COLS]
                        dve.tensor_tensor(a, a, bank[:, 4 + b, :], ALU.add).then_inc(s_added, 1)
                    split(n, per, i)

            steps(dve, inner, outer)


def finish(core, dram, acc):
    nc = core.nc
    with phase(nc) as ctx:
        ln_w = ctx.enter_context(nc.sbuf_tensor("ln2_w", [P, D], F32))
        ln_b = ctx.enter_context(nc.sbuf_tensor("ln2_b", [P, D], F32))
        ln = LayerNorm(core, ctx, "ln2")
        s_params, s_chain, s_normed, s_out = (phase_semaphore(nc, ctx, "finish_" + n) for n in (
            "params_loaded", "dve_chain", "out_normed", "out_written"))
        block = ctx.enter_context(nc.Block())

        @block.sync
        def _(sp):
            sp.dma_start(ln_w[:, :], dram["ln2_w"].partition_broadcast(P)).then_inc(s_params, 16)
            sp.dma_start(ln_b[:, :], dram["ln2_b"].partition_broadcast(P)).then_inc(s_params, 16)
            for n in range(TB):
                sp.wait_ge(s_normed, n + 1)
                sp.dma_start(dram["out"][n * P:(n + 1) * P, :], acc[:, n, :]).then_inc(s_out, 16)
            sp.wait_ge(s_out, 16 * TB)

        @block.vector
        def _(dve):
            chain = Chain(dve, s_chain, 0)
            dve.wait_ge(s_params, 32)
            for n in range(TB):
                ln.on_vector(dve, chain, n, acc[:, n, :], acc[:, n, :], ln_w[:, :], ln_b[:, :], s_normed)

        @block.gpsimd
        def _(pool):
            for n in range(TB):
                ln.on_gpsimd(pool, n)


_OUT = (1, T, D)


def build(nc, dram, stop=99):
    with ExitStack() as ctx:
        core = Core(nc, ctx)
        constants(core)
        with ExitStack() as mem_ctx:
            mem_hi = mem_ctx.enter_context(nc.sbuf_tensor("mem_hi", [P, KD, M], F32R))
            mem_lo = mem_ctx.enter_context(nc.sbuf_tensor("mem_lo", [P, KD, M], F32R))
            embed(core, mem_hi, mem_lo, dram)
            if stop >= 2:
                attention(core, mem_hi, mem_lo, dram)
        if stop >= 3:
            delta_net(core, dram)
        if stop >= 4:
            mix_out(core, dram)
        if stop >= 5:
            with nc.sbuf_tensor("chosen", [P, 3, TB, PH * TOPK], F32) as chosen:
                route(core, dram, chosen)
                spread(core, dram, chosen)
        if stop >= 6:
            with nc.sbuf_tensor("acc", [P, TB, D], F32) as acc:
                experts(core, dram, acc)
                finish(core, dram, acc)


def kernel(**inputs):
    import concourse.bacc as bacc
    from concourse.bass_utils import run_bass_kernel_spmd

    a = {k: np.asarray(v) for k, v in inputs.items()}

    def by_column_block(w):
        n = w.shape[1] // P
        return w.reshape(KD, P, n, P).transpose(2, 1, 0, 3).reshape(n, P, UNIT)

    def by_row_block(w):
        m, n = w.shape[0] // (KQ * P), w.shape[1] // COLS
        return w.reshape(m, KQ, P, n, COLS).transpose(0, 3, 2, 1, 4).reshape(m, n, P, UNIT)

    w_in = a["w_in"][0]
    gw, sw = GH * P, SH * P
    units = by_column_block(np.concatenate([w_in[:, :4 * gw], w_in[:, 4 * gw + 2 * GH:]], axis=1))
    q, k, v, z = (units[n * GH:(n + 1) * GH] for n in range(4))
    sq, sk, sv, mq = (units[4 * GH + n * SH:4 * GH + (n + 1) * SH] for n in range(4))
    kv = by_column_block(a["w_mem_kv"][0])
    conv = a["conv_w"][0].reshape(TAPS, 3, GH, P)
    arrays = {
        "x": a["x"][0], "mem": a["mem"][0],
        "w_att": np.stack([mq, sq, sk, sv], axis=1).reshape(4 * SH, P, UNIT),
        "w_gdn": np.stack([q, k, v, z], axis=1).reshape(4 * GH, P, UNIT),
        "w_mem_kv": np.stack([kv[:MH], kv[MH:]], axis=1).reshape(2 * MH, P, UNIT),
        "w_gates": w_in[:, 4 * gw:4 * gw + 2 * GH].reshape(KD, P, 2 * GH).transpose(1, 0, 2),
        "conv_w": conv.transpose(3, 2, 1, 0).reshape(P, GH * 3 * TAPS),
        "a_log": a["a_log"], "dt_bias": a["dt_bias"],
        "gdn_norm_w": a["gdn_norm_w"].T,
        "att_norm_w": np.stack([a["mem_norm_w"][0].reshape(MH, P), a["sb_norm_w"][0].reshape(SH, P)],
                               axis=1).reshape(MH + SH, P).T,
        "w_out": by_row_block(a["w_out"][0]),
        "peer_wq": by_column_block(a["peer_wq"][0]),
        "peer_keys": np.concatenate([a["peer_keys1"][0].T, a["peer_keys2"][0].T], axis=1),
        "peer_u": a["peer_u"][0].reshape(KEYS, P, KD, P).transpose(0, 3, 2, 1).reshape(KEYS, P, UNIT),
        "peer_v": by_row_block(a["peer_v"][0]),
    }
    for name in ("ln_emb", "ln_mem", "ln1", "ln2"):
        for part in ("_w", "_b"):
            arrays[name + part] = a[name + part].reshape(D)
    arrays = {k: np.ascontiguousarray(v) for k, v in arrays.items()}

    nc = bacc.Bacc("TRN2", target_bir_lowering=False, num_devices=1)
    dram = {k: nc.dram_tensor("in_" + k, v.shape, F32, kind="ExternalInput").ap() for k, v in arrays.items()}
    for name, shape in (("h_kept", (T, D)), ("h1_kept", (T, D)), ("o_kept", (HEADS, P, T)),
                        ("gates_kept", (NTG, P, KEYS, TG))):
        dram[name] = nc.dram_tensor(name, shape, F32).ap()
    dram["out"] = nc.dram_tensor("out", (T, D), F32, kind="ExternalOutput").ap()
    build(nc, dram)
    r = run_bass_kernel_spmd(nc, [{"in_" + k: v for k, v in arrays.items()}], core_ids=[0])
    return np.asarray(r.results[0]["out"]).reshape(_OUT)
```

```python
from contextlib import ExitStack, contextmanager

import numpy as np

import concourse.bass as bass
from concourse import mybir

F32 = mybir.dt.float32
F32R = mybir.dt.float32r
U32 = mybir.dt.uint32
ALU = mybir.AluOpType
ACT = mybir.ActivationFunctionType
AX_X = mybir.AxisListType.X

P = 128
T = 512
TB = T // P
D = 2048
KD = D // P
M = 256
MB = M // P
GH, SH, MH = 8, 4, 4
HEADS = GH + SH + MH
TAPS = 4
LEVELS = 7
PH, KEYS, TOPK = 8, 128, 16
EB = 4
GROUPS = KEYS // EB
AHEAD = 5
TG = 32
NTG = T // TG
UNIT = 2048
COLS = 512
DB = D // COLS
KQ = UNIT // COLS
LN_EPS, RMS_EPS = 1e-5, 1e-6
ALPHA = 2.0 ** 0.25
SCALE = float(P) ** -0.5
NEG = -3.0e38
G_LOG, G_RUN, G_BETA_HALF, G_NEG_BETA, G_BETA_EXP, G_TO_END, G_TOTAL = range(7)
G_KINDS = 7
FILL_FIRST, FILL_LEVEL, FILL_CHUNK, FILL_LAST = 8, 10, 8, 12
UNITS_ATT = 6 * SH
UNITS_GDN = 4 * GH
UNITS_OUT = DB * (HEADS // KQ)
UNITS_Q = 2 * PH


def at(const, per=0, i=None):
    return const if i is None else i * per + const


def over_blocks(tile):
    return tile.unsqueeze(1).to_broadcast([P, TB, P])


def over_columns(col):
    return col.unsqueeze(2).to_broadcast([P, TB, P])


def blocks(tile):
    return tile.rearrange("p (b n) -> p b n", b=TB)


class Chain:

    def __init__(self, eng, sem, base, per=0, i=None, apart=None):
        self.apart = apart
        self.eng, self.sem, self.base, self.per, self.i, self.n = eng, sem, base, per, i, 0

    def mark(self, ins):
        self.n += 1
        ins.then_inc(self.sem, 1)

    def wait(self):
        self.eng.wait_ge(self.sem, at(self.base + self.n, self.per, self.i))

    def wait_apart(self):
        self.wait()
        self.eng.sem_inc(self.apart, 1)

    def link(self, ins):
        self.mark(ins)
        self.wait()


@contextmanager
def phase(nc):
    with ExitStack() as ctx:
        ctx.semaphores = []
        yield ctx
    nc.clear_and_free_semaphores(ctx.semaphores)
    nc.all_engine_barrier()


def phase_semaphore(nc, ctx, name):
    ctx.semaphores.append(nc.alloc_semaphore(name))
    return ctx.semaphores[-1]


class Core:

    def __init__(self, nc, ctx):
        self.nc = nc

        def sb(name, shape, dt=F32):
            return ctx.enter_context(nc.sbuf_tensor(name, shape, dt))

        def sem(name):
            return ctx.enter_context(nc.semaphore(name))

        self.s_free = {name: sem(name) for name in (
            "att_ot_free", "gdn_ot_free", "gdn_bank_free", "mix_added", "route_scores_read", "spread_mm", "spread_copied", "spread_out_free",
            "spread_products", "spread_products_free", "expert_added")}
        self.ident = sb("ident", [P, P])
        self.ones = sb("ones", [P, P])
        self.tri_le = sb("tri_le", [P, P])
        self.tri_ge = sb("tri_ge", [P, P])
        self.iota = sb("iota", [P, P])
        self.half_neg = sb("half_neg", [P, 2 * TB])
        self.rms_eps = sb("rms_eps", [P, 1])
        self.act_hi = sb("act_hi", [P, KD, T], F32R)
        self.act_lo = sb("act_lo", [P, KD, T], F32R)
        self.w_raw = sb("w_raw", [P, 2, UNIT])
        self.w_hi = sb("w_hi", [P, 2, UNIT], F32R)
        self.w_lo = sb("w_lo", [P, 2, UNIT], F32R)
        self.bank = ctx.enter_context(nc.psum_tensor("bank", [P, 8, 512], F32))
        self.s_loaded = [sem("w_loaded_even"), sem("w_loaded_odd")]
        self.s_hi = sem("w_hi_done")
        self.s_lo = sem("w_lo_done")
        self.s_used = sem("w_unit_used")

    def load_unit(self, sp, src, c, per=0, i=None):
        if c >= 2:
            sp.wait_ge(self.s_lo, at(c - 1, per, i))
        sp.dma_start(self.w_raw[:, c % 2, :], src).then_inc(self.s_loaded[c % 2], 16)

    def split_hi(self, act, c, per=0, i=None):
        act.wait_ge(self.s_loaded[c % 2], at(16 * (c // 2 + 1), 8 * per, i))
        if c >= 2:
            act.wait_ge(self.s_used, at(c - 1, per, i))
        act.activation(self.w_hi[:, c % 2, :], self.w_raw[:, c % 2, :], ACT.Copy).then_inc(self.s_hi, 1)

    def split_lo(self, eng, c, per=0, i=None):
        eng.wait_ge(self.s_hi, at(c + 1, per, i))
        eng.tensor_tensor(self.w_lo[:, c % 2, :], self.w_raw[:, c % 2, :],
                          self.w_hi[:, c % 2, :].bitcast(F32), ALU.subtract).then_inc(self.s_lo, 1)

    def by_feature(self, pe, out, c, per=0, i=None, part=(0, 48), hi=None, lo=None):
        hi = self.act_hi if hi is None else hi
        lo = self.act_lo if lo is None else lo
        slot = c % 2
        for m in range(*part):
            k, term = divmod(m, 3)
            if m == 0:
                pe.wait_ge(self.s_lo, at(c + 1, per, i))
            w = (self.w_lo if term == 2 else self.w_hi)[:, slot, k * P:(k + 1) * P]
            x = (lo if term == 1 else hi)[:, k, :]
            mm = pe.matmul(out, w, x, start=(m == 0), stop=(m == 3 * KD - 1))
            if m == 3 * KD - 1:
                mm.then_inc(self.s_used, 1)

    def by_token(self, pe, outs, hi, lo, first, last, c, per=0, i=None):
        slot = c % 2
        pe.wait_ge(self.s_lo, at(c + 1, per, i))
        for b in range(TB):
            for k in range(KQ):
                for term in range(3):
                    x = (lo if term == 2 else hi)[:, k, b * P:(b + 1) * P]
                    w = (self.w_lo if term == 1 else self.w_hi)[:, slot, k * COLS:(k + 1) * COLS]
                    mm = pe.matmul(outs[b], x, w, start=(first and k == 0 and term == 0),
                                   stop=(last and k == KQ - 1 and term == 2))
        mm.then_inc(self.s_used, 1)


def constants(core):
    nc = core.nc
    with phase(nc) as ctx:
        filled, cut = (phase_semaphore(nc, ctx, n) for n in ("const_filled", "const_cut"))
        block = ctx.enter_context(nc.Block())

        @block.gpsimd
        def _(pool):
            pool.memset(core.ident[:, :], 0.0).then_inc(filled, 1)
            for tile in (core.ones, core.tri_le, core.tri_ge):
                pool.memset(tile[:, :], 1.0).then_inc(filled, 1)
            pool.memset(core.half_neg[:, :], -0.5).then_inc(filled, 1)
            pool.memset(core.rms_eps[:, :], RMS_EPS).then_inc(filled, 1)
            pool.wait_ge(filled, 6)
            pool.affine_select(out=core.ident[:, :], in_=core.ident[:, :], compare_op=ALU.not_equal, fill=1.0,
                               base=0, pattern=[[-1, P]], channel_multiplier=1).then_inc(cut, 1)
            pool.affine_select(out=core.tri_le[:, :], in_=core.tri_le[:, :], compare_op=ALU.is_ge, fill=0.0,
                               base=0, pattern=[[1, P]], channel_multiplier=-1).then_inc(cut, 1)
            pool.affine_select(out=core.tri_ge[:, :], in_=core.tri_ge[:, :], compare_op=ALU.is_ge, fill=0.0,
                               base=0, pattern=[[-1, P]], channel_multiplier=1).then_inc(cut, 1)
            pool.iota(core.iota[:, :], pattern=[[1, P]], base=0, channel_multiplier=0,
                      allow_small_or_imprecise_dtypes=True).then_inc(cut, 1)


class LayerNorm:

    def __init__(self, core, ctx, name, slots):
        nc = core.nc
        f = lambda n, shape: ctx.enter_context(nc.sbuf_tensor(name + n, [P, slots] + shape, F32))
        self.core, self.name, self.slots = core, name, slots
        self.stats, self.mean_var = f("_stats", [4, 6]), f("_mean_var", [2])
        self.var, self.rstd, self.shift = f("_var_eps", [1]), f("_rstd", [1]), f("_shift", [1])

    def open(self, ctx):
        self.s_var, self.s_rstd, self.s_shift, self.s_scaled, self.s_weighed = (
            phase_semaphore(self.core.nc, ctx, self.name + n)
            for n in ("_var_ready", "_rstd_ready", "_shift_ready", "_rows_scaled", "_rows_weighed"))
        return self

    def statistics(self, dve, chain, n, x):
        for q in range(4):
            chain.mark(dve.bn_stats(self.stats[:, n % self.slots, q, :], x[:, q * 512:(q + 1) * 512]))
        chain.wait()

    def variance(self, dve, chain, n):
        m = n % self.slots
        chain.link(dve.bn_aggr(self.mean_var[:, m, :], self.stats[:, m, :, :]))
        dve.tensor_scalar(self.var[:, m, :], self.mean_var[:, m, 1:2], LN_EPS, None, ALU.add).then_inc(self.s_var, 1)

    def power(self, pool, n):
        m = n % self.slots
        pool.wait_ge(self.s_var, n + 1)
        pool.tensor_tensor(self.rstd[:, m, :], self.var[:, m, :], self.core.half_neg[:, 0:1], ALU.pow).then_inc(self.s_rstd, 1)

    def shift_of(self, dve, n):
        m = n % self.slots
        dve.wait_ge(self.s_rstd, n + 1)
        dve.scalar_tensor_tensor(out=self.shift[:, m, :], in0=self.mean_var[:, m, 0:1], scalar=-1.0, in1=self.rstd[:, m, :],
                                 op0=ALU.mult, op1=ALU.mult).then_inc(self.s_shift, 1)

    def scale(self, act, n, x):
        m = n % self.slots
        act.wait_ge(self.s_shift, n + 1)
        act.activation(x, x, ACT.Identity, scale=self.rstd[:, m, :], bias=self.shift[:, m, :]).then_inc(self.s_scaled, 1)

    def weigh(self, dve, n, x, weight):
        dve.wait_ge(self.s_scaled, n + 1)
        dve.tensor_tensor(x, x, weight, ALU.mult).then_inc(self.s_weighed, 1)

    def add_bias(self, eng, n, x, bias, signal):
        eng.wait_ge(self.s_weighed, n + 1)
        eng.tensor_tensor(x, x, bias, ALU.add).then_inc(signal, 1)


def embed(core, mem_hi, mem_lo, dram):
    nc = core.nc
    tiles = [("x", b) for b in range(TB)] + [("m", b) for b in range(MB)]
    with phase(nc) as ctx:
        def sb(name, shape, dt=F32):
            return ctx.enter_context(nc.sbuf_tensor(name, shape, dt))

        def sem(name):
            return phase_semaphore(nc, ctx, "embed_" + name)

        R = 3
        rows = sb("rows", [P, R, D])
        params = {n: sb(n, [P, D]) for n in ("ln_emb_w", "ln_emb_b", "ln_mem_w", "ln_mem_b")}
        ln = LayerNorm(core, ctx, "ln0", 2).open(ctx)
        s_params, s_chain = {"x": sem("x_params_loaded"), "m": sem("mem_params_loaded")}, sem("dve_chain")
        s_row = [sem(f"rows_loaded{r}") for r in range(R)]
        s_normed, s_turned = [sem("rows_normed_even"), sem("rows_normed_odd")], sem("rows_turned")
        s_t_hi, s_t_lo = sem("turned_hi"), sem("turned_lo")
        s_kept = [sem(f"h_kept{r}") for r in range(R)]
        block = ctx.enter_context(nc.Block())

        @block.sync
        def _(sp):
            def load_rows(n):
                kind, b = tiles[n]
                sp.dma_start(rows[:, n % R, :], dram["x" if kind == "x" else "mem"][b * P:(b + 1) * P, :]).then_inc(s_row[n % R], 16)

            def load_params(kind, name):
                for part in ("_w", "_b"):
                    sp.dma_start(params[name + part][:, :], dram[name + part].partition_broadcast(P)).then_inc(s_params[kind], 16)

            load_rows(0)
            load_rows(1)
            load_params("x", "ln_emb")
            load_rows(2)
            load_params("m", "ln_mem")
            for n in range(len(tiles)):
                if n < TB:
                    sp.wait_ge(s_normed[n % 2], n // 2 + 1)
                    sp.dma_start(dram["h_kept"][n * P:(n + 1) * P, :], rows[:, n % R, :]).then_inc(s_kept[n % R], 16)
                if n + R < len(tiles):
                    sp.wait_ge(s_turned, 4 * (n + 1))
                    if n < TB:
                        sp.wait_ge(s_kept[n % R], 16 * (n // R + 1))
                    load_rows(n + R)
                if n < 2:
                    core.load_unit(sp, dram["w_att"][n + 1], n)
            for r, kept in enumerate(s_kept):
                sp.wait_ge(kept, 16 * len(range(r, TB, R)))

        def bias_of(n):
            return params["ln_emb_b" if n < TB else "ln_mem_b"][:, :]

        @block.gpsimd
        def _(pool):
            ln.power(pool, 0)
            for n in range(len(tiles)):
                if n + 1 < len(tiles) and n != TB - 1:
                    ln.power(pool, n + 1)
                if n % 2 == 0:
                    ln.add_bias(pool, n, rows[:, n % R, :], bias_of(n), s_normed[0])
                if n == TB - 1:
                    ln.power(pool, n + 1)

        @block.tensor
        def _(pe):
            for n in range(len(tiles)):
                if n == TB:
                    pe.wait_ge(s_t_lo, 4 * TB)
                    core.by_feature(pe, core.bank[:, 4, :], 0)
                pe.wait_ge(s_normed[n % 2], n // 2 + 1)
                for q in range(4):
                    u = 4 * n + q
                    if u >= 4:
                        pe.wait_ge(s_t_lo, u - 3)
                    for j in range(4):
                        k = 4 * q + j
                        mm = pe.transpose(core.bank[:, u % 4, j * P:(j + 1) * P],
                                          rows[:, n % R, k * P:(k + 1) * P], core.ident[:, :])
                    mm.then_inc(s_turned, 1)

        def slots(n, q):
            kind, b = tiles[n]
            hi, lo = (core.act_hi, core.act_lo) if kind == "x" else (mem_hi, mem_lo)
            return [a[:, 4 * q:4 * q + 4, b * P:(b + 1) * P] for a in (hi, lo)]

        @block.scalar
        def _(act):
            ln.scale(act, 0, rows[:, 0, :])
            for n in range(len(tiles)):
                if n + 1 < len(tiles) and n != TB - 1:
                    ln.scale(act, n + 1, rows[:, (n + 1) % R, :])
                for q in range(4):
                    u = 4 * n + q
                    act.wait_ge(s_turned, u + 1)
                    act.activation(slots(n, q)[0], blocks(core.bank[:, u % 4, :]), ACT.Copy).then_inc(s_t_hi, 1)
                if n == TB - 1:
                    ln.scale(act, n + 1, rows[:, (n + 1) % R, :])
                if n in (1, 2):
                    core.split_hi(act, n - 1)

        @block.vector
        def _(dve):
            chain = Chain(dve, s_chain, 0)

            def statistics(n):
                dve.wait_ge(s_row[n % R], 16 * (n // R + 1))
                ln.statistics(dve, chain, n, rows[:, n % R, :])
                ln.variance(dve, chain, n)

            def low_parts(n):
                for q in range(4):
                    u = 4 * n + q
                    dve.wait_ge(s_t_hi, u + 1)
                    hi, lo = slots(n, q)
                    dve.tensor_tensor(lo, blocks(core.bank[:, u % 4, :]), hi.bitcast(F32), ALU.subtract).then_inc(s_t_lo, 1)

            statistics(0)
            ln.shift_of(dve, 0)
            for n in range(len(tiles)):
                last_x = n == TB - 1
                if n + 1 < len(tiles) and not last_x:
                    statistics(n + 1)
                if n in (0, TB):
                    dve.wait_ge(s_params["x" if n < TB else "m"], 32)
                ln.weigh(dve, n, rows[:, n % R, :], params["ln_emb_w" if n < TB else "ln_mem_w"][:, :])
                if n + 1 < len(tiles) and not last_x:
                    ln.shift_of(dve, n + 1)
                if n % 2:
                    ln.add_bias(dve, n, rows[:, n % R, :], bias_of(n), s_normed[1])
                if n not in (0, TB):
                    low_parts(n - 1)
                if n == 2:
                    core.split_lo(dve, 0)
                if last_x:
                    low_parts(n)
                    statistics(n + 1)
                    ln.shift_of(dve, n + 1)
            low_parts(len(tiles) - 1)
            core.split_lo(dve, 1)


class RmsTail:

    def __init__(self, core, ctx, name, sq):
        nc = core.nc
        self.core, self.sq = core, sq
        f = lambda n, s: ctx.enter_context(nc.sbuf_tensor(name + n, s, F32))
        sem = lambda n: phase_semaphore(nc, ctx, name + n)
        self.o, self.on, self.ot = (f(x, [P, TB, P]) for x in ("_o", "_on", "_ot"))
        self.ms, self.rstd = f("_ms", [P, TB]), f("_rstd", [P, TB])
        self.s_ms, self.s_rstd, self.s_on = sem("_ms_ready"), sem("_rstd_ready"), sem("_normed")
        self.s_turned, self.s_ot, self.s_kept = sem("_turned"), sem("_ot_ready"), sem("_kept")

    def norm_on_vector(self, dve, chain, count):
        chain.link(dve.tensor_tensor(self.sq[:, :, :], self.o[:, :, :], self.o[:, :, :], ALU.mult))
        chain.link(dve.tensor_reduce(self.ms[:, :], self.sq[:, :, :], AX_X, ALU.add))
        dve.tensor_scalar(self.ms[:, :], self.ms[:, :], 1.0 / P, RMS_EPS, ALU.mult, ALU.add).then_inc(self.s_ms, 1)
        dve.wait_ge(self.s_rstd, count)
        dve.tensor_tensor(self.on[:, :, :], self.o[:, :, :], over_columns(self.rstd[:, :]), ALU.mult).then_inc(self.s_on, 1)

    def on_gpsimd(self, pool, n):
        pool.wait_ge(self.s_ms, n + 1)
        pool.tensor_tensor(self.rstd[:, :], self.ms[:, :], self.core.half_neg[:, 0:TB], ALU.pow).then_inc(self.s_rstd, 1)

    def turn(self, pe, n, bank):
        pe.wait_ge(self.s_on, n + 1)
        for b in range(TB):
            mm = pe.transpose(bank[:, b * P:(b + 1) * P], self.on[:, b, :], self.core.ident[:, :])
        mm.then_inc(self.s_turned, 1)

    def keep(self, pool, n, dst):
        pool.wait_ge(self.s_ot, n + 1)
        pool.dma_start(dst, self.ot[:, :, :].rearrange("p b n -> p (b n)")).then_inc(self.s_kept, 16)


def attention(core, mem_hi, mem_lo, dram):
    nc = core.nc
    bank = core.bank
    with phase(nc) as ctx:
        def sb(name, shape, dt=F32):
            return ctx.enter_context(nc.sbuf_tensor(name, shape, dt))

        def sem(name):
            return phase_semaphore(nc, ctx, "attention_" + name)

        mk, mv, mvt = sb("mk", [P, M]), sb("mv", [P, M]), sb("mvt", [P, MB, P])
        mq, sq, sk, sv = (sb(x, [P, T]) for x in ("mq", "sq", "sk", "sv"))
        svt = sb("svt", [P, TB, P])
        neg_max, row_sum, inv_sum = (sb(x, [P, TB]) for x in ("neg_max", "row_sum", "inv_sum"))
        prob, prob_t = sb("prob", [P, TB, M]), sb("prob_t", [P, MB, T])
        z, soft, absz = sb("z", [P, TB, T]), sb("soft", [P, TB, T]), sb("absz", [P, 2, T])
        before, not_before = sb("before", [P, P]), sb("not_before", [P, P])
        norm_w = sb("norm_w", [P, MH + SH])
        norm_now = sb("norm_now", [P, 2])
        sq_tail = sb("sq_tail", [P, TB, P])
        mt, st = RmsTail(core, ctx, "mem", sq_tail), RmsTail(core, ctx, "stick", sq_tail)
        s_chain, s_const, s_ot_free = sem("dve_chain"), sem("masks_made"), core.s_free["att_ot_free"]
        s_params = sem("params_loaded")
        s_proj = [sem(f"{x}_copied") for x in ("sq", "sk", "mk", "mv", "mq", "sv")]
        s_mvt, s_mvt_sb, s_svt, s_svt_sb = sem("mv_turned"), sem("mvt_copied"), sem("sv_turned"), sem("svt_copied")
        s_scores, s_max, s_prob = sem("mem_scores"), sem("mem_max"), sem("mem_prob")
        s_probt, s_probt_sb, s_mo = sem("prob_turned"), sem("prob_t_copied"), sem("mem_o")
        s_z, s_z_sb, s_abs, s_exp, s_ln = sem("z_ready"), sem("z_copied"), sem("abs_z"), sem("exp_abs"), sem("ln_one_plus")
        s_soft, s_masked = sem("softplus"), sem("softplus_masked")
        s_after, s_arg, s_att, s_amasked, s_so = sem("suffix_sums"), sem("log_weight"), sem("att_exp"), sem("att_masked"), sem("stick_o")
        block = ctx.enter_context(nc.Block())
        UT = 6

        @block.sync
        def _(sp):
            sp.dma_start(norm_w[:, :], dram["att_norm_w"]).then_inc(s_params, 16)

            def unit(s, u):
                if u in (2, 3):
                    return dram["w_mem_kv"][s * 2 + u - 2]
                return dram["w_att"][s * 4 + {0: 1, 1: 2, 4: 0, 5: 3}[u]]

            core.load_unit(sp, unit(0, 2), 2)
            with sp.Fori(0, SH - 1) as s:
                for n in range(3, UT + 3):
                    core.load_unit(sp, unit(s, n) if n < UT else unit(s + 1, n - UT), n, UT, s)
            for n in range(3, UT + 2):
                core.load_unit(sp, unit(SH - 1, n) if n < UT else dram["w_gdn"][n - UT], UT * (SH - 1) + n)

        SQ, SK, MK, MV, MQ, SV = range(UT)

        @block.tensor
        def _(pe):
            def turn(i, base, more):
                s1 = lambda m, k: at(m * base + k, m, i)

                def project(u, out, part=(0, 48)):
                    hl = dict(hi=mem_hi, lo=mem_lo) if u in (MK, MV) else {}
                    core.by_feature(pe, out, UT * base + u, UT, i, part, **hl)

                def next_sq(part):
                    if more:
                        project(UT, bank[:, 0, :], part)

                project(SK, bank[:, 1, :])
                pe.wait_ge(s_proj[SQ], s1(1, 1))
                pe.wait_ge(s_proj[SK], s1(1, 1))
                for j in range(TB):
                    w = j * P
                    pe.matmul(bank[:, 4 + j, w:T], sk[:, w:w + P], sq[:, w:T], start=True, stop=True).then_inc(s_z, 1)
                project(MK, bank[:, 0, 0:M])
                project(MV, bank[:, 1, 0:M])
                pe.wait_ge(s_proj[MK], s1(1, 1))
                project(MQ, bank[:, 0, :], (0, 12))
                pe.wait_ge(s_proj[MV], s1(1, 1))
                pe.wait_ge(s_ot_free, s1(1, 1))
                for j in range(MB):
                    mm = pe.transpose(bank[:, 2, j * P:(j + 1) * P], mv[:, j * P:(j + 1) * P], core.ident[:, :])
                mm.then_inc(s_mvt, 1)
                project(MQ, bank[:, 0, :], (12, 30))
                pe.wait_ge(s_masked, s1(4, 4))
                for j in range(TB):
                    for jj in range(j, TB):
                        mm = pe.matmul(bank[:, 4 + j, jj * P:T], (core.tri_ge if jj == j else core.ones)[:, :],
                                       soft[:, jj, jj * P:T], start=(jj == j), stop=(jj == TB - 1))
                    mm.then_inc(s_after, 1)
                project(MQ, bank[:, 0, :], (30, 48))
                project(SV, bank[:, 1, :], (0, 12))
                pe.wait_ge(s_proj[MQ], s1(1, 1))
                pe.wait_ge(s_mvt_sb, s1(1, 1))
                for b in range(TB):
                    mm = pe.matmul(bank[:, 2 + b // 2, (b % 2) * M:(b % 2 + 1) * M], mq[:, b * P:(b + 1) * P],
                                   mk[:, :], start=True, stop=True)
                mm.then_inc(s_scores, 1)
                project(SV, bank[:, 1, :], (12, 48))
                next_sq((0, 8))
                pe.wait_ge(s_prob, s1(4, 4))
                pe.wait_ge(s_arg, s1(4, 4))
                for j in range(MB):
                    for b in range(TB):
                        mm = pe.transpose(bank[:, 4 + j, b * P:(b + 1) * P], prob[:, b, j * P:(j + 1) * P], core.ident[:, :])
                mm.then_inc(s_probt, 1)
                pe.wait_ge(s_proj[SV], s1(1, 1))
                for j in range(TB):
                    mm = pe.transpose(bank[:, 6, j * P:(j + 1) * P], sv[:, j * P:(j + 1) * P], core.ident[:, :])
                mm.then_inc(s_svt, 1)
                next_sq((8, 22))
                pe.wait_ge(s_probt_sb, s1(1, 1))
                for b in range(TB):
                    for j in range(MB):
                        mm = pe.matmul(bank[:, 7, b * P:(b + 1) * P], prob_t[:, j, b * P:(b + 1) * P], mvt[:, j, :],
                                       start=(j == 0), stop=(j == MB - 1))
                mm.then_inc(s_mo, 1)
                pe.wait_ge(s_att, s1(4, 4))
                pe.wait_ge(s_svt_sb, s1(1, 1))
                for b in range(TB):
                    for j in range(b + 1):
                        mm = pe.matmul(bank[:, 2, b * P:(b + 1) * P], z[:, j, b * P:(b + 1) * P], svt[:, j, :],
                                       start=(j == 0), stop=(j == b))
                mm.then_inc(s_so, 1)
                next_sq((22, 48))
                mt.turn(pe, s1(1, 0), bank[:, 3, :])
                st.turn(pe, s1(1, 0), bank[:, 2, :])

            with pe.Fori(0, SH - 1) as i:
                turn(i, 0, True)
            turn(None, SH - 1, False)

        @block.scalar
        def _(act):
            act.preload_act_table_set("natural_log_exp_and_others")

            def turn(i, base, more):
                s1 = lambda m, k: at(m * base + k, m, i)

                def copied(u, dst, src, scale=1.0):
                    act.wait_ge(core.s_used, s1(UT, u + 1))
                    act.activation(dst, src, ACT.Copy, scale=scale).then_inc(s_proj[u % UT], 1)
                    core.split_hi(act, UT * base + u + 2, UT, i)

                def softplus(j):
                    w = slice(j * P, T)
                    act.wait_ge(s_z, s1(4, j + 1))
                    act.activation(z[:, j, w], bank[:, 4 + j, w], ACT.Copy).then_inc(s_z_sb, 1)
                    act.wait_ge(s_abs, s1(4, j + 1))
                    act.activation(absz[:, j % 2, w], absz[:, j % 2, w], ACT.Exp, scale=-1.0).then_inc(s_exp, 1)
                    act.wait_ge(s_exp, s1(4, j + 1))
                    act.activation(absz[:, j % 2, w], absz[:, j % 2, w], ACT.Ln, bias=1.0).then_inc(s_ln, 1)

                copied(SK, sk[:, :], bank[:, 1, :])
                softplus(0)
                softplus(1)
                copied(MK, mk[:, :], bank[:, 0, 0:M])
                softplus(2)
                softplus(3)
                copied(MV, mv[:, :], bank[:, 1, 0:M])
                act.wait_ge(s_mvt, s1(1, 1))
                act.activation(mvt[:, :, :], bank[:, 2, 0:M].rearrange("p (b n) -> p b n", b=MB), ACT.Copy).then_inc(s_mvt_sb, 1)
                copied(MQ, mq[:, :], bank[:, 0, :], SCALE)
                for j in range(TB):
                    act.wait_ge(s_amasked, s1(4, j + 1))
                    act.activation(z[:, j, j * P:T], z[:, j, j * P:T], ACT.Exp).then_inc(s_att, 1)
                act.wait_ge(s_max, s1(2, 2))
                for b in range(TB):
                    act.activation(prob[:, b, :], bank[:, 2 + b // 2, (b % 2) * M:(b % 2 + 1) * M], ACT.Exp,
                                   bias=neg_max[:, b:b + 1], accum_out=row_sum[:, b:b + 1]).then_inc(s_prob, 1)
                copied(SV, sv[:, :], bank[:, 1, :])
                act.wait_ge(s_probt, s1(1, 1))
                act.activation(prob_t[:, :, :], bank[:, 4:6, :], ACT.Copy).then_inc(s_probt_sb, 1)
                act.wait_ge(s_svt, s1(1, 1))
                act.activation(svt[:, :, :], blocks(bank[:, 6, :]), ACT.Copy).then_inc(s_svt_sb, 1)
                if more:
                    copied(UT, sq[:, :], bank[:, 0, :], SCALE)

            act.activation(sq[:, :], bank[:, 4, :], ACT.Copy, scale=SCALE).then_inc(s_proj[SQ], 1)
            core.split_hi(act, 2)
            with act.Fori(0, SH - 1) as i:
                turn(i, 0, True)
            turn(None, SH - 1, False)

        @block.vector
        def _(dve):
            core.split_lo(dve, 2)
            PER = 8
            dve.wait_ge(s_params, 16)

            def turn(i, base, more):
                chain = Chain(dve, s_chain, PER * base, PER, i)
                s1 = lambda m, k: at(m * base + k, m, i)

                def split(u):
                    core.split_lo(dve, UT * base + u, UT, i)

                def softplus(j):
                    w = slice(j * P, T)
                    dve.wait_ge(s_z_sb, s1(4, j + 1))
                    dve.scalar_tensor_tensor(out=absz[:, j % 2, w], in0=z[:, j, w], scalar=-1.0, in1=z[:, j, w],
                                             op0=ALU.mult, op1=ALU.max).then_inc(s_abs, 1)
                    dve.wait_ge(s_ln, s1(4, j + 1))
                    dve.scalar_tensor_tensor(out=soft[:, j, w], in0=bank[:, 4 + j, w], scalar=0.0, in1=absz[:, j % 2, w],
                                             op0=ALU.max, op1=ALU.add).then_inc(s_soft, 1)

                split(3)
                softplus(0)
                softplus(1)
                split(4)
                softplus(2)
                softplus(3)
                split(5)
                for j in range(TB):
                    w = slice(j * P, T)
                    dve.wait_ge(s_after, s1(4, j + 1))
                    dve.tensor_tensor(z[:, j, w], z[:, j, w], bank[:, 4 + j, w], ALU.subtract).then_inc(s_arg, 1)
                split(6)
                dve.wait_ge(s_scores, s1(1, 1))
                for b in range(2):
                    dve.tensor_reduce(neg_max[:, 2 * b:2 * b + 2], bank[:, 2 + b, :].rearrange("p (b n) -> p b n", b=2),
                                      AX_X, ALU.max, negate=True).then_inc(s_max, 1)
                dve.wait_ge(s_ot_free, s1(1, 1))
                chain.mark(dve.tensor_copy(norm_now[:, :], norm_w[:, bass.ds(at(2 * base, 2, i), 2)]))
                dve.wait_ge(s_prob, s1(4, 4))
                chain.link(dve.reciprocal(inv_sum[:, :], row_sum[:, :]))
                split(7)
                dve.wait_ge(s_mo, s1(1, 1))
                chain.link(dve.tensor_tensor(mt.o[:, :, :], blocks(bank[:, 7, :]), over_columns(inv_sum[:, :]), ALU.mult))
                mt.norm_on_vector(dve, chain, s1(1, 1))
                dve.wait_ge(s_so, s1(1, 1))
                chain.link(dve.tensor_copy(st.o[:, :, :], blocks(bank[:, 2, :])))
                st.norm_on_vector(dve, chain, s1(1, 1))
                if more:
                    split(8)
                dve.wait_ge(mt.s_turned, s1(1, 1))
                dve.tensor_scalar(mt.ot[:, :, :], blocks(bank[:, 3, :]), norm_now[:, 0:1], None, ALU.mult).then_inc(mt.s_ot, 1)
                dve.wait_ge(st.s_turned, s1(1, 1))
                dve.tensor_scalar(st.ot[:, :, :], blocks(bank[:, 2, :]), norm_now[:, 1:2], None, ALU.mult).then_inc(st.s_ot, 1)
                return chain.n

            with dve.Fori(0, SH - 1) as i:
                n = turn(i, 0, True)
            assert n == PER, n
            turn(None, SH - 1, False)

        @block.gpsimd
        def _(pool):
            pool.tensor_tensor(before[:, :], core.tri_le[:, :], core.ident[:, :], ALU.subtract).then_inc(s_const, 1)
            pool.wait_ge(s_const, 1)
            pool.tensor_scalar(not_before[:, :], before[:, :], 1e30, -1e30, ALU.mult, ALU.add).then_inc(s_const, 1)
            pool.wait_ge(s_const, 2)
            pool.sem_inc(s_ot_free, 1)
            with pool.Fori(0, SH) as s:
                for j in range(TB):
                    d = soft[:, j, j * P:(j + 1) * P]
                    pool.wait_ge(s_soft, 4 * s + j + 1)
                    pool.tensor_tensor(d, d, before[:, :], ALU.mult).then_inc(s_masked, 1)
                for j in range(TB):
                    d = z[:, j, j * P:(j + 1) * P]
                    pool.wait_ge(s_arg, 4 * s + j + 1)
                    pool.tensor_tensor(d, d, not_before[:, :], ALU.add).then_inc(s_amasked, 1)
                mt.on_gpsimd(pool, s)
                st.on_gpsimd(pool, s)
                mt.keep(pool, s, dram["o_kept"][s + GH + SH])
                st.keep(pool, s, dram["o_kept"][s + GH])
                pool.wait_ge(mt.s_kept, 16 * s + 16)
                pool.wait_ge(st.s_kept, 16 * s + 16)
                pool.sem_inc(s_ot_free, 1)


def delta_net(core, dram):
    nc = core.nc
    bank = core.bank
    U0, UT = UNITS_ATT, 4
    Q, K, V, Z = range(4)
    PAD = TAPS - 1
    with phase(nc) as ctx:
        def sb(name, shape, dt=F32):
            return ctx.enter_context(nc.sbuf_tensor(name, shape, dt))

        def sem(name):
            return phase_semaphore(nc, ctx, "delta_" + name)

        level_mask = sb("level_mask", [P, LEVELS, P])
        wg, wg_hi, wg_lo = sb("wg", [P, KD, 2 * GH]), sb("wg_hi", [P, KD, 2 * GH], F32R), sb("wg_lo", [P, KD, 2 * GH], F32R)
        ab_t = sb("gates_t", [2 * GH, T])
        dt_bias, a_log = sb("dt_bias", [P, GH]), sb("a_log", [P, GH])
        gx, gabs, glog, gtotal, gbeta = (sb(n, [P, TB, GH]) for n in ("gx", "gabs", "glog", "gtotal", "gbeta"))
        gate_cols = sb("gate_cols", [P, GH, G_KINDS, TB])
        conv_w, norm_w = sb("conv_w", [P, GH * 3 * TAPS]), sb("gdn_norm_w", [P, 1])
        taps = sb("taps", [P, 3, TAPS])
        pre = sb("pre", [P, 4, PAD + T])
        y, th, squares = sb("y", [P, 4, T]), sb("th", [P, T]), sb("squares", [P, 2, T])
        log_row, beta_row = sb("log_row", [P, TB, P]), sb("beta_row", [P, TB, P])
        decay, decay_le, exp_run = sb("decay", [P, T]), sb("decay_le", [P, T]), sb("exp_run", [P, T])
        sq_sum, inv_norm = sb("sq_sum", [P, 2, TB]), sb("inv_norm", [P, 2, TB])
        col = sb("col", [P, 5, TB])
        now, gate = sb("col_now", [P, 5, TB]), sb("gate", [P, G_KINDS, TB])
        low_t, qk_t, q_run = sb("low_t", [P, T]), sb("qk_t", [P, T]), sb("q_run", [P, T])
        prod, inv, inv_t = sb("prod", [P, T]), sb("inv", [P, T]), sb("inv_t", [P, T])
        k_beta, k_end, v_beta = sb("k_beta", [P, T]), sb("k_end", [P, T]), sb("v_beta", [P, T])
        w_t, v_new, state = sb("w_t", [P, T]), sb("v_new", [P, T]), sb("state", [P, P])
        tail = RmsTail(core, ctx, "gdn", sb("gdn_sq", [P, TB, P]))
        C_RQ, C_RK, C_NEG_BETA, C_BETA_EXP, C_TO_END = range(5)

        s_params, s_chain, s_zero, s_ot_free = sem("params_loaded"), sem("dve_chain"), sem("pads_zeroed"), core.s_free["gdn_ot_free"]
        s_g_copied = sem("gates_copied")
        s_bank_free = core.s_free["gdn_bank_free"]
        s_g_in, s_g_split, s_g_proj, s_g_dve, s_g_act, s_g_sums = (
            sem(n) for n in ("gates_in", "gates_split", "gates_proj", "gates_dve", "gates_act", "gates_sums"))
        s_fill, s_cut = sem("masks_filled"), sem("masks_cut")
        s_copied = [sem(f"copied_{x}") for x in "qkvz"]
        s_conv, s_tanh, s_y = ([sem(f"{n}_{x}") for x in "qkvz"] for n in ("conv", "tanh", "silu"))
        s_squares, s_ssq, s_sum, s_inv_norm = sem("squares"), sem("square_sums"), sem("sums_plus_eps"), sem("inv_norms")
        s_log_row, s_beta_row, s_log_b, s_beta_b = sem("log_row"), sem("beta_row"), sem("log_broadcast"), sem("beta_broadcast")
        s_diff, s_exp, s_exp_run, s_decay, s_decay_le = sem("log_decay"), sem("decay_exp"), sem("run_exp"), sem("decay"), sem("decay_masked")
        s_q_run, s_turned_k, s_turned_v, s_kk, s_qk = sem("q_decayed"), sem("k_turned"), sem("v_turned"), sem("kk_ready"), sem("qk_ready")
        s_low, s_prod_mm, s_prod = sem("low_ready"), sem("prod_mm"), sem("prod_ready")
        s_x_mm, s_x, s_xt_mm, s_xt = sem("inv_mm"), sem("inv_ready"), sem("inv_t_mm"), sem("inv_t_ready")
        s_taken, s_w_mm, s_w = sem("kv_scaled"), sem("w_mm"), sem("w_ready")
        s_v_mm, s_v, s_s_mm, s_s, s_o = sem("v_new_mm"), sem("v_new_ready"), sem("state_mm"), sem("state_ready"), sem("o_ready")
        block = ctx.enter_context(nc.Block())

        def chunk(tile, n):
            return tile[:, n * P:(n + 1) * P]

        def kind(k):
            return gate_cols[:, :, k, :].rearrange("p h b -> p b h")

        def per_head(row):
            return row.unsqueeze(1).to_broadcast([P, TB, GH])

        def column(k, head):
            return gate_cols[:, bass.ds(head, 1), k, :].rearrange("p h b -> p (h b)")

        @block.sync
        def _(sp):
            sp.dma_start(wg[:, :, :], dram["w_gates"]).then_inc(s_g_in, 16)
            sp.dma_start(dt_bias[:, :], dram["dt_bias"].partition_broadcast(P)).then_inc(s_g_in, 16)
            sp.dma_start(a_log[:, :], dram["a_log"].partition_broadcast(P)).then_inc(s_g_in, 16)
            sp.dma_start(conv_w[:, :], dram["conv_w"]).then_inc(s_params, 16)
            sp.dma_start(norm_w[:, :], dram["gdn_norm_w"]).then_inc(s_params, 16)
            with sp.Fori(0, GH - 1) as i:
                for u in range(UT):
                    core.load_unit(sp, dram["w_gdn"][i * UT + u + 2], U0 + 2 + u, UT, i)
            for u in range(UT):
                n = (GH - 1) * UT + u + 2
                src = dram["w_gdn"][n] if n < UNITS_GDN else dram["w_out"][n - UNITS_GDN, 0]
                core.load_unit(sp, src, U0 + n)

        @block.tensor
        def _(pe):
            def broadcast_logs(h):
                pe.wait_ge(s_log_row, h)
                pe.matmul(bank[:, 2, :], core.ones[:, :], log_row[:, :, :], start=True, stop=True).then_inc(s_log_b, 1)

            def broadcast_betas(h):
                pe.wait_ge(s_beta_row, h)
                pe.matmul(bank[:, 3, :], core.ones[:, :], beta_row[:, :, :], start=True, stop=True).then_inc(s_beta_b, 1)

            def square_sums(h):
                pe.wait_ge(s_squares, h)
                for x in (Q, K):
                    for n in range(TB):
                        mm = pe.matmul(bank[:, 3, TB * x + n:TB * x + n + 1], chunk(squares[:, x, :], n), core.ones[:, 0:1],
                                       start=True, stop=True)
                mm.then_inc(s_ssq, 1)

            def turn(i, base, project):
                s1 = lambda m, k: at(m * base + k, m, i)
                c = U0 + UT * (base + 1)
                filled = [0]

                def fill(n):
                    while project and n > 0:
                        u, m = divmod(filled[0], 48)
                        e = min(48, m + n)
                        if m == 0 and u >= 2:
                            pe.wait_ge(s_copied[u - 2], s1(1, 2))
                        core.by_feature(pe, bank[:, u % 2, :], c + u, UT, i, (m, e))
                        filled[0] += e - m
                        n -= e - m

                for x in (Q, K, V):
                    pe.wait_ge(s_y[x], s1(1, 1))
                for n in range(TB):
                    mm = pe.matmul(chunk(bank[:, 5, :], n), chunk(y[:, K, :], n), chunk(y[:, K, :], n), start=True, stop=True)
                mm.then_inc(s_kk, 1)
                for n in range(TB):
                    mm = pe.transpose(chunk(bank[:, 7, :], n), chunk(y[:, V, :], n), core.ident[:, :])
                mm.then_inc(s_turned_v, 1)
                for n in range(TB):
                    mm = pe.matmul(chunk(bank[:, 4, :], n), chunk(y[:, K, :], n), chunk(y[:, Q, :], n), start=True, stop=True)
                mm.then_inc(s_qk, 1)
                fill(FILL_FIRST)
                pe.wait_ge(s_bank_free, s1(1, 1))
                for n in range(TB):
                    mm = pe.transpose(chunk(bank[:, 6, :], n), chunk(y[:, K, :], n), core.ident[:, :])
                mm.then_inc(s_turned_k, 1)
                for lv in range(LEVELS):
                    fill(FILL_LEVEL)
                    if lv == 0:
                        pe.wait_ge(s_low, s1(1, 1))
                    else:
                        pe.wait_ge(s_x, s1(LEVELS - 1, lv))
                    for n in range(TB):
                        if lv == 0:
                            mm = pe.transpose(chunk(bank[:, 2, :], n), chunk(low_t, n), core.ident[:, :])
                        else:
                            mm = pe.matmul(chunk(bank[:, 2, :], n), chunk(low_t, n), chunk(inv, n), start=True, stop=True)
                    mm.then_inc(s_prod_mm, 1)
                    fill(FILL_LEVEL)
                    pe.wait_ge(s_prod, s1(LEVELS, lv + 1))
                    if lv:
                        pe.wait_ge(s_xt, s1(LEVELS, lv))
                        if lv < LEVELS - 1:
                            for n in range(TB):
                                mm = pe.matmul(chunk(bank[:, 3, :], n), chunk(inv_t, n), chunk(prod, n), start=True, stop=True)
                            mm.then_inc(s_x_mm, 1)
                    for n in range(TB):
                        if lv == 0:
                            mm = pe.transpose(chunk(bank[:, 5, :], n), chunk(prod, n), core.ident[:, :])
                        else:
                            mm = pe.matmul(chunk(bank[:, 5, :], n), chunk(prod, n), chunk(inv_t, n), start=True, stop=True)
                    mm.then_inc(s_xt_mm, 1)
                if project:
                    broadcast_logs(s1(1, 2))
                pe.wait_ge(s_xt, s1(LEVELS, LEVELS))
                pe.wait_ge(s_taken, s1(4, 4))
                for n in range(TB):
                    mm = pe.matmul(chunk(bank[:, 6, :], n), chunk(k_beta, n), chunk(inv_t, n), start=True, stop=True)
                mm.then_inc(s_w_mm, 1)
                for n in range(TB):
                    if n == 1:
                        pe.wait_ge(s_w, s1(1, 1))
                        pe.wait_ge(s_q_run, s1(1, 1))
                    if n:
                        pe.wait_ge(s_s, s1(TB - 1, n))
                    mm = pe.matmul(chunk(bank[:, 7, :], n), chunk(inv_t, n), chunk(v_beta, n), start=True, stop=(n == 0))
                    if n:
                        mm = pe.matmul(chunk(bank[:, 7, :], n), chunk(w_t, n), state[:, :], start=False, stop=True)
                    mm.then_inc(s_v_mm, 1)
                    if n:
                        pe.matmul(chunk(bank[:, 4, :], n), chunk(q_run, n), state[:, :], start=True, stop=False)
                    fill(FILL_CHUNK)
                    pe.wait_ge(s_v, s1(TB, n + 1))
                    if n < TB - 1:
                        pe.matmul(bank[:, 5, 0:P], chunk(k_end, n), chunk(v_new, n), start=True, stop=True).then_inc(s_s_mm, 1)
                    mm = pe.matmul(chunk(bank[:, 4, :], n), chunk(qk_t, n), chunk(v_new, n), start=(n == 0), stop=True)
                    if n == 1 and project:
                        square_sums(s1(1, 2))
                mm.then_inc(s_o, 1)
                if project:
                    broadcast_betas(s1(1, 2))
                fill(FILL_LAST)
                tail.turn(pe, s1(1, 0), bank[:, 6, :])
                assert not project or filled[0] == 4 * 48

            pe.wait_ge(s_g_split, 2)
            for k in range(KD):
                for term, (x, w) in enumerate(((core.act_hi, wg_hi), (core.act_hi, wg_lo), (core.act_lo, wg_hi))):
                    mm = pe.matmul(bank[0:2 * GH, 2, :], w[:, k, :], x[:, k, :], start=(k == 0 and term == 0),
                                   stop=(k == KD - 1 and term == 2))
            mm.then_inc(s_g_proj, 1)
            core.by_feature(pe, bank[:, 0, :], U0, part=(0, 12))
            pe.wait_ge(s_g_copied, 1)
            for b in range(TB):
                mm = pe.transpose(bank[:, 5, b * 2 * GH:(b + 1) * 2 * GH], ab_t[:, b * P:(b + 1) * P], core.ident[0:2 * GH, 0:2 * GH])
            mm.then_inc(s_g_proj, 1)
            core.by_feature(pe, bank[:, 0, :], U0, part=(12, 48))
            pe.wait_ge(s_g_dve, 6)
            flat = glog[:, :, :].rearrange("p b h -> p (b h)")
            pe.matmul(bank[:, 3, 0:TB * GH], core.tri_le[:, :], flat, start=True, stop=True).then_inc(s_g_sums, 1)
            pe.matmul(bank[:, 4, 0:TB * GH], core.ones[:, :], flat, start=True, stop=True).then_inc(s_g_sums, 1)
            for u in range(1, UT):
                if u >= 2:
                    pe.wait_ge(s_copied[u - 2], 1)
                core.by_feature(pe, bank[:, u % 2, :], U0 + u)
                if u == 2:
                    broadcast_logs(1)
            square_sums(1)
            broadcast_betas(1)
            with pe.Fori(0, GH - 1) as i:
                turn(i, 0, True)
            turn(None, GH - 1, False)

        @block.scalar
        def _(act):
            def copied(u, h, used, per, i):
                act.wait_ge(core.s_used, at(used, per, i))
                act.activation(pre[:, u, PAD:PAD + T], bank[:, u % 2, :], ACT.Copy).then_inc(s_copied[u], 1)

            def tanh(x, h):
                act.wait_ge(s_conv[x], h)
                act.activation(th[:, :], y[:, x, :], ACT.Tanh, scale=0.5).then_inc(s_tanh[x], 1)

            def tanh_z(h):
                act.wait_ge(s_y[V], h)
                act.wait_ge(s_copied[Z], h)
                act.activation(th[:, :], pre[:, Z, PAD:PAD + T], ACT.Tanh, scale=0.5).then_inc(s_tanh[Z], 1)

            def square(h):
                act.wait_ge(s_y[Q], h)
                act.wait_ge(s_y[K], h)
                act.activation(squares[:, :, :], y[:, Q:K + 1, :], ACT.Square, scale=0.5).then_inc(s_squares, 1)

            def exp_of_runs(h):
                act.wait_ge(s_log_b, h)
                act.activation(exp_run[:, :], bank[:, 2, :], ACT.Exp).then_inc(s_exp_run, 1)

            def exp_of_decays(h):
                act.wait_ge(s_diff, h)
                act.activation(decay[:, :], decay[:, :], ACT.Exp).then_inc(s_exp, 1)

            def turn(i, base, project):
                s1 = lambda m, k: at(m * base + k, m, i)
                c = U0 + UT * (base + 1)

                def take(u):
                    if project:
                        copied(u, None, c + u + 1, UT, i)
                        core.split_hi(act, c + u + 2, UT, i)

                def take_w():
                    act.wait_ge(s_w_mm, s1(1, 1))
                    act.activation(w_t[:, :], bank[:, 6, :], ACT.Copy, scale=-1.0).then_inc(s_w, 1)

                tanh_z(s1(1, 1))
                if not project:
                    take_w()
                    return
                h = s1(1, 2)
                take(0)
                tanh(Q, h)
                take(1)
                tanh(K, h)
                take(2)
                exp_of_runs(h)
                take_w()
                square(h)
                exp_of_decays(h)
                tanh(V, h)
                take(3)

            act.preload_act_table_set("natural_log_exp_and_others")
            act.wait_ge(s_g_in, 48)
            act.activation(wg_hi[:, :, :], wg[:, :, :], ACT.Copy).then_inc(s_g_split, 1)
            act.activation(a_log[:, :], a_log[:, :], ACT.Exp).then_inc(s_g_act, 1)
            act.wait_ge(s_g_proj, 1)
            act.activation(ab_t[:, :], bank[0:2 * GH, 2, :], ACT.Copy).then_inc(s_g_copied, 1)
            act.wait_ge(s_g_dve, 3)
            act.activation(gabs[:, :, :], gabs[:, :, :], ACT.Exp, scale=-1.0).then_inc(s_g_act, 1)
            act.wait_ge(s_g_act, 2)
            act.activation(gabs[:, :, :], gabs[:, :, :], ACT.Ln, bias=1.0).then_inc(s_g_act, 1)
            act.activation(gbeta[:, :, :], gbeta[:, :, :], ACT.Exp, scale=-1.0).then_inc(s_g_act, 1)
            act.preload_act_table_set("exp_and_others")
            copied(0, 1, U0 + 1, 0, None)
            core.split_hi(act, U0 + 2)
            act.wait_ge(s_g_dve, 13)
            act.activation(gx[:, :, :], gx[:, :, :], ACT.Exp).then_inc(s_g_act, 1)
            act.activation(gabs[:, :, :], gabs[:, :, :], ACT.Exp).then_inc(s_g_act, 1)
            act.activation(gtotal[:, :, :], gtotal[:, :, :], ACT.Exp).then_inc(s_g_act, 1)
            tanh(Q, 1)
            copied(1, 1, U0 + 2, 0, None)
            core.split_hi(act, U0 + 3)
            tanh(K, 1)
            square(1)
            copied(2, 1, U0 + 3, 0, None)
            core.split_hi(act, U0 + 4)
            exp_of_runs(1)
            exp_of_decays(1)
            tanh(V, 1)
            copied(3, 1, U0 + 4, 0, None)
            core.split_hi(act, U0 + 5)
            with act.Fori(0, GH - 1) as i:
                turn(i, 0, True)
            turn(None, GH - 1, False)

        @block.vector
        def _(dve):
            n_taps = 3 * TAPS

            def conv(chain, x, h, some):
                if some[0] == 0:
                    dve.wait_ge(s_copied[x], h)
                for tap in some:
                    src, w = pre[:, x, tap:tap + T], taps[:, x, tap:tap + 1]
                    if tap == 0:
                        ins = dve.tensor_scalar(y[:, x, :], src, w, None, ALU.mult)
                    else:
                        ins = dve.scalar_tensor_tensor(out=y[:, x, :], in0=src, scalar=w, in1=y[:, x, :],
                                                       op0=ALU.mult, op1=ALU.add)
                    if tap == TAPS - 1:
                        ins.then_inc(s_conv[x], 1)
                    else:
                        chain.link(ins)

            def silu(x, h):
                dve.wait_ge(s_tanh[x], h)
                src = pre[:, Z, PAD:PAD + T] if x == Z else y[:, x, :]
                dve.scalar_tensor_tensor(out=y[:, x, :], in0=th[:, :], scalar=1.0, in1=src,
                                         op0=ALU.add, op1=ALU.mult).then_inc(s_y[x], 1)

            def log_rows(h):
                dve.tensor_tensor(log_row[:, :, :], over_blocks(core.tri_le[:, :]), over_columns(column(G_LOG, h)), ALU.mult).then_inc(s_log_row, 1)

            def decays(chain, head, h):
                dve.wait_ge(s_log_b, h)
                dve.wait_ge(s_exp_run, h)
                chain.link(dve.tensor_tensor(blocks(decay[:, :]), blocks(bank[:, 2, :]), over_columns(column(G_RUN, head)), ALU.subtract))
                dve.tensor_scalar(decay[:, :], decay[:, :], 0.0, None, ALU.min).then_inc(s_diff, 1)

            def norms(h):
                dve.wait_ge(s_ssq, h)
                dve.tensor_scalar(sq_sum[:, :, :], bank[:, 3, 0:2 * TB].rearrange("p (x b) -> p x b", x=2), RMS_EPS, None,
                                  ALU.add).then_inc(s_sum, 1)

            def columns(chain, head, h):
                dve.wait_ge(s_inv_norm, h)
                chain.mark(dve.tensor_scalar(col[:, C_RQ, :], inv_norm[:, Q, :], 0.5 * SCALE, None, ALU.mult))
                chain.link(dve.tensor_scalar(col[:, C_RK, :], inv_norm[:, K, :], 0.5, None, ALU.mult))
                chain.mark(dve.tensor_tensor(col[:, C_NEG_BETA, :], column(G_NEG_BETA, head), col[:, C_RK, :], ALU.mult))
                chain.mark(dve.tensor_tensor(col[:, C_BETA_EXP, :], column(G_BETA_EXP, head), col[:, C_RK, :], ALU.mult))
                chain.mark(dve.tensor_tensor(col[:, C_TO_END, :], column(G_TO_END, head), col[:, C_RK, :], ALU.mult))
                chain.wait()
                dve.tensor_tensor(beta_row[:, :, :], over_blocks(core.ident[:, :]), over_columns(col[:, C_NEG_BETA, :]), ALU.mult).then_inc(s_beta_row, 1)
                dve.wait_ge(s_exp, h)
                dve.tensor_tensor(blocks(decay[:, :]), blocks(decay[:, :]), over_columns(col[:, C_RK, :]), ALU.mult).then_inc(s_decay, 1)

            def turn(i, base, project, start, per):
                s1 = lambda m, k: at(m * base + k, m, i)
                c = U0 + UT * (base + 1)
                chain = Chain(dve, s_chain, start + per * base, per, i)
                h, head = s1(1, 2), s1(1, 1)

                def split(u):
                    core.split_lo(dve, c + u + 2, UT, i)

                chain.mark(dve.tensor_copy(gate[:, :, :], gate_cols[:, bass.ds(s1(1, 0), 1), :, :].rearrange("p h k b -> p (h k) b")))
                chain.mark(dve.tensor_copy(now[:, :, :], col[:, :, :]))
                dve.wait_ge(s_kk, s1(1, 1))
                dve.wait_ge(s_decay, s1(1, 1))
                chain.link(dve.tensor_tensor(low_t[:, :], bank[:, 5, :], decay[:, :], ALU.mult))
                dve.wait_ge(s_beta_b, s1(1, 1))
                dve.tensor_tensor(low_t[:, :], low_t[:, :], bank[:, 3, :], ALU.mult).then_inc(s_low, 1)
                if project:
                    chain.link(dve.tensor_copy(taps[:, :, :].rearrange("p c k -> p (c k)"), conv_w[:, bass.ds(s1(n_taps, n_taps), n_taps)]))
                for lv in range(LEVELS):
                    dve.wait_ge(s_prod_mm, s1(LEVELS, lv + 1))
                    mask = level_mask[:, lv, :].unsqueeze(1).to_broadcast([P, TB, P])
                    dve.tensor_tensor(blocks(prod[:, :]), blocks(bank[:, 2, :]), mask, ALU.mult).then_inc(s_prod, 1)
                    if lv == 0:
                        dve.wait_ge(s_prod, s1(LEVELS, 1))
                        dve.tensor_tensor(blocks(inv[:, :]), blocks(prod[:, :]), over_blocks(core.ident[:, :]), ALU.add).then_inc(s_x, 1)
                        dve.wait_ge(s_turned_k, s1(1, 1))
                        dve.tensor_tensor(blocks(k_beta[:, :]), blocks(bank[:, 6, :]), over_columns(now[:, C_BETA_EXP, :]), ALU.mult).then_inc(s_taken, 1)
                    elif lv < LEVELS - 1:
                        dve.wait_ge(s_x_mm, s1(LEVELS - 2, lv))
                        dve.tensor_tensor(inv[:, :], inv[:, :], bank[:, 3, :], ALU.add).then_inc(s_x, 1)
                    dve.wait_ge(s_xt_mm, s1(LEVELS, lv + 1))
                    x_t = blocks(inv_t[:, :]) if lv else over_blocks(core.ident[:, :])
                    dve.tensor_tensor(blocks(inv_t[:, :]), x_t, blocks(bank[:, 5, :]), ALU.add).then_inc(s_xt, 1)
                    if lv == 1:
                        dve.tensor_tensor(blocks(k_end[:, :]), blocks(bank[:, 6, :]), over_columns(now[:, C_TO_END, :]), ALU.mult).then_inc(s_taken, 1)
                        dve.wait_ge(s_turned_v, s1(1, 1))
                        dve.tensor_tensor(blocks(v_beta[:, :]), blocks(bank[:, 7, :]), over_columns(gate[:, G_BETA_HALF, :]), ALU.mult).then_inc(s_taken, 1)
                        silu(Z, s1(1, 1))
                    if lv == 2:
                        dve.wait_ge(s_qk, s1(1, 1))
                        dve.wait_ge(s_decay_le, s1(1, 1))
                        dve.tensor_tensor(qk_t[:, :], bank[:, 4, :], decay_le[:, :], ALU.mult).then_inc(s_taken, 1)
                        if project:
                            dve.wait_ge(s_q_run, s1(1, 1))
                            split(0)
                            conv(chain, Q, h, (0, 1))
                    if project and lv == 3:
                        conv(chain, Q, h, (2, 3))
                    if project and lv == 4:
                        silu(Q, h)
                        split(1)
                        conv(chain, K, h, (0,))
                    if project and lv == 5:
                        conv(chain, K, h, (1, 2, 3))
                        log_rows(head)
                if project:
                    silu(K, h)
                    split(2)
                for n in range(TB):
                    dve.wait_ge(s_v_mm, s1(TB, n + 1))
                    dve.tensor_copy(chunk(v_new, n), chunk(bank[:, 7, :], n)).then_inc(s_v, 1)
                    if n < TB - 1:
                        dve.wait_ge(s_s_mm, s1(TB - 1, n + 1))
                        if n == 0:
                            dve.tensor_copy(state[:, :], bank[:, 5, 0:P]).then_inc(s_s, 1)
                        else:
                            dve.wait_ge(s_s, s1(TB - 1, n))
                            dve.scalar_tensor_tensor(out=state[:, :], in0=state[:, :], scalar=gate[:, G_TOTAL, n:n + 1],
                                                     in1=bank[:, 5, 0:P], op0=ALU.mult, op1=ALU.add).then_inc(s_s, 1)
                    if project and n == 0:
                        conv(chain, V, h, (0, 1))
                    if project and n == 1:
                        conv(chain, V, h, (2, 3))
                        norms(h)
                    if project and n == 2:
                        decays(chain, head, h)
                if project:
                    columns(chain, head, h)
                dve.wait_ge(s_o, s1(1, 1))
                chain.link(dve.tensor_tensor(tail.o[:, :, :], blocks(bank[:, 4, :]), over_columns(now[:, C_RQ, :]), ALU.mult))
                tail.norm_on_vector(dve, chain, s1(1, 1))
                if project:
                    silu(V, h)
                    split(3)
                dve.wait_ge(tail.s_turned, s1(1, 1))
                dve.wait_ge(s_ot_free, s1(1, 1))
                dve.scalar_tensor_tensor(out=tail.ot[:, :, :], in0=blocks(bank[:, 6, :]), scalar=norm_w[:, 0:1],
                                         in1=blocks(y[:, Z, :]), op0=ALU.mult, op1=ALU.mult).then_inc(tail.s_ot, 1)
                return chain.n

            g_links = [0]

            def link(ins):
                g_links[0] += 1
                ins.then_inc(s_g_dve, 1)
                dve.wait_ge(s_g_dve, g_links[0])

            dve.memset(pre[:, :, 0:PAD], 0.0).then_inc(s_zero, 1)
            dve.wait_ge(s_g_split, 1)
            dve.tensor_tensor(wg_lo[:, :, :], wg[:, :, :], wg_hi[:, :, :].bitcast(F32), ALU.subtract).then_inc(s_g_split, 1)
            dve.wait_ge(s_g_proj, 2)
            ab = bank[:, 5, 0:TB * 2 * GH].rearrange("p (b k h) -> p b k h", b=TB, k=2)
            link(dve.tensor_tensor(gx[:, :, :], ab[:, :, 0, :], per_head(dt_bias[:, :]), ALU.add))
            link(dve.scalar_tensor_tensor(out=gabs[:, :, :], in0=gx[:, :, :], scalar=-1.0, in1=gx[:, :, :],
                                          op0=ALU.mult, op1=ALU.max))
            link(dve.tensor_copy(gbeta[:, :, :], ab[:, :, 1, :]))
            dve.wait_ge(s_g_act, 3)
            link(dve.scalar_tensor_tensor(out=glog[:, :, :], in0=gx[:, :, :], scalar=0.0, in1=gabs[:, :, :],
                                          op0=ALU.max, op1=ALU.add))
            link(dve.tensor_tensor(glog[:, :, :], glog[:, :, :], per_head(a_log[:, :]), ALU.mult))
            link(dve.tensor_scalar(glog[:, :, :], glog[:, :, :], -1.0, None, ALU.mult))
            dve.wait_ge(s_g_act, 4)
            link(dve.tensor_scalar(gbeta[:, :, :], gbeta[:, :, :], 1.0, None, ALU.add))
            link(dve.reciprocal(gbeta[:, :, :], gbeta[:, :, :]))
            link(dve.tensor_scalar(kind(G_BETA_HALF), gbeta[:, :, :], 0.5, None, ALU.mult))
            link(dve.tensor_scalar(kind(G_NEG_BETA), gbeta[:, :, :], -1.0, None, ALU.mult))
            dve.wait_ge(s_g_sums, 2)
            run = bank[:, 3, 0:TB * GH].rearrange("p (b h) -> p b h", b=TB)
            link(dve.tensor_copy(gx[:, :, :], run))
            link(dve.tensor_copy(gtotal[:, :, :], bank[:, 4, 0:TB * GH].rearrange("p (b h) -> p b h", b=TB)))
            link(dve.tensor_tensor(gabs[:, :, :], gtotal[:, :, :], gx[:, :, :], ALU.subtract))
            link(dve.tensor_copy(kind(G_RUN), run))
            link(dve.tensor_copy(kind(G_LOG), glog[:, :, :]))
            log_rows(0)
            core.split_lo(dve, U0 + 2)
            dve.wait_ge(s_g_act, 7)
            link(dve.tensor_tensor(kind(G_BETA_EXP), gbeta[:, :, :], gx[:, :, :], ALU.mult))
            link(dve.tensor_copy(kind(G_TO_END), gabs[:, :, :]))
            link(dve.tensor_copy(kind(G_TOTAL), gtotal[:, :, :]))
            chain = Chain(dve, s_chain, 0)
            dve.wait_ge(s_zero, 1)
            dve.wait_ge(s_params, 32)
            dve.wait_ge(s_cut, 2 * LEVELS)
            chain.link(dve.tensor_scalar(norm_w[:, :], norm_w[:, :], 0.5, None, ALU.mult))
            chain.link(dve.tensor_copy(taps[:, :, :].rearrange("p c k -> p (c k)"), conv_w[:, 0:n_taps]))
            conv(chain, Q, 1, range(TAPS))
            silu(Q, 1)
            core.split_lo(dve, U0 + 3)
            conv(chain, K, 1, range(TAPS))
            silu(K, 1)
            core.split_lo(dve, U0 + 4)
            decays(chain, 0, 1)
            conv(chain, V, 1, range(TAPS))
            silu(V, 1)
            norms(1)
            columns(chain, 0, 1)
            core.split_lo(dve, U0 + 5)
            PER = 22
            with dve.Fori(0, GH - 1) as i:
                n = turn(i, 0, True, chain.n, PER)
            assert n == PER, n
            turn(None, GH - 1, False, chain.n, PER)

        @block.gpsimd
        def _(pool):
            def inv_norms(h):
                pool.wait_ge(s_sum, h)
                pool.tensor_tensor(inv_norm[:, :, :], sq_sum[:, :, :], core.half_neg[:, :].rearrange("p (x b) -> p x b", x=2), ALU.pow).then_inc(s_inv_norm, 1)

            def masked_decay(h):
                pool.wait_ge(s_decay, h)
                pool.tensor_tensor(blocks(decay_le[:, :]), blocks(decay[:, :]), over_blocks(core.tri_le[:, :]), ALU.mult).then_inc(s_decay_le, 1)

            def turn(i, base, project):
                s1 = lambda m, k: at(m * base + k, m, i)
                pool.wait_ge(s_y[Q], s1(1, 1))
                pool.wait_ge(s_exp_run, s1(1, 1))
                pool.tensor_tensor(q_run[:, :], y[:, Q, :], exp_run[:, :], ALU.mult).then_inc(s_q_run, 1)
                if project:
                    inv_norms(s1(1, 2))
                    masked_decay(s1(1, 2))
                tail.on_gpsimd(pool, s1(1, 0))
                pool.wait_ge(tail.s_ot, s1(1, 1))
                pool.sem_inc(s_bank_free, 1)
                tail.keep(pool, s1(1, 0), dram["o_kept"][s1(1, 0)])
                pool.wait_ge(tail.s_kept, s1(16, 16))
                pool.sem_inc(s_ot_free, 1)

            pool.memset(level_mask[:, :, :], 0.0).then_inc(s_fill, 1)
            pool.wait_ge(s_fill, 1)
            for lv in range(LEVELS):
                s = 1 << lv
                n = P // (2 * s)
                low = level_mask[:, lv, :].rearrange("p (n s) -> p n s", s=2 * s)[:, :, 0:s]
                pool.memset(low, 1.0).then_inc(s_fill, 1)
                pool.wait_ge(s_fill, lv + 2)
                pool.affine_select(out=low, in_=low, compare_op=ALU.is_ge, fill=0.0, base=-s,
                                   pattern=[[-2 * s, n], [0, s]], channel_multiplier=1).then_inc(s_cut, 1)
                pool.wait_ge(s_cut, 2 * lv + 1)
                pool.affine_select(out=low, in_=low, compare_op=ALU.is_ge, fill=0.0, base=2 * s - 1,
                                   pattern=[[2 * s, n], [0, s]], channel_multiplier=-1).then_inc(s_cut, 1)
            pool.sem_inc(s_ot_free, 1)
            pool.sem_inc(s_bank_free, 1)
            inv_norms(1)
            masked_decay(1)
            with pool.Fori(0, GH - 1) as i:
                turn(i, 0, True)
            turn(None, GH - 1, False)


def mix_out(core, dram):
    nc = core.nc
    bank = core.bank
    U0 = UNITS_ATT + UNITS_GDN
    STAGES = 4
    with phase(nc) as ctx:
        def sb(name, shape, dt=F32):
            return ctx.enter_context(nc.sbuf_tensor(name, shape, dt))

        def sem(name):
            return phase_semaphore(nc, ctx, "mix_out_" + name)

        rows, staged = sb("mix_rows", [P, TB, D]), sb("o_staged", [P, STAGES, T])
        ln_w, ln_b = sb("ln1_w", [P, D]), sb("ln1_b", [P, D])
        ln = LayerNorm(core, ctx, "ln1", TB).open(ctx)
        s_params, s_rows, s_chain, s_stats = sem("params_loaded"), sem("h_loaded"), sem("dve_chain"), sem("row_stats")
        s_o = [sem(f"o_loaded{n}") for n in range(STAGES)]
        s_o_hi, s_o_lo, s_added = sem("o_hi"), sem("o_lo"), core.s_free["mix_added"]
        s_normed, s_turned, s_t_hi, s_t_lo, s_kept = [sem("h1_normed_even"), sem("h1_normed_odd")], sem("h1_turned"), sem("turned_hi"), sem("turned_lo"), sem("h1_kept")
        block = ctx.enter_context(nc.Block())

        def slots(n, q):
            return [a[:, 4 * q:4 * q + 4, n * P:(n + 1) * P] for a in (core.act_hi, core.act_lo)]

        def low_part(dve, u):
            dve.wait_ge(s_t_hi, u + 1)
            hi, lo = slots(u // 4, u % 4)
            dve.tensor_tensor(lo, blocks(bank[:, u % 4, :]), hi.bitcast(F32), ALU.subtract).then_inc(s_t_lo, 1)

        @block.sync
        def _(sp):
            for h in range(HEADS):
                if h >= STAGES:
                    sp.wait_ge(s_o_lo, h - STAGES + 1)
                sp.dma_start(staged[:, h % STAGES, :], dram["o_kept"][h]).then_inc(s_o[h % STAGES], 16)
            for u in range(UNITS_OUT):
                if u == 2:
                    sp.dma_start(rows[:, :, :], dram["h_kept"].rearrange("(b p) d -> p b d", p=P)).then_inc(s_rows, 16)
                if u == 4:
                    for tile, name in ((ln_w, "ln1_w"), (ln_b, "ln1_b")):
                        sp.dma_start(tile[:, :], dram[name].partition_broadcast(P)).then_inc(s_params, 16)
                n = u + 2
                src = dram["w_out"][n % DB, n // DB] if n < UNITS_OUT else dram["peer_wq"][n - UNITS_OUT]
                core.load_unit(sp, src, U0 + n)
            for n in range(TB):
                sp.wait_ge(s_normed[n % 2], n // 2 + 1)
                sp.dma_start(dram["h1_kept"][n * P:(n + 1) * P, :], rows[:, n, :]).then_inc(s_kept, 16)
            sp.wait_ge(s_kept, 16 * TB)

        @block.tensor
        def _(pe):
            with pe.Fori(0, 2) as i:
                for d in range(2):
                    pe.wait_ge(s_added, i * 8 + 4 * d + 4)
                    for q in range(DB):
                        if d == 0:
                            pe.wait_ge(s_o_lo, KQ * (q + 1))
                        core.by_token(pe, [bank[:, 4 * d + b, :] for b in range(TB)],
                                      core.act_hi[:, 4 * q:4 * q + 4, :], core.act_lo[:, 4 * q:4 * q + 4, :],
                                      q == 0, q == DB - 1, U0 + 4 * d + q, 8, i)
            for n in range(TB):
                pe.wait_ge(s_normed[n % 2], n // 2 + 1)
                for q in range(4):
                    u = 4 * n + q
                    if u >= 4:
                        pe.wait_ge(s_t_lo, u - 3)
                    for j in range(4):
                        k = 4 * q + j
                        mm = pe.transpose(bank[:, u % 4, j * P:(j + 1) * P], rows[:, n, k * P:(k + 1) * P], core.ident[:, :])
                    mm.then_inc(s_turned, 1)

        @block.scalar
        def _(act):
            for h in range(HEADS):
                act.wait_ge(s_o[h % STAGES], 16 * (h // STAGES + 1))
                act.activation(core.act_hi[:, h, :], staged[:, h % STAGES, :], ACT.Copy).then_inc(s_o_hi, 1)
            with act.Fori(0, 2) as i:
                for u in range(8):
                    core.split_hi(act, U0 + u + 2, 8, i)
            ln.scale(act, 0, rows[:, 0, :])
            for u in range(4 * TB):
                if u % 4 == 0 and u // 4 + 1 < TB:
                    ln.scale(act, u // 4 + 1, rows[:, u // 4 + 1, :])
                act.wait_ge(s_turned, u + 1)
                act.activation(slots(u // 4, u % 4)[0], blocks(bank[:, u % 4, :]), ACT.Copy).then_inc(s_t_hi, 1)

        @block.vector
        def _(dve):
            dve.sem_inc(s_added, 8)
            for h in range(HEADS):
                dve.wait_ge(s_o_hi, h + 1)
                dve.tensor_tensor(core.act_lo[:, h, :], staged[:, h % STAGES, :], core.act_hi[:, h, :].bitcast(F32),
                                  ALU.subtract).then_inc(s_o_lo, 1)
            with dve.Fori(0, 2) as i:
                for d in range(2):
                    for q in range(DB):
                        core.split_lo(dve, U0 + 4 * d + q + 2, 8, i)
                    dve.wait_ge(core.s_used, at(U0 + 4 * d + 4, 8, i))
                    dve.wait_ge(s_rows, 16)
                    for b in range(TB):
                        r = rows[:, b, bass.ds(i * 2 * COLS + d * COLS, COLS)]
                        dve.scalar_tensor_tensor(out=r, in0=r, scalar=ALPHA, in1=bank[:, 4 * d + b, :],
                                                 op0=ALU.mult, op1=ALU.add).then_inc(s_added, 1)
                    dve.wait_ge(s_added, i * 8 + 4 * d + 4 + 8)
                    for b in range(TB):
                        dve.bn_stats(ln.stats[:, b, bass.ds(i * 2 + d, 1), :].rearrange("p q s -> p (q s)"),
                                     rows[:, b, bass.ds(i * 2 * COLS + d * COLS, COLS)]).then_inc(s_stats, 1)
            dve.wait_ge(s_stats, 16)
            dve.wait_ge(s_params, 32)
            chain = Chain(dve, s_chain, 0)
            for n in range(TB):
                ln.variance(dve, chain, n)
            for n in range(TB):
                ln.shift_of(dve, n)
            for n in range(TB):
                ln.weigh(dve, n, rows[:, n, :], ln_w[:, :])
                if n % 2 == 0:
                    ln.add_bias(dve, n, rows[:, n, :], ln_b[:, :], s_normed[0])
                for q in range(4 * (n - 1), 4 * n) if n else ():
                    low_part(dve, q)
            for q in range(4 * (TB - 1), 4 * TB):
                low_part(dve, q)

        @block.gpsimd
        def _(pool):
            for n in range(TB):
                ln.power(pool, n)
            for n in range(1, TB, 2):
                ln.add_bias(pool, n, rows[:, n, :], ln_b[:, :], s_normed[1])


def route(core, dram, chosen):
    nc = core.nc
    bank = core.bank
    U0, UT = UNITS_ATT + UNITS_GDN + UNITS_OUT, 2
    E0 = U0 + UNITS_Q
    C = TOPK * TOPK
    with phase(nc) as ctx:
        def sb(name, shape, dt=F32):
            return ctx.enter_context(nc.sbuf_tensor(name, shape, dt))

        def sem(name):
            return phase_semaphore(nc, ctx, "route_" + name)

        keys, q_t = sb("keys", [P, 2, KEYS]), sb("q_t", [P, 2, T])
        score, left = sb("score", [P, 2 * TB, KEYS]), sb("left", [P, 2 * TB, KEYS])
        best, best_i, best_f = sb("best", [P, 2 * TB, TOPK]), sb("best_i", [P, 2 * TB, TOPK], U32), sb("best_f", [P, 2 * TB, TOPK])
        cand, cand_left = sb("cand", [P, TB, C]), sb("cand_left", [P, TB, C])
        top, pos = sb("top", [P, TB, TOPK]), sb("pos", [P, TB, TOPK], U32)
        rank_i, rank = sb("rank_i", [P, 2, TB, TOPK], U32), sb("rank", [P, 2, TB, TOPK])
        hit = sb("hit", [P, 2, TB, C])
        total, inv = sb("total", [P, TB, PH]), sb("inv_total", [P, TB, PH])
        gate = chosen[:, 2, :, :]
        products = sb("products_first", [P, EB, T])
        s_products, s_stored = sem("products_copied"), sem("products_kept")
        s_read = core.s_free["route_scores_read"]
        s_keys, s_chain, s_apart = sem("keys_loaded"), sem("dve_chain"), sem("waits_apart")
        s_q, s_score_mm, s_score, s_shifted, s_ex = (
            sem(n) for n in ("q_copied", "score_mm", "score_copied", "top_shifted", "top_exp"))
        block = ctx.enter_context(nc.Block())

        def grid(tile):
            return tile.rearrange("p b (k a) -> p b k a", a=TOPK)

        def along_rank(tile):
            return tile.unsqueeze(3).to_broadcast([P, TB, TOPK, TOPK])

        def along_chosen(tile):
            return tile.unsqueeze(2).to_broadcast([P, TB, TOPK, TOPK])

        numbers = core.iota[:, 0:TOPK].unsqueeze(1).unsqueeze(1).to_broadcast([P, TB, TOPK, TOPK])

        @block.sync
        def _(sp):
            sp.dma_start(keys[:, :, :], dram["peer_keys"].rearrange("p (s k) -> p s k", s=2)).then_inc(s_keys, 16)
            with sp.Fori(0, PH - 1) as h:
                for u in range(UT):
                    core.load_unit(sp, dram["peer_wq"][h * UT + u + 2], U0 + u + 2, UT, h)
            for c in range(EB + 2):
                core.load_unit(sp, dram["peer_u"][c], E0 + c)
            for c in range(EB):
                sp.wait_ge(s_products, c + 1)
                sp.dma_start(dram["products_kept"][c], products[:, c, :]).then_inc(s_stored, 16)
            sp.wait_ge(s_stored, 16 * EB)

        @block.tensor
        def _(pe):
            pe.wait_ge(s_keys, 16)
            with pe.Fori(0, PH) as h:
                for u in range(UT):
                    core.by_feature(pe, bank[:, u, :], U0 + u, UT, h)
                for u in range(UT):
                    pe.wait_ge(s_q, h * 2 + u + 1)
                    for b in range(TB):
                        mm = pe.matmul(bank[:, 2 + u, b * P:(b + 1) * P], q_t[:, u, b * P:(b + 1) * P], keys[:, u, :],
                                       start=True, stop=True)
                mm.then_inc(s_score_mm, 1)
            for c in range(EB):
                core.by_feature(pe, bank[:, 4 + c, :], E0 + c)

        @block.scalar
        def _(act):
            def queries(h):
                for u in range(UT):
                    act.wait_ge(core.s_used, at(U0 + u + 1, UT, h))
                    act.activation(q_t[:, u, :], bank[:, u, :], ACT.Copy).then_inc(s_q, 1)
                    core.split_hi(act, U0 + u + 2, UT, h)

            def scores(h):
                act.wait_ge(s_score_mm, h + 1)
                act.wait_ge(s_read, h + 1)
                act.activation(score[:, :, :].rearrange("p b n -> p (b n)").rearrange("p (s n) -> p s n", s=2),
                               bank[:, 2:4, :], ACT.Copy).then_inc(s_score, 1)

            with act.Fori(0, PH) as h:
                queries(h)
                scores(h)
            for c in range(EB):
                act.wait_ge(core.s_used, E0 + c + 1)
                act.activation(products[:, c, :], bank[:, 4 + c, :], ACT.Copy).then_inc(s_products, 1)
                core.split_hi(act, E0 + c + 2)
            act.wait_ge(s_shifted, 1)
            act.activation(gate, gate, ACT.Exp).then_inc(s_ex, 1)

        @block.vector
        def _(dve):
            def top16(chain, x, spare, val, idx, n):
                for b in range(n):
                    chain.mark(dve.max(val[:, b, 0:8], x[:, b, :]))
                chain.wait_apart()
                for b in range(n):
                    chain.mark(dve.max_index(idx[:, b, 0:8], val[:, b, 0:8], x[:, b, :]))
                    chain.mark(dve.match_replace(spare[:, b, :], val[:, b, 0:8], x[:, b, :], NEG))
                chain.wait_apart()
                for b in range(n):
                    chain.mark(dve.max(val[:, b, 8:16], spare[:, b, :]))
                chain.wait_apart()
                for b in range(n):
                    chain.mark(dve.max_index(idx[:, b, 8:16], val[:, b, 8:16], spare[:, b, :]))
                chain.wait_apart()

            dve.sem_inc(s_read, 1)
            PER = 71
            with dve.Fori(0, PH) as h:
                chain = Chain(dve, s_chain, 0, PER, h, apart=s_apart)
                dve.wait_ge(s_score, h + 1)
                dve.sem_inc(s_apart, 1)
                top16(chain, score, left, best, best_i, 2 * TB)
                chain.mark(dve.tensor_copy(best_f[:, :, :], best_i[:, :, :]))
                dve.tensor_tensor(grid(cand[:, :, :]), along_rank(best[:, 0:TB, :]), along_chosen(best[:, TB:2 * TB, :]),
                                  ALU.add).then_inc(s_read, 1)
                dve.wait_ge(s_read, h + 2)
                dve.sem_inc(s_apart, 1)
                chain.wait_apart()
                top16(chain, cand, cand_left, top, pos, TB)
                chain.mark(dve.tensor_scalar(rank_i[:, 0, :, :], pos[:, :, :], 4, None, ALU.logical_shift_right))
                chain.mark(dve.tensor_scalar(rank_i[:, 1, :, :], pos[:, :, :], TOPK - 1, None, ALU.bitwise_and))
                here = bass.ds(h * TOPK, TOPK)
                chain.mark(dve.tensor_tensor(gate[:, :, here], top[:, :, :], top[:, :, 0:1].to_broadcast([P, TB, TOPK]), ALU.subtract))
                chain.wait()
                chain.link(dve.tensor_copy(rank[:, :, :, :], rank_i[:, :, :, :]))
                for s in range(2):
                    chain.mark(dve.tensor_tensor(grid(hit[:, s, :, :]), along_rank(rank[:, s, :, :]), numbers, ALU.is_equal))
                chain.wait()
                for s in range(2):
                    chain.mark(dve.tensor_tensor(grid(hit[:, s, :, :]), grid(hit[:, s, :, :]), along_chosen(best_f[:, s * TB:(s + 1) * TB, :]), ALU.mult))
                chain.wait()
                for s in range(2):
                    chain.mark(dve.tensor_reduce(chosen[:, s, :, here], grid(hit[:, s, :, :]), AX_X, ALU.add))
                chain.wait()
            assert chain.n == PER, chain.n
            dve.sem_inc(s_shifted, 1)
            by_head = gate.rearrange("p b (h k) -> p b h k", k=TOPK)
            tail = Chain(dve, s_chain, PER * PH)
            dve.wait_ge(s_ex, 1)
            tail.link(dve.tensor_reduce(total[:, :, :], by_head, AX_X, ALU.add))
            tail.link(dve.reciprocal(inv[:, :, :], total[:, :, :]))
            tail.mark(dve.tensor_tensor(by_head, by_head, inv[:, :, :].unsqueeze(3).to_broadcast([P, TB, PH, TOPK]), ALU.mult))

        @block.gpsimd
        def _(pool):
            core.split_lo(pool, U0 + 2)
            core.split_lo(pool, U0 + 3)
            with pool.Fori(0, PH - 1) as h:
                core.split_lo(pool, U0 + 4, UT, h)
                core.split_lo(pool, U0 + 5, UT, h)
            for c in range(2, EB + 2):
                core.split_lo(pool, E0 + c)


def spread(core, dram, chosen):
    nc = core.nc
    bank = core.bank
    QUADS = TG // 4
    U0 = UNITS_ATT + UNITS_GDN + UNITS_OUT + UNITS_Q + EB
    assert NTG == EB * (AHEAD - 1)
    with phase(nc) as ctx:
        def sb(name, shape, dt=F32):
            return ctx.enter_context(nc.sbuf_tensor(name, shape, dt))

        def sem(name):
            return phase_semaphore(nc, ctx, "spread_" + name)

        by_choice = sb("by_choice", [P, 3, T])
        now = sb("choices_now", [P, 2, 3, TG])
        row_hot, col_hot = sb("row_hot", [P, 2, 4, KEYS]), sb("col_hot", [P, 2, 4, KEYS])
        out = sb("gates_out", [P, 2, KEYS, TG])
        products = sb("products_out", [P, 2, T])
        s_turned, s_by_choice, s_now = sem("chosen_turned"), sem("by_choice_copied"), sem("group_taken")
        s_hot, s_mm = sem("one_hots_ready"), core.s_free["spread_mm"]
        s_out, s_free = core.s_free["spread_copied"], core.s_free["spread_out_free"]
        s_kept = [sem("gates_kept_even"), sem("gates_kept_odd")]
        s_products, s_products_free = core.s_free["spread_products"], core.s_free["spread_products_free"]
        s_stored = [sem("products_kept_even"), sem("products_kept_odd")]
        block = ctx.enter_context(nc.Block())

        @block.sync
        def _(sp):
            sp.sem_inc(s_free, 2)
            sp.sem_inc(s_products_free, 2)

            def turn(i, base, sources):
                for par in range(2):
                    n = 2 * base + par
                    core.load_unit(sp, sources[par], U0 + n + 2, 2, i)
                    sp.wait_ge(s_out, at((n + 1) * QUADS + 4, 2 * QUADS, i))
                    sp.dma_start(dram["gates_kept"][at(n, 2, i)], out[:, par, :, :]).then_inc(s_kept[par], 16)
                    sp.wait_ge(s_products, at(n + 3, 2, i))
                    sp.dma_start(dram["products_kept"][at(EB + n, 2, i)], products[:, par, :]).then_inc(s_stored[par], 16)
                    sp.wait_ge(s_kept[par], at(16 * (base + 1), 16, i))
                    sp.sem_inc(s_free, 1)
                    sp.wait_ge(s_stored[par], at(16 * (base + 1), 16, i))
                    sp.sem_inc(s_products_free, 1)

            with sp.Fori(0, NTG // 2 - 1) as i:
                turn(i, 0, [dram["peer_u"][i * 2 + par + EB + 2] for par in range(2)])
            turn(None, NTG // 2 - 1, [dram["peer_u"][EB * AHEAD + par] for par in range(2)])

        @block.tensor
        def _(pe):
            for kind in range(3):
                for b in range(TB):
                    mm = pe.transpose(bank[:, kind, b * P:(b + 1) * P], chosen[:, kind, b, :], core.ident[:, :])
                mm.then_inc(s_turned, 1)
            pe.sem_inc(s_mm, 2)
            with pe.Fori(0, NTG // 2) as i:
                for q in range(2 * QUADS):
                    par, part = divmod(q, QUADS)
                    pe.wait_ge(s_hot, i * 2 * QUADS + q + 1)
                    pe.wait_ge(s_out, i * 2 * QUADS + q + 1)
                    for t in range(4):
                        mm = pe.matmul(bank[:, 4 + q % 4, t * P:(t + 1) * P], col_hot[:, q % 2, t, :], row_hot[:, q % 2, t, :],
                                       start=True, stop=True)
                    mm.then_inc(s_mm, 1)
                    if part == 0:
                        pe.wait_ge(s_products, i * 2 + par + 1)
                    core.by_feature(pe, bank[:, par, :], U0 + par, 2, i, (48 // QUADS * part, 48 // QUADS * (part + 1)))

        @block.scalar
        def _(act):
            for kind in range(3):
                act.wait_ge(s_turned, kind + 1)
                act.activation(by_choice[:, kind, :], bank[:, kind, :], ACT.Copy).then_inc(s_by_choice, 1)
            act.sem_inc(s_out, 4)
            act.sem_inc(s_products, 2)
            with act.Fori(0, NTG // 2) as i:
                for q in range(2 * QUADS):
                    par, t = divmod(q, QUADS)
                    if t == 0:
                        act.wait_ge(s_free, i * 2 + par + 1)
                    act.wait_ge(s_mm, i * 2 * QUADS + q + 3)
                    act.activation(out[:, par, :, 4 * t:4 * t + 4], bank[:, 4 + q % 4, :].rearrange("p (t n) -> p n t", t=4),
                                   ACT.Copy).then_inc(s_out, 1)
                    if t == QUADS - 1:
                        act.wait_ge(core.s_used, at(U0 + par + 1, 2, i))
                        act.wait_ge(s_products_free, i * 2 + par + 1)
                        act.activation(products[:, par, :], bank[:, par, :], ACT.Copy).then_inc(s_products, 1)
                        core.split_hi(act, U0 + par + 2, 2, i)

        @block.gpsimd
        def _(pool):
            with pool.Fori(0, NTG // 2) as i:
                for par in range(2):
                    core.split_lo(pool, U0 + par + 2, 2, i)

        @block.vector
        def _(dve):
            dve.wait_ge(s_by_choice, 3)
            with dve.Fori(0, NTG // 2) as i:
                for par in range(2):
                    dve.wait_ge(s_mm, i * 2 * QUADS + par * QUADS + 1)
                    dve.tensor_copy(now[:, par, :, :], by_choice[:, :, bass.ds(i * 2 * TG + par * TG, TG)]).then_inc(s_now, 1)
                    dve.wait_ge(s_now, i * 2 + par + 1)
                    for q in range(QUADS):
                        n = par * QUADS + q
                        dve.wait_ge(s_mm, i * 2 * QUADS + n + 1)
                        dve.tensor_tensor(row_hot[:, n % 2, :, :], core.iota[:, :].unsqueeze(1).to_broadcast([P, 4, P]),
                                          now[:, par, 0, 4 * q:4 * q + 4].unsqueeze(2).to_broadcast([P, 4, P]), ALU.is_equal)
                        for t in range(4):
                            c = 4 * q + t
                            ins = dve.tensor_scalar(col_hot[:, n % 2, t, :], core.iota[:, :], now[:, par, 1, c:c + 1],
                                                    now[:, par, 2, c:c + 1], ALU.is_equal, ALU.mult)
                        ins.then_inc(s_hot, 1)


def experts(core, dram, acc, ln, gates):
    nc = core.nc
    bank = core.bank
    E0 = UNITS_ATT + UNITS_GDN + UNITS_OUT + UNITS_Q
    with phase(nc) as ctx:
        def sb(name, shape, dt=F32):
            return ctx.enter_context(nc.sbuf_tensor(name, shape, dt))

        def sem(name):
            return phase_semaphore(nc, ctx, "experts_" + name)

        gelu, weighted = sb("gelu", [P, 2, T]), sb("weighted", [P, 2, T])
        p_hi, p_lo = sb("p_hi", [P, 2, EB, T], F32R), sb("p_lo", [P, 2, EB, T], F32R)
        s_gates = [sem("gates_even"), sem("gates_odd")]
        s_products = [sem("products_even"), sem("products_odd")]
        s_params = sem("ln2_params_loaded")
        s_acc, s_scaled = sem("h1_loaded"), sem("h1_scaled")
        s_gelu, s_weighted, s_p_hi, s_p_lo = sem("gelu_done"), sem("gates_applied"), sem("p_hi_done"), sem("p_lo_done")
        s_out, s_added, s_stats = sem("out_block_ready"), core.s_free["expert_added"], sem("row_stats")
        block = ctx.enter_context(nc.Block())

        def u_unit(g, c):
            return (E0 + EB * AHEAD if g == first else E0 + 8 * g[0] - 4) + c, 8 * g[1], g[2]

        def v_unit(g, d):
            if g[0] < AHEAD:
                return E0 + EB * (AHEAD + 1) + DB * g[0] + d, 4 * g[1], g[2]
            return E0 + 8 * g[0] + (4 if g == last else 8) + d, 8 * g[1], g[2]

        first, last = (AHEAD, 0, None), (GROUPS - 1, 0, None)

        def steps(eng, kept, split, held, inner, outer, before_outer=lambda: None):
            for c in range(EB):
                kept((0, 0, None), c)
                if c % 2:
                    split(*u_unit(first, c // 2))
            split(*u_unit(first, 2))
            split(*u_unit(first, 3))
            before_outer()
            with eng.Fori(0, (AHEAD - 1) // 2) as j:
                for k in range(2):
                    for c in range(EB):
                        kept((k + 1, 2, j), c)
                        outer((k, 2, j), c)
            for d in range(DB):
                held(d)
                outer((AHEAD - 1, 0, None), d)
            with eng.Fori(0, (GROUPS - AHEAD - 1) // 2) as j:
                for k in range(AHEAD, AHEAD + 2):
                    inner((k + 1, 2, j))
                    for d in range(DB):
                        outer((k, 2, j), d)
            for d in range(DB):
                outer(last, d)

        @block.sync
        def _(sp):
            def load_gates(g):
                if g[0] >= 2:
                    sp.wait_ge(s_weighted, at(EB * (g[0] - 1), EB * g[1], g[2]))
                src = dram["gates_kept"][:, :, bass.ds(at(EB * g[0], EB * g[1], g[2]), EB), :]
                sp.dma_start(gates[:, g[0] % 2, :, :, :].rearrange("p g k t -> p g (k t)"),
                             src.rearrange("g p k t -> p g (k t)")).then_inc(s_gates[g[0] % 2], 16)

            def load_products(g, c):
                if c >= 2 or g:
                    sp.wait_ge(s_weighted, EB * g + c - 1)
                sp.dma_start(gelu[:, c % 2, :], dram["products_kept"][EB * g + c]).then_inc(s_products[c % 2], 16)

            def load(unit, src):
                core.load_unit(sp, src, *unit)

            def load_u(g, c):
                load(u_unit(g, c), dram["peer_u"][at(EB * g[0] + c, EB * g[1], g[2])])

            def load_v(g, d):
                load(v_unit(g, d), dram["peer_v"][at(g[0], g[1], g[2]), d])

            load_gates((0, 0, None))
            load_products(0, 0)
            load_products(0, 1)
            load_u(first, 2)
            load_u(first, 3)
            load_gates((1, 0, None))
            load_products(0, 2)
            load_products(0, 3)
            sp.dma_start(acc[:, :, :], dram["h1_kept"].rearrange("(b p) d -> p b d", p=P)).then_inc(s_acc, 16)
            for d in (0, 1):
                load_v((0, 0, None), d)
            for g in range(AHEAD - 1):
                load_gates((g + 2, 0, None))
                for d in range(DB):
                    load_products(g + 1, d)
                    n = DB * g + d + 2
                    load_v((n // DB, 0, None), n % DB)
            load_gates((AHEAD + 1, 0, None))
            for d in (2, 3):
                load_v((AHEAD - 1, 0, None), d)
            for c in (0, 1):
                load_u((AHEAD + 1, 0, None), c)

            def load_step(k, per=0, j=None):
                before, now, after = (k, per, j), (k + 1, per, j), (k + 2, per, j)
                for c in (2, 3):
                    load_u(now, c)
                if now != last:
                    load_gates(after)
                for d in range(DB):
                    load_v(before, d)
                for c in (0, 1):
                    load_u(after, c) if now != last else load_v(last, c)

            with sp.Fori(0, (GROUPS - AHEAD - 1) // 2 - 1) as j:
                load_step(AHEAD, 2, j)
                load_step(AHEAD + 1, 2, j)
            load_step(GROUPS - 3)
            load_step(GROUPS - 2)
            for d in (2, 3):
                load_v(last, d)
            for n, name in enumerate(("ln2_w", "ln2_b")):
                sp.wait_ge(s_weighted, EB * (GROUPS - 1 + n))
                sp.dma_start(gates[:, n, :, :, :].rearrange("p g k t -> p (g k t)"), dram[name].partition_broadcast(P)).then_inc(s_params, 16)
            sp.wait_ge(s_params, 32)

        @block.tensor
        def _(pe):
            def inner(g):
                for c in range(EB):
                    pe.wait_ge(s_gelu, at(EB * g[0] + c - 1, EB * g[1], g[2]))
                    core.by_feature(pe, bank[:, c % 2, :], *u_unit(g, c))

            def outer(g, d):
                n, per, i = v_unit(g, d)
                pe.wait_ge(core.s_lo, at(n + 1, per, i))
                for b in range(TB):
                    pe.wait_ge(s_added, at(16 * g[0] + 4 * d + b + 1, 16 * g[1], g[2]))
                    for k in range(EB):
                        if d == 0 and b == 0:
                            pe.wait_ge(s_p_lo, at(EB * g[0] + k + 1, EB * g[1], g[2]))
                        for term in range(3):
                            x = (p_lo if term == 2 else p_hi)[:, g[0] % 2, k, b * P:(b + 1) * P]
                            w = (core.w_lo if term == 1 else core.w_hi)[:, n % 2, k * COLS:(k + 1) * COLS]
                            mm = pe.matmul(bank[:, 4 + b, :], x, w, start=(k == 0 and term == 0),
                                           stop=(k == EB - 1 and term == 2))
                    mm.then_inc(core.s_used if b == TB - 1 else s_out, 1)

            for c in range(EB):
                core.by_feature(pe, bank[:, c, :], *u_unit(first, c))
            steps(pe, lambda g, c: None, lambda n, per, i: None, lambda c: None, inner, outer)

        @block.scalar
        def _(act):
            def split(n, per, i):
                if per or n + 2 < E0 + 2 * KEYS:
                    core.split_hi(act, n + 2, per, i)

            def high(g, c):
                act.wait_ge(s_weighted, at(EB * g[0] + c + 1, EB * g[1], g[2]))
                act.activation(p_hi[:, g[0] % 2, c, :], weighted[:, c % 2, :], ACT.Copy).then_inc(s_p_hi, 1)

            def kept(g, c):
                act.wait_ge(s_products[c % 2], at(16 * ((EB * g[0] + c) // 2 + 1), 8 * EB * g[1], g[2]))
                act.activation(gelu[:, c % 2, :], gelu[:, c % 2, :], ACT.Gelu).then_inc(s_gelu, 1)
                high(g, c)

            def inner(g):
                for c in range(EB):
                    n, per, i = u_unit(g, c)
                    act.wait_ge(core.s_used, at(n + 1, per, i))
                    act.wait_ge(s_weighted, at(EB * g[0] + c - 1, EB * g[1], g[2]))
                    act.activation(gelu[:, c % 2, :], bank[:, c % 2, :], ACT.Gelu).then_inc(s_gelu, 1)
                    split(n, per, i)
                    high(g, c)

            act.preload_act_table_set("gelu_and_others")
            def held(c):
                act.wait_ge(s_weighted, EB * AHEAD + c - 1)
                act.activation(gelu[:, c % 2, :], bank[:, c, :], ACT.Gelu).then_inc(s_gelu, 1)
                high(first, c)

            steps(act, kept, split, held, inner, lambda g, d: split(*v_unit(g, d)))

        @block.gpsimd
        def _(pool):
            def apply_gates(g, c):
                cnt = lambda k: at(EB * g[0] + c + k, EB * g[1], g[2])
                if c == 0:
                    pool.wait_ge(s_gates[g[0] % 2], at(16 * (g[0] // 2 + 1), 8 * g[1], g[2]))
                pool.wait_ge(s_gelu, cnt(1))
                if c >= 2 or g[0]:
                    pool.wait_ge(s_p_lo, cnt(-1))
                pool.tensor_tensor(weighted[:, c % 2, :].rearrange("p (g t) -> p g t", g=NTG),
                                   gelu[:, c % 2, :].rearrange("p (g t) -> p g t", g=NTG),
                                   gates[:, g[0] % 2, :, c, :], ALU.mult).then_inc(s_weighted, 1)

            def inner(g):
                for c in range(EB):
                    apply_gates(g, c)

            steps(pool, apply_gates, lambda n, per, i: None, lambda c: apply_gates(first, c), inner, lambda g, d: None)

        @block.vector
        def _(dve):
            dve.sem_inc(s_added, TB)

            def split(n, per, i):
                if per or n + 2 < E0 + 2 * KEYS:
                    core.split_lo(dve, n + 2, per, i)

            def low(g, c):
                dve.wait_ge(s_p_hi, at(EB * g[0] + c + 1, EB * g[1], g[2]))
                dve.tensor_tensor(p_lo[:, g[0] % 2, c, :], weighted[:, c % 2, :], p_hi[:, g[0] % 2, c, :].bitcast(F32),
                                  ALU.subtract).then_inc(s_p_lo, 1)

            def inner(g):
                for c in range(EB):
                    split(*u_unit(g, c))
                    low(g, c)

            def outer(g, d):
                n, per, i = v_unit(g, d)
                for b in range(TB):
                    if b < TB - 1:
                        dve.wait_ge(s_out, at(12 * g[0] + 3 * d + b + 1, 12 * g[1], g[2]))
                    else:
                        dve.wait_ge(core.s_used, at(n + 1, per, i))
                    a = acc[:, b, d * COLS:(d + 1) * COLS]
                    dve.tensor_tensor(a, a, bank[:, 4 + b, :], ALU.add).then_inc(s_added, 1)
                if g == last:
                    dve.wait_ge(s_added, 16 * g[0] + 4 * (d + 1) + 4)
                    for b in range(TB):
                        dve.bn_stats(ln.stats[:, b, d, :], acc[:, b, d * COLS:(d + 1) * COLS]).then_inc(s_stats, 1)
                split(n, per, i)

            def scale_acc():
                dve.wait_ge(s_acc, 16)
                dve.tensor_scalar(acc[:, :, :], acc[:, :, :], ALPHA, None, ALU.mult).then_inc(s_scaled, 1)
                dve.wait_ge(s_scaled, 1)

            steps(dve, low, split, lambda c: low(first, c), inner, outer, scale_acc)


def finish(core, dram, acc, ln, ln_w, ln_b):
    nc = core.nc
    with phase(nc) as ctx:
        ln.open(ctx)
        s_chain, s_by_pool, s_by_dve, s_out = (phase_semaphore(nc, ctx, "finish_" + n) for n in (
            "dve_chain", "out_normed_even", "out_normed_odd", "out_written"))
        block = ctx.enter_context(nc.Block())

        @block.sync
        def _(sp):
            for n in range(TB):
                sp.wait_ge((s_by_pool, s_by_dve)[n % 2], n // 2 + 1)
                sp.dma_start(dram["out"][n * P:(n + 1) * P, :], acc[:, n, :]).then_inc(s_out, 16)
            sp.wait_ge(s_out, 16 * TB)

        @block.scalar
        def _(act):
            for n in range(TB):
                ln.scale(act, n, acc[:, n, :])

        @block.vector
        def _(dve):
            chain = Chain(dve, s_chain, 0)
            for n in range(TB):
                ln.variance(dve, chain, n)
            for n in range(TB):
                ln.shift_of(dve, n)
            for n in range(TB):
                ln.weigh(dve, n, acc[:, n, :], ln_w)
                if n % 2:
                    ln.add_bias(dve, n, acc[:, n, :], ln_b, s_by_dve)

        @block.gpsimd
        def _(pool):
            for n in range(TB):
                ln.power(pool, n)
            for n in range(0, TB, 2):
                ln.add_bias(pool, n, acc[:, n, :], ln_b, s_by_pool)


_OUT = (1, T, D)


def build(nc, dram, stop=99):
    with ExitStack() as ctx:
        core = Core(nc, ctx)
        constants(core)
        with ExitStack() as mem_ctx:
            mem_hi = mem_ctx.enter_context(nc.sbuf_tensor("mem_hi", [P, KD, M], F32R))
            mem_lo = mem_ctx.enter_context(nc.sbuf_tensor("mem_lo", [P, KD, M], F32R))
            embed(core, mem_hi, mem_lo, dram)
            if stop >= 2:
                attention(core, mem_hi, mem_lo, dram)
        if stop >= 3:
            delta_net(core, dram)
        if stop >= 4:
            mix_out(core, dram)
        if stop >= 5:
            with nc.sbuf_tensor("chosen", [P, 3, TB, PH * TOPK], F32) as chosen:
                route(core, dram, chosen)
                spread(core, dram, chosen)
        if stop >= 6:
            with ExitStack() as out_ctx:
                acc = out_ctx.enter_context(nc.sbuf_tensor("acc", [P, TB, D], F32))
                ln = LayerNorm(core, out_ctx, "ln2", TB)
                gates = out_ctx.enter_context(nc.sbuf_tensor("gates_in", [P, 2, NTG, EB, TG], F32))
                experts(core, dram, acc, ln, gates)
                ln_w, ln_b = (gates[:, n, :, :, :].rearrange("p g k t -> p (g k t)") for n in range(2))
                finish(core, dram, acc, ln, ln_w, ln_b)


def kernel(**inputs):
    import concourse.bacc as bacc
    from concourse.bass_utils import run_bass_kernel_spmd

    a = {k: np.asarray(v) for k, v in inputs.items()}

    def by_column_block(w):
        n = w.shape[1] // P
        return w.reshape(KD, P, n, P).transpose(2, 1, 0, 3).reshape(n, P, UNIT)

    def by_row_block(w):
        m, n = w.shape[0] // (KQ * P), w.shape[1] // COLS
        return w.reshape(m, KQ, P, n, COLS).transpose(0, 3, 2, 1, 4).reshape(m, n, P, UNIT)

    w_in = a["w_in"][0]
    gw, sw = GH * P, SH * P
    units = by_column_block(np.concatenate([w_in[:, :4 * gw], w_in[:, 4 * gw + 2 * GH:]], axis=1))
    q, k, v, z = (units[n * GH:(n + 1) * GH] for n in range(4))
    sq, sk, sv, mq = (units[4 * GH + n * SH:4 * GH + (n + 1) * SH] for n in range(4))
    kv = by_column_block(a["w_mem_kv"][0])
    conv = a["conv_w"][0].reshape(TAPS, 3, GH, P)
    arrays = {
        "x": a["x"][0], "mem": a["mem"][0],
        "w_att": np.stack([mq, sq, sk, sv], axis=1).reshape(4 * SH, P, UNIT),
        "w_gdn": np.stack([q, k, v, z], axis=1).reshape(4 * GH, P, UNIT),
        "w_mem_kv": np.stack([kv[:MH], kv[MH:]], axis=1).reshape(2 * MH, P, UNIT),
        "w_gates": w_in[:, 4 * gw:4 * gw + 2 * GH].reshape(KD, P, 2 * GH).transpose(1, 0, 2),
        "conv_w": conv.transpose(3, 2, 1, 0).reshape(P, GH * 3 * TAPS),
        "a_log": a["a_log"], "dt_bias": a["dt_bias"],
        "gdn_norm_w": a["gdn_norm_w"].T,
        "att_norm_w": np.stack([a["mem_norm_w"][0].reshape(MH, P), a["sb_norm_w"][0].reshape(SH, P)],
                               axis=1).reshape(MH + SH, P).T,
        "w_out": by_row_block(a["w_out"][0]),
        "peer_wq": by_column_block(a["peer_wq"][0]),
        "peer_keys": np.concatenate([a["peer_keys1"][0].T, a["peer_keys2"][0].T], axis=1),
        "peer_u": a["peer_u"][0].reshape(KEYS, P, KD, P).transpose(0, 3, 2, 1).reshape(KEYS, P, UNIT),
        "peer_v": by_row_block(a["peer_v"][0]),
    }
    for name in ("ln_emb", "ln_mem", "ln1", "ln2"):
        for part in ("_w", "_b"):
            arrays[name + part] = a[name + part].reshape(D)
    arrays = {k: np.ascontiguousarray(v) for k, v in arrays.items()}

    nc = bacc.Bacc("TRN2", target_bir_lowering=False, num_devices=1)
    dram = {k: nc.dram_tensor("in_" + k, v.shape, F32, kind="ExternalInput").ap() for k, v in arrays.items()}
    for name, shape in (("h_kept", (T, D)), ("h1_kept", (T, D)), ("o_kept", (HEADS, P, T)),
                        ("gates_kept", (NTG, P, KEYS, TG)), ("products_kept", (EB * AHEAD, P, T))):
        dram[name] = nc.dram_tensor(name, shape, F32).ap()
    dram["out"] = nc.dram_tensor("out", (T, D), F32, kind="ExternalOutput").ap()
    build(nc, dram)
    r = run_bass_kernel_spmd(nc, [{"in_" + k: v for k, v in arrays.items()}], core_ids=[0])
    return np.asarray(r.results[0]["out"]).reshape(_OUT)
```
